# Optimizing a Trainium2 kernel written in Bass

```python
import jax, jax.numpy as jnp
from jax import lax
import numpy as np

D_MODEL = 1024
BATCH = 1
SEQ = 256
DEPTH = 2
DEC_BATCH = 8
DEC_SEQ = 8
PAST_LEN = 1024
PAGE_SIZE = 128

N_MIXERS = 2
N_GDN_LAYERS = (DEPTH + 1) // 2
N_NSA_LAYERS = DEPTH // 2
RMS_EPS = 1e-6

GDN_QK_HEADS = 8
GDN_V_HEADS = 16
GDN_DK = 128
GDN_DV = 128
GDN_QK_DIM = GDN_QK_HEADS * GDN_DK
GDN_V_DIM = GDN_V_HEADS * GDN_DV
GDN_CONV_CH = 2 * GDN_QK_DIM + GDN_V_DIM
GDN_CONV_W = 4
GDN_CHUNK = 64
GDN_PROJ = GDN_CONV_CH + GDN_V_DIM + 2 * GDN_V_HEADS

NSA_HEADS = 16
NSA_KV_GROUPS = 4
NSA_GROUP_SIZE = NSA_HEADS // NSA_KV_GROUPS
NSA_DH = 64
NSA_Q_DIM = NSA_HEADS * NSA_DH
NSA_KV_DIM = NSA_KV_GROUPS * NSA_DH
NSA_N_KV = 6
NSA_N_GATES = 3
NSA_PROJ = NSA_Q_DIM + NSA_N_KV * NSA_KV_DIM + NSA_N_GATES * NSA_HEADS
CMP_STRIDE = 16
CMP_LEN = 2 * CMP_STRIDE
CMP_HIDDEN = 256
SEL_BLOCK = 64
SEL_TOPN = 8
WINDOW = 512
NSA_Q_BLOCK = 64
NEG_INF = -1e30
FORCE_SCORE = 1e9

D_FF = 2816
FFN_CONV_W = 3

kernel_name = "hybrid_gdn_nsa_convffn_step"

def rms_norm(x, w):
    xf = x.astype(jnp.float32)
    xf = xf * lax.rsqrt(jnp.mean(xf * xf, axis=-1, keepdims=True) + RMS_EPS)
    return xf.astype(x.dtype) * w

def l2_normalize(x):
    xf = x.astype(jnp.float32)
    return (xf * lax.rsqrt(jnp.sum(xf * xf, axis=-1, keepdims=True) + 1e-6)).astype(x.dtype)

def causal_dwconv(x, buf, w):
    width = w.shape[0]
    t = x.shape[1]
    xp = jnp.concatenate([buf.astype(x.dtype), x], axis=1)
    y = sum(xp[:, i:i + t] * w[i] for i in range(width))
    return y, xp[:, t:]

def masked_softmax(s, mask):
    p = jax.nn.softmax(jnp.where(mask, s, NEG_INF), axis=-1)
    return p * mask

def alibi_slopes():
    return 2.0 ** (-8.0 * jnp.arange(1, NSA_HEADS + 1, dtype=jnp.float32) / NSA_HEADS)

def chunk_gated_delta(q, k, v, g, beta, s0):
    b, t, h, dk = q.shape
    dv = v.shape[-1]
    c = min(GDN_CHUNK, t)
    n = -(-t // c)
    pad = n * c - t

    def to_chunks(a):
        a = jnp.pad(a.astype(jnp.float32), [(0, 0), (0, pad)] + [(0, 0)] * (a.ndim - 2))
        a = a.reshape((b, n, c) + a.shape[2:])
        return jnp.moveaxis(a, (1, 3), (0, 2))

    qc, kc, vc, gc, bc = map(to_chunks, (q, k, v, g, beta))
    gcum = jnp.cumsum(gc, axis=-1)
    tri = jnp.tril(jnp.ones((c, c), dtype=bool))
    stri = jnp.tril(jnp.ones((c, c), dtype=bool), -1)
    diff = gcum[..., :, None] - gcum[..., None, :]
    decay = jnp.where(tri, jnp.exp(jnp.where(tri, diff, 0.0)), 0.0)
    kb = kc * bc[..., None]
    a_mat = jnp.where(stri, jnp.einsum('nbhid,nbhjd->nbhij', kb, kc) * decay, 0.0) + jnp.eye(c, dtype=jnp.float32)
    u = lax.linalg.triangular_solve(a_mat, vc * bc[..., None], left_side=True, lower=True, unit_diagonal=True)
    w = lax.linalg.triangular_solve(a_mat, kb * jnp.exp(gcum)[..., None], left_side=True, lower=True, unit_diagonal=True)
    qk = jnp.where(tri, jnp.einsum('nbhid,nbhjd->nbhij', qc, kc) * decay, 0.0)
    q_dec = qc * jnp.exp(gcum)[..., None]
    k_dec = kc * jnp.exp(gcum[..., -1:] - gcum)[..., None]
    g_tot = jnp.exp(gcum[..., -1])

    def step(s, xs):
        qk_i, qd_i, kd_i, u_i, w_i, gt_i = xs
        v_new = u_i - jnp.einsum('bhcd,bhde->bhce', w_i, s)
        o_i = jnp.einsum('bhcd,bhde->bhce', qd_i, s) + jnp.einsum('bhij,bhje->bhie', qk_i, v_new)
        s = s * gt_i[..., None, None] + jnp.einsum('bhcd,bhce->bhde', kd_i, v_new)
        return s, o_i

    s_fin, o = lax.scan(step, s0.astype(jnp.float32), (qk, q_dec, k_dec, u, w, g_tot))
    o = jnp.moveaxis(o, (0, 2), (1, 3)).reshape(b, n * c, h, dv)[:, :t]
    return o.astype(v.dtype), s_fin.astype(s0.dtype)

def gdn_mixer(x, s0, conv_buf, norm_w, w_in, conv_w, a_log, dt_bias, out_norm_w, w_out):
    b, t, _ = x.shape
    proj = rms_norm(x, norm_w) @ w_in
    qkv, z, a, beta_logit = jnp.split(
        proj, [GDN_CONV_CH, GDN_CONV_CH + GDN_V_DIM, GDN_CONV_CH + GDN_V_DIM + GDN_V_HEADS], axis=-1)
    qkv, new_buf = causal_dwconv(qkv, conv_buf, conv_w)
    qkv = jax.nn.silu(qkv)
    q, k, v = jnp.split(qkv, [GDN_QK_DIM, 2 * GDN_QK_DIM], axis=-1)
    rep = GDN_V_HEADS // GDN_QK_HEADS
    q = jnp.repeat(l2_normalize(q.reshape(b, t, GDN_QK_HEADS, GDN_DK)), rep, axis=2) * (GDN_DK ** -0.5)
    k = jnp.repeat(l2_normalize(k.reshape(b, t, GDN_QK_HEADS, GDN_DK)), rep, axis=2)
    v = v.reshape(b, t, GDN_V_HEADS, GDN_DV)
    beta = jax.nn.sigmoid(beta_logit.astype(jnp.float32))
    g = -jnp.exp(a_log.astype(jnp.float32)) * jax.nn.softplus(a.astype(jnp.float32) + dt_bias.astype(jnp.float32))
    o, s_new = chunk_gated_delta(q, k, v, g, beta, s0)
    o = rms_norm(o, out_norm_w) * jax.nn.silu(z.reshape(b, t, GDN_V_HEADS, GDN_DV))
    return o.reshape(b, t, GDN_V_DIM) @ w_out, s_new, new_buf

def compress_blocks(kv, pe, w1, w2):
    b, tk, g, dh = kv.shape
    n_sub = tk // CMP_STRIDE
    sub = kv[:, :n_sub * CMP_STRIDE].reshape(b, n_sub, CMP_STRIDE, g, dh)
    pe = pe.reshape(2, CMP_STRIDE, 1, dh)
    w1 = w1.reshape(2, CMP_STRIDE, dh, CMP_HIDDEN)
    first = jnp.einsum('bnsgd,sdh->bngh', sub + pe[0], w1[0])
    second = jnp.einsum('bnsgd,sdh->bngh', sub + pe[1], w1[1])
    hid = jax.nn.silu(first[:, :-1] + second[:, 1:])
    return hid @ w2

def nsa_mixer(x, past_kv, win_buf, norm_w, w_in, cmp_pe, cmp_w1, cmp_w2, w_out):
    b, t, _ = x.shape
    p_len = past_kv.shape[1]
    w_len = win_buf.shape[1]
    g, r, dh = NSA_KV_GROUPS, NSA_GROUP_SIZE, NSA_DH
    proj = rms_norm(x, norm_w) @ w_in
    q = proj[..., :NSA_Q_DIM].reshape(b, t, g, r, dh)
    kv = proj[..., NSA_Q_DIM:NSA_Q_DIM + NSA_N_KV * NSA_KV_DIM].reshape(b, t, NSA_N_KV, g, dh)
    gates = jax.nn.sigmoid(proj[..., NSA_Q_DIM + NSA_N_KV * NSA_KV_DIM:].astype(jnp.float32))
    gates = gates.reshape(b, t, g, r, NSA_N_GATES).astype(x.dtype)
    new_rows = kv[:, :, :4]
    win_all = jnp.concatenate([win_buf.astype(x.dtype), kv[:, :, 4:]], axis=1)
    full = jnp.concatenate([past_kv.astype(x.dtype), new_rows], axis=1)
    tk = p_len + t

    cmp_k = compress_blocks(full[:, :, 0], cmp_pe[0], cmp_w1[0], cmp_w2[0])
    cmp_v = compress_blocks(full[:, :, 1], cmp_pe[1], cmp_w1[1], cmp_w2[1])
    n_cmp = cmp_k.shape[1]
    cmp_end = jnp.arange(n_cmp) * CMP_STRIDE + (CMP_LEN - 1)

    n_blk = -(-tk // SEL_BLOCK)
    sel = jnp.pad(full[:, :, 2:4], [(0, 0), (0, n_blk * SEL_BLOCK - tk), (0, 0), (0, 0), (0, 0)])
    sel = sel.reshape(b, n_blk, SEL_BLOCK, 2, g, dh).transpose(0, 4, 1, 2, 3, 5)
    start = jnp.arange(n_cmp)[:, None] * CMP_STRIDE
    blk_start = jnp.arange(n_blk)[None, :] * SEL_BLOCK
    overlap = ((start < blk_start + SEL_BLOCK) & (start + CMP_LEN > blk_start)).astype(jnp.float32)
    top_n = min(SEL_TOPN, n_blk)

    win_pad = jnp.pad(win_all, [(0, 0), (WINDOW, 0), (0, 0), (0, 0), (0, 0)])
    slopes = alibi_slopes().reshape(g, r)[:, :, None, None]
    qb = NSA_Q_BLOCK if t % NSA_Q_BLOCK == 0 else t
    scale = dh ** -0.5
    b_idx = jnp.arange(b)[:, None, None, None]
    g_idx = jnp.arange(g)[None, :, None, None]

    def query_block(i):
        o0 = i * qb
        q_b = lax.dynamic_slice_in_dim(q, o0, qb, axis=1)
        gate_b = lax.dynamic_slice_in_dim(gates, o0, qb, axis=1)
        t_pos = p_len + o0 + jnp.arange(qb)
        dist = t_pos[:, None] - cmp_end[None, :]
        s = jnp.einsum('bqgrd,bngd->bgrqn', q_b, cmp_k).astype(jnp.float32) * scale - slopes * dist.astype(jnp.float32)
        p_cmp = masked_softmax(s, dist >= 0)
        o_cmp = jnp.einsum('bgrqn,bngd->bqgrd', p_cmp.astype(x.dtype), cmp_v)
        imp = jnp.einsum('bgrqn,nj->bgqj', p_cmp, overlap)
        j = jnp.arange(n_blk)
        cur = (t_pos // SEL_BLOCK)[:, None]
        forced = (j == 0) | (j == cur) | (j == cur - 1)
        imp = jnp.where(forced, FORCE_SCORE, imp)
        imp = jnp.where(j > cur, -FORCE_SCORE, imp)
        _, idx = lax.top_k(imp, top_n)
        gathered = sel[b_idx, g_idx, idx].reshape(b, g, qb, top_n * SEL_BLOCK, 2, dh)
        key_pos = (idx[..., None] * SEL_BLOCK + jnp.arange(SEL_BLOCK)).reshape(b, g, qb, top_n * SEL_BLOCK)
        dist = (t_pos[:, None] - key_pos)[:, :, None]
        s = jnp.einsum('bqgrd,bgqkd->bgrqk', q_b, gathered[..., 0, :]).astype(jnp.float32) * scale - slopes * dist.astype(jnp.float32)
        p_sel = masked_softmax(s, dist >= 0)
        o_sel = jnp.einsum('bgrqk,bgqkd->bqgrd', p_sel.astype(x.dtype), gathered[..., 1, :])
        win_b = lax.dynamic_slice_in_dim(win_pad, o0 + w_len, WINDOW + qb, axis=1)
        w_pos = p_len + o0 - WINDOW + jnp.arange(WINDOW + qb)
        dist = t_pos[:, None] - w_pos[None, :]
        mask = (dist >= 0) & (dist < WINDOW) & (w_pos[None, :] >= 0)
        s = jnp.einsum('bqgrd,bkgd->bgrqk', q_b, win_b[:, :, 0]).astype(jnp.float32) * scale - slopes * dist.astype(jnp.float32)
        p_win = masked_softmax(s, mask)
        o_win = jnp.einsum('bgrqk,bkgd->bqgrd', p_win.astype(x.dtype), win_b[:, :, 1])
        o = gate_b[..., 0:1] * o_cmp + gate_b[..., 1:2] * o_sel + gate_b[..., 2:3] * o_win
        return o.reshape(b, qb, NSA_Q_DIM).astype(x.dtype)

    out = lax.map(query_block, jnp.arange(t // qb))
    out = jnp.moveaxis(out, 0, 1).reshape(b, t, NSA_Q_DIM)
    new_win = win_all[:, win_all.shape[1] - min(WINDOW, tk):]
    return out @ w_out, new_rows, new_win

def conv_ffn(x, buf, norm_w, w_up, conv_w, w_down):
    h = rms_norm(x, norm_w) @ w_up
    a, gate = jnp.split(h, [D_FF], axis=-1)
    a, new_buf = causal_dwconv(a, buf, conv_w)
    return (jax.nn.silu(a) * gate) @ w_down, new_buf

def trunk(x, past_kv_fn, nsa_win, gdn_state, gdn_conv, ffn_conv,
          gdn_norm, gdn_w_in, gdn_conv_w, gdn_a_log, gdn_dt_bias, gdn_out_norm, gdn_w_out,
          nsa_norm, nsa_w_in, nsa_cmp_pe, nsa_cmp_w1, nsa_cmp_w2, nsa_w_out,
          ffn_norm, ffn_w_up, ffn_conv_w, ffn_w_down, final_norm):
    rows_l, win_l, s_l, gconv_l, fconv_l = [], [], [], [], []
    for i in range(DEPTH):
        j = i // N_MIXERS
        if i % N_MIXERS == 0:
            y, s_new, cb = gdn_mixer(x, gdn_state[j], gdn_conv[j], gdn_norm[j], gdn_w_in[j], gdn_conv_w[j],
                                     gdn_a_log[j], gdn_dt_bias[j], gdn_out_norm[j], gdn_w_out[j])
            s_l.append(s_new)
            gconv_l.append(cb)
        else:
            y, rows, wb = nsa_mixer(x, past_kv_fn(j), nsa_win[j], nsa_norm[j], nsa_w_in[j],
                                    nsa_cmp_pe[j], nsa_cmp_w1[j], nsa_cmp_w2[j], nsa_w_out[j])
            rows_l.append(rows)
            win_l.append(wb)
        x = x + y
        y, fb = conv_ffn(x, ffn_conv[i], ffn_norm[i], ffn_w_up[i], ffn_conv_w[i], ffn_w_down[i])
        x = x + y
        fconv_l.append(fb)
    return (rms_norm(x, final_norm), jnp.stack(rows_l), jnp.stack(win_l), jnp.stack(s_l),
            jnp.stack(gconv_l), jnp.stack(fconv_l))

def setup_inputs(seed: int = 0) -> dict:
    key = jax.random.key(seed)
    ks = jax.random.split(key, 32)
    f32 = jnp.float32
    n_pages = PAST_LEN // PAGE_SIZE
    n_used = DEC_BATCH * n_pages
    n_pool = n_used + n_used // 4
    win_len = min(WINDOW, PAST_LEN)

    def normal(k, shape, scale):
        return jax.random.normal(k, shape, f32) * scale

    def gain(k, shape):
        return 1.0 + 0.02 * jax.random.normal(k, shape, f32)

    page_table = jax.random.permutation(ks[0], n_pool)[:n_used].reshape(DEC_BATCH, n_pages).astype(jnp.int32)
    return {
        "x_prompt": normal(ks[1], (BATCH, SEQ, D_MODEL), 1.0),
        "x_sample": normal(ks[2], (DEC_BATCH, DEC_SEQ, D_MODEL), 1.0),
        "cache_nsa_kv": normal(ks[3], (N_NSA_LAYERS, n_pool, PAGE_SIZE, 4, NSA_KV_GROUPS, NSA_DH), 1.0),
        "cache_nsa_win": normal(ks[4], (N_NSA_LAYERS, DEC_BATCH, win_len, 2, NSA_KV_GROUPS, NSA_DH), 1.0),
        "state_gdn_s": normal(ks[5], (N_GDN_LAYERS, DEC_BATCH, GDN_V_HEADS, GDN_DK, GDN_DV), GDN_DK ** -0.5),
        "state_gdn_conv": normal(ks[6], (N_GDN_LAYERS, DEC_BATCH, GDN_CONV_W - 1, GDN_CONV_CH), 1.0),
        "state_ffn_conv": normal(ks[7], (DEPTH, DEC_BATCH, FFN_CONV_W - 1, D_FF), 1.0),
        "page_table": page_table,
        "gdn_norm": gain(ks[8], (N_GDN_LAYERS, D_MODEL)),
        "gdn_w_in": normal(ks[9], (N_GDN_LAYERS, D_MODEL, GDN_PROJ), D_MODEL ** -0.5),
        "gdn_conv_w": normal(ks[10], (N_GDN_LAYERS, GDN_CONV_W, GDN_CONV_CH), GDN_CONV_W ** -0.5),
        "gdn_a_log": jnp.log(jax.random.uniform(ks[11], (N_GDN_LAYERS, GDN_V_HEADS), f32, 1.0, 16.0)),
        "gdn_dt_bias": normal(ks[12], (N_GDN_LAYERS, GDN_V_HEADS), 0.1),
        "gdn_out_norm": gain(ks[13], (N_GDN_LAYERS, GDN_DV)),
        "gdn_w_out": normal(ks[14], (N_GDN_LAYERS, GDN_V_DIM, D_MODEL), GDN_V_DIM ** -0.5),
        "nsa_norm": gain(ks[15], (N_NSA_LAYERS, D_MODEL)),
        "nsa_w_in": normal(ks[16], (N_NSA_LAYERS, D_MODEL, NSA_PROJ), D_MODEL ** -0.5),
        "nsa_cmp_pe": normal(ks[17], (N_NSA_LAYERS, 2, CMP_LEN, NSA_DH), 0.1),
        "nsa_cmp_w1": normal(ks[18], (N_NSA_LAYERS, 2, CMP_LEN, NSA_DH, CMP_HIDDEN), (CMP_LEN * NSA_DH) ** -0.5),
        "nsa_cmp_w2": normal(ks[19], (N_NSA_LAYERS, 2, CMP_HIDDEN, NSA_DH), CMP_HIDDEN ** -0.5),
        "nsa_w_out": normal(ks[20], (N_NSA_LAYERS, NSA_Q_DIM, D_MODEL), NSA_Q_DIM ** -0.5),
        "ffn_norm": gain(ks[21], (DEPTH, D_MODEL)),
        "ffn_w_up": normal(ks[22], (DEPTH, D_MODEL, 2 * D_FF), D_MODEL ** -0.5),
        "ffn_conv_w": normal(ks[23], (DEPTH, FFN_CONV_W, D_FF), FFN_CONV_W ** -0.5),
        "ffn_w_down": normal(ks[24], (DEPTH, D_FF, D_MODEL), D_FF ** -0.5),
        "final_norm": gain(ks[25], (D_MODEL,)),
    }

def reference(x_prompt, x_sample, cache_nsa_kv, cache_nsa_win, state_gdn_s, state_gdn_conv, state_ffn_conv,
              page_table, gdn_norm, gdn_w_in, gdn_conv_w, gdn_a_log, gdn_dt_bias, gdn_out_norm, gdn_w_out,
              nsa_norm, nsa_w_in, nsa_cmp_pe, nsa_cmp_w1, nsa_cmp_w2, nsa_w_out,
              ffn_norm, ffn_w_up, ffn_conv_w, ffn_w_down, final_norm):
    weights = (gdn_norm, gdn_w_in, gdn_conv_w, gdn_a_log, gdn_dt_bias, gdn_out_norm, gdn_w_out,
               nsa_norm, nsa_w_in, nsa_cmp_pe, nsa_cmp_w1, nsa_cmp_w2, nsa_w_out,
               ffn_norm, ffn_w_up, ffn_conv_w, ffn_w_down, final_norm)
    dt = x_prompt.dtype
    bp = x_prompt.shape[0]
    n_gdn = state_gdn_s.shape[0]
    n_nsa = cache_nsa_kv.shape[0]

    (y_prompt, kv_rows_prompt, win_prompt, gdn_s_prompt, gdn_conv_prompt, ffn_conv_prompt) = trunk(
        x_prompt,
        lambda j: jnp.zeros((bp, 0, 4, NSA_KV_GROUPS, NSA_DH), dt),
        jnp.zeros((n_nsa, bp, 0, 2, NSA_KV_GROUPS, NSA_DH), dt),
        jnp.zeros((n_gdn, bp, GDN_V_HEADS, GDN_DK, GDN_DV), dt),
        jnp.zeros((n_gdn, bp, GDN_CONV_W - 1, GDN_CONV_CH), dt),
        jnp.zeros((DEPTH, bp, FFN_CONV_W - 1, D_FF), dt),
        *weights)

    n_seq = page_table.shape[0]

    def past_sample(j):
        return cache_nsa_kv[j][page_table].reshape(n_seq, -1, 4, NSA_KV_GROUPS, NSA_DH)

    (y_sample, kv_rows_sample, win_sample, gdn_s_sample, gdn_conv_sample, ffn_conv_sample) = trunk(
        x_sample, past_sample, cache_nsa_win, state_gdn_s, state_gdn_conv, state_ffn_conv, *weights)

    return (y_prompt, y_sample, kv_rows_prompt, kv_rows_sample, win_prompt, win_sample,
            gdn_s_prompt, gdn_s_sample, gdn_conv_prompt, gdn_conv_sample, ffn_conv_prompt, ffn_conv_sample)


_drawn_inputs = setup_inputs


def setup_inputs(seed=0):
    import zlib

    import numpy as np

    out = dict(_drawn_inputs(seed))
    spreads = {}
    factors = {'gdn_dt_bias': 5.738,
     'gdn_out_norm': 4.883,
     'nsa_norm': 2.852,
     'final_norm': 7.892,
     'nsa_cmp_pe': 4.138}
    for name, (base, spread) in spreads.items():
        noise = np.random.default_rng([zlib.crc32(name.encode()), seed]).standard_normal(out[name].shape)
        drawn = base * np.exp(spread * noise) if base else spread * noise
        out[name] = __import__('jax').numpy.asarray(drawn.astype(out[name].dtype))
    for name, factor in factors.items():
        out[name] = (out[name] * factor).astype(out[name].dtype)
    return out
```

```python
from contextlib import ExitStack

import numpy as np

import concourse.bass as bass
from concourse import mybir

ALU = mybir.AluOpType
ACT = mybir.ActivationFunctionType
F32 = mybir.dt.float32
I32 = mybir.dt.int32
AX = mybir.AxisListType

P = 128
D = 1024
KD = D // P
TP, NB, TQ = 256, 8, 8
TS = NB * TQ
T = TP + TS
EPS = 1e-6

QKH, VH, DK = 8, 16, 128
CONV_CH = (2 * QKH + VH) * DK
V_DIM = VH * DK
NCT = CONV_CH // P
GW = 4
GP = GW - 1
FF = 2816
NFT = FF // P
FW = 3
FP = FW - 1

HEADS, GROUPS, DH = 16, 4, 64
REP = HEADS // GROUPS
Q_DIM = HEADS * DH
KV_DIM = GROUPS * DH
NKV = 6
PAST, PAGE, NPOOL = 1024, 128, 80
NPG = PAST // PAGE
WIN = 512
STRIDE, CLEN, CHID = 16, 32, 256
NSUB = PAST // STRIDE
NCMP = NSUB - 1
PSUB = TP // STRIDE
PCMP = PSUB - 1
SELB, TOPN = 64, 8
NPB = PAST // SELB
FREE_BLKS = NPB - 2
FREE_TOP = TOPN - 3
MASKED = -1e30

RING = 4
SLOT = NFT * P

UNITS = {}
_at = 0
for _name, _n in (("gdn_in", 24), ("gdn_out", 8), ("ffn_up0", 22), ("ffn_down0", 8),
                  ("nsa_in", 10), ("nsa_out", 4), ("ffn_up1", 22), ("ffn_down1", 8)):
    UNITS[_name] = (_at, _n)
    _at += _n


def constants():
    parts, where, at = [], {}, 0

    def put(name, a):
        nonlocal at
        a = np.asarray(a, np.float32).reshape(a.shape[0], -1)
        full = np.zeros((P, a.shape[1]), np.float32)
        full[:a.shape[0]] = a
        parts.append(full)
        where[name] = (at, a.shape[1])
        at += a.shape[1]

    eye = np.eye(P)
    t = np.arange(P)
    up = (t[:, None] <= t[None, :]) * 1.0
    same8 = (t[:64, None] // TQ == t[None, :64] // TQ) * 1.0
    pad = lambda a: np.concatenate([a, np.zeros((P - a.shape[0], a.shape[1]))])
    put("ident", eye)
    put("ones", np.ones((P, P)))
    causal3 = np.concatenate([up, up, pad(up[:64, :64] * same8)], 1)
    eye3 = np.concatenate([eye, eye, pad(eye[:64, :64])], 1)
    put("causal3", causal3)
    put("strict3", causal3 - eye3)
    put("eye3", eye3)
    low = [((t[:, None] >> k) % 2 == 1) & ((t[None, :] >> k) == (t[:, None] >> k) - 1) for k in range(7)]
    for k in range(3):
        m = low[k] * 1.0
        put(f"level{k}", np.concatenate([m, m, pad(m[:64, :64])], 1))
    for k in range(3, 7):
        put(f"level{k}", low[k] * 1.0)
    m = low[0].T * 1.0
    put("level0T", np.concatenate([m, m, pad(m[:64, :64])], 1))
    b = np.arange(NB)
    put("tok_seq", (t[:64, None] // TQ == b[None, :]) * 1.0)
    put("col_seq", np.broadcast_to((np.arange(TS)[None, :] // TQ == b[:, None]) * 1.0, (P, NB, TS)))
    carry = np.ones(T)
    carry[[0, 128]] = 0
    carry[TP::TQ] = 0
    put("carry", np.broadcast_to(carry, (VH, T)))
    base = at

    slopes = 2.0 ** (-8.0 * np.arange(1, HEADS + 1) / HEADS)
    put("slopes", np.broadcast_to(slopes, (P, HEADS)))
    pos = np.arange(TP)
    dist = lambda q, k: np.where(q[:, None] >= k[None, :], -(q[:, None] - k[None, :]) * 1.0, -1e33)
    put("dist0", dist(t, pos[:P]))
    put("dist1", dist(t + P, pos))
    ce = np.arange(PCMP) * STRIDE + CLEN - 1
    put("cdist", np.stack([dist(t, ce), dist(t + P, ce)], 1))
    put("cvalid", np.stack([t[:, None] >= ce, t[:, None] + P >= ce], 1) * 1.0)
    row_slope = slopes[t // TQ]
    tq = PAST + t % TQ
    past = np.arange(PAST)
    put("bias_sel", -row_slope[:, None] * (tq[:, None] - past[None, :]))
    k = np.arange(TS)
    new = np.full((P, NB, TS), MASKED)
    for s in range(NB):
        ok = (k[None, :] // TQ == s) & (k[None, :] % TQ <= t[:, None] % TQ)
        new[:, s] = np.where(ok, -row_slope[:, None] * (t[:, None] % TQ - k[None, :] % TQ), MASKED)
    put("bias_new", new)
    dw = tq[:, None] - past[None, PAST - WIN:]
    put("bias_win", np.where(dw < WIN, -row_slope[:, None] * dw, MASKED))
    ce = np.arange(NCMP) * STRIDE + CLEN - 1
    put("bias_cmp", -row_slope[:, None] * (tq[:, None] - ce[None, :]))
    put("group_sum", (t[:, None] // 32 == t[None, :] // 32) & (t[:, None] % TQ == t[None, :] % TQ))
    st = np.arange(NCMP)[:, None] * STRIDE
    bs = (1 + np.arange(FREE_BLKS))[None, :] * SELB
    put("same_q", (t[:64, None] % TQ == t[None, :] % TQ))
    put("own_head", np.repeat(t[:, None] // TQ == np.arange(HEADS)[None, :], 3, axis=1))
    put("overlap", (st < bs + SELB) & (st + CLEN > bs))
    j = np.arange(FREE_BLKS)
    put("earlier", np.broadcast_to(j[None, None, :] < j[None, :, None], (P, FREE_BLKS, FREE_BLKS)))
    return np.concatenate(parts, 1), where, base


class Steps:

    def __init__(self, sem, order, loop):
        self.sem, self.order, self.at, self.first = sem, order, 0, 1 if loop else 0
        self.index = {name: n for n, name in enumerate(order)}
        assert len(self.index) == len(order)

    def step(self, name):
        assert self.order[self.at] == name, (name, self.order[self.at])
        self.at = (self.at + 1) % len(self.order)
        return 1

    def count(self, name, it=0):
        return it * len(self.order) + self.index[name] + 1 + self.first

    def all_before(self, it, extra=0):
        return it * len(self.order) + extra + self.first


class Space:

    def __init__(self, tensor, size):
        self.tensor, self.size, self.at, self.most = tensor, size, 0, 0

    def take(self, *dims, parts=P, off=None):
        n = int(np.prod(dims))
        if off is None:
            off = self.at
            self.at += n
        self.most = max(self.most, off + n)
        assert off + n <= self.size, (off + n, self.size)
        ap = self.tensor[0:parts, off:off + n]
        if len(dims) > 1:
            names = "abcd"[:len(dims)]
            ap = ap.rearrange(f"p ({' '.join(names)}) -> p {' '.join(names)}", **dict(zip(names, dims)))
        return ap


def seqs(ap):
    return ap.rearrange("p (b q) -> p b q", b=NB)


def build(nc, ins, outs, where, base_cols):
    ctx = ExitStack()
    with ctx:
        def sem(name):
            return ctx.enter_context(nc.semaphore(name))

        def steps(name, order, loop=False):
            return Steps(sem(name), order, loop)

        size = 53136
        sbuf = ctx.enter_context(nc.sbuf_tensor("sbuf", [P, size], F32))
        pages_sb = ctx.enter_context(nc.sbuf_tensor("page_rows", [1, NB * NPG], I32))
        psum = ctx.enter_context(nc.psum_tensor("psum", [P, 8, 512], F32))
        space = Space(sbuf, size)

        tables = space.take(base_cols)

        def const(name, parts=P):
            at, n = where[name]
            return tables[0:parts, at:at + n]

        ident, ones = const("ident"), const("ones")
        norm_w = space.take(KD, 5)
        gconv = space.take(NCT, NB * GP + GW)
        fconv = [space.take(NFT, NB * FP + FW) for _ in range(2)]
        out_norm = space.take(1)
        a_log = space.take(1, parts=VH)
        dt_bias = space.take(1, parts=VH)
        xT = space.take(KD, T)
        hT = space.take(KD, T)
        rinv = space.take(T)
        w_ab = space.take(KD, 2 * VH)
        ring = [space.take(SLOT) for _ in range(RING)]
        xpg_at = space.at
        xpg = [space.take(GP + TP + NB * (GP + TQ)) for _ in range(2)]
        xpf = [v[:, 0:FP + TP + NB * (FP + TQ)] for v in xpg]
        conv_y = [space.take(T) for _ in range(2)]
        kmask_space = space.take(NB * TS, off=space.at - 2 * T)
        tails = space.take(8, 27)
        eps_col = space.take(1)
        embed = space.take(32)
        phase = space.at

        w_in = [sem(f"weights_in_slot{j}") for j in range(RING)]
        half_done = sem("unit_first_tile_done")
        unit_done = sem("unit_done")
        lane_free = [sem(f"lane{l}_banks_free") for l in range(2)]
        stage_closed = sem("stage_closed")
        const_in, rows_in, x_in, small_in = sem("const_in"), sem("rows_in"), sem("x_in"), sem("small_in")
        stored = sem("stored")
        n_stored = [0]

        def slot(w):
            return ring[w % RING]

        space.at = phase
        x_tok = space.take(3, D)
        norm_rows = space.take(D, parts=5)
        g_rows = space.take(CONV_CH, parts=NB * GP + GW)
        f_rows = [space.take(FF, parts=NB * FP + FW) for _ in range(2)]

        e_rows = space.take(P, parts=32)
        turns = []
        for tb, rows in ((0, P), (1, P), (2, TS)):
            for half in range(2):
                turns.append((4 * P, [xT[:, 4 * half:4 * half + 4, tb * P:tb * P + rows]],
                              [(x_tok[0:rows, tb, (4 * half + j) * P:(4 * half + j + 1) * P], rows, j * P)
                               for j in range(4)], rows))
        turns.append((0, [norm_w], [(norm_rows[:, k * P:(k + 1) * P], 5, 5 * k) for k in range(KD)], 5))
        n = NB * GP + GW
        for half in range(2):
            turns.append((0, [gconv[:, 16 * half:16 * half + 16, :]],
                          [(g_rows[:, (16 * half + j) * P:(16 * half + j + 1) * P], n, n * j)
                           for j in range(16)], n))
        n = NB * FP + FW
        for l in range(2):
            turns.append((0, [fconv[l]], [(f_rows[l][:, k * P:(k + 1) * P], n, n * k) for k in range(NFT)], n))
        turns.append((0, [embed.rearrange("p (a b) -> p a b", a=1)], [(e_rows, 32, 0)], 32))
        NTURN = len(turns)
        S1 = dict(pe=steps("turned", [f"g{n}" for n in range(NTURN)]),
                  dve=steps("turned_copied_dve", [f"g{n}" for n in range(0, NTURN, 2)]),
                  act=steps("turned_copied_act", [f"g{n}" for n in range(1, NTURN, 2)]))

        def pe_turns(pe):
            pe.wait_ge(const_in, 16)
            for n, (_, dst, items, rows) in enumerate(turns):
                if n == 0:
                    pe.wait_ge(x_in, 32)
                if n == 6:
                    pe.wait_ge(rows_in, 16 * 12)
                if n >= 8:
                    pe.wait_ge(S1["dve" if n % 2 == 0 else "act"].sem, S1["dve" if n % 2 == 0 else "act"].count(f"g{n - 8}"))
                for src, r, col in items:
                    last = pe.transpose(psum[:, n % 8, col:col + r], src, ident[0:r, 0:r])
                last.then_inc(S1["pe"].sem, S1["pe"].step(f"g{n}"))

        def copy_turned(eng, kind):
            for n, (pitch, dst, items, rows) in enumerate(turns):
                if n % 2 != (kind == "act"):
                    continue
                eng.wait_ge(S1["pe"].sem, S1["pe"].count(f"g{n}"))
                a, b = dst[0].shape[1], dst[0].shape[2]
                if pitch:
                    src = psum[:, n % 8, :].rearrange("p (a b) -> p a b", a=4)[:, :, 0:rows]
                else:
                    src = psum[:, n % 8, 0:a * b].rearrange("p (a b) -> p a b", a=a)
                ins_ = eng.tensor_copy(dst[0], src) if kind == "dve" else eng.copy(dst[0], src)
                ins_.then_inc(S1[kind].sem, S1[kind].step(f"g{n}"))

        def dve_prepare(dve):
            dve.memset(eps_col, EPS)
            dve.memset(xpg[0][:, 0:GP], 0.0).then_inc(lane_free[0], 2)
            dve.memset(xpg[1][:, 0:GP], 0.0).then_inc(lane_free[1], 2)

        def norm_stage(name, which):
            s = dict(act=steps(f"{name}_act", ["square", "root"]),
                     pe=steps(f"{name}_pe", ["sum"]),
                     dve=steps(f"{name}_dve", ["inverse", "scaled"]))

            def act(eng):
                eng.activation(hT, xT, ACT.Square).then_inc(s["act"].sem, s["act"].step("square"))
                eng.wait_ge(s["pe"].sem, s["pe"].count("sum"))
                eng.activation(rinv, psum[:, 0, 0:T], ACT.Sqrt, bias=eps_col, scale=1.0 / D).then_inc(s["act"].sem, s["act"].step("root"))

            def pe(eng):
                eng.wait_ge(s["act"].sem, s["act"].count("square"))
                for k in range(KD):
                    last = eng.matmul(psum[:, 0, 0:T], ones, hT[:, k, :], start=(k == 0), stop=(k == KD - 1))
                last.then_inc(s["pe"].sem, s["pe"].step("sum"))

            def dve(eng):
                eng.wait_ge(s["act"].sem, s["act"].count("root"))
                eng.reciprocal(rinv, rinv).then_inc(s["dve"].sem, s["dve"].step("inverse"))
                eng.wait_ge(s["dve"].sem, s["dve"].count("inverse"))
                for k in range(KD):
                    last = eng.scalar_tensor_tensor(out=hT[:, k, :], in0=xT[:, k, :], scalar=norm_w[:, k, which:which + 1],
                                                    in1=rinv, op0=ALU.mult, op1=ALU.mult)
                last.then_inc(s["dve"].sem, s["dve"].step("scaled"))
            return pe, act, dve

        half_before, lane_before = {}, [{}, {}]
        h, ln = 0, [0, 0]
        for name, (w0, n) in UNITS.items():
            two = not ("out" in name and name == "gdn_out" or "down" in name)
            half_before[name] = h
            lane_before[0][name], lane_before[1][name] = ln
            h += n * two
            ln = [ln[0] + n * two, ln[1] + n]

        def stream(sp, name, source):
            w0, n = UNITS[name]

            def load(i, j, fresh=False):
                if not fresh:
                    sp.wait_ge(unit_done, w0 + 4 * i + j - RING + 1)
                for dst, src in source(4 * i + j, slot(w0 + j)):
                    sp.dma_start(dst, src).then_inc(w_in[(w0 + j) % RING], 16)

            first = 1 if w0 == 0 else 0
            for j in range(4 * first):
                load(0, j, fresh=True)
            with sp.Fori(first, n // 4) as i:
                for j in range(4):
                    load(i, j)
            for j in range(n % 4):
                load(n // 4, j)

        tile_done = (half_done, unit_done)

        def landed_count(name, i, j):
            w = UNITS[name][0] + j
            more = 32 if w >= UNITS["nsa_in"][0] else 0
            return 32 * (w // RING + i + 1) + more

        def free_count(name, i, j, l):
            return lane_before[l][name] + 4 * i + j + 1

        def read_count(name, i, j, l):
            return lane_before[l][name] + 4 * i + j + 3

        def product_count(name, i, j, l):
            if l == 0:
                return half_before[name] + 4 * i + j + 1
            return UNITS[name][0] + 4 * i + j + 1

        def bank(name, j, l):
            return psum[:, 2 * l + (UNITS[name][0] + j) % 2, :]

        def one(ap):
            return ap.rearrange("p o t -> p (o t)")

        def multiply_unit(pe, name, i, j, lhs, rhs, kn, lanes=(0, 1)):
            pe.wait_ge(w_in[(UNITS[name][0] + j) % RING], landed_count(name, i, j))
            sl = slot(UNITS[name][0] + j)
            for l in lanes:
                pe.wait_ge(lane_free[l], free_count(name, i, j, l))
                for k in range(kn):
                    last = pe.matmul(bank(name, j, l)[:, 0:T], lhs(sl, k, l), rhs[:, k, :],
                                     start=(k == 0), stop=(k == kn - 1))
                last.then_inc(half_done if l == 0 else unit_done, 1)

        def pair_tile(sl, k, l):
            return sl[:, 0:KD * 256].rearrange("p (k n) -> p k n", k=KD)[:, k, l * P:(l + 1) * P]

        def pair_source(w):
            v = w.rearrange("(k p) n -> p k n", p=P)

            def source(n, sl):
                dst = sl[:, 0:KD * 256].rearrange("p (k n) -> p k n", k=KD)
                return [(dst[:, h:h + 4, :], v[:, h:h + 4, bass.ds(n * 256, 256)]) for h in (0, 4)]
            return source

        def single_source(w, kn):
            v = w.rearrange("(k p) n -> p k n", p=P)
            m = kn // 2

            def source(n, sl):
                dst = sl[:, 0:kn * P].rearrange("p (k n) -> p k n", k=kn)
                return [(dst[:, a:b, :], v[:, a:b, bass.ds(n * P, P)]) for a, b in ((0, m), (m, kn))]
            return source

        def single_tile(kn):
            return lambda sl, k, l: sl[:, 0:kn * P].rearrange("p (k n) -> p k n", k=kn)[:, k, :]

        def padded(xp, hist):
            return xp[:, hist + TP:hist + TP + NB * (hist + TQ)].rearrange("p (b c) -> p b c", b=NB)

        def take_in(act, src, xp, tail, state, hist):
            pad = padded(xp, hist)
            act.copy(pad[:, :, 0:hist], state)
            act.copy(xp[:, hist:hist + TP], src[:, 0:TP])
            act.copy(tail[:, 0:hist], src[:, TP - hist:TP])
            act.copy(pad[:, :, hist:hist + TQ], seqs(src[:, TP:T]))
            return act.copy(tail[:, hist:hist + NB * hist].rearrange("p (b c) -> p b c", b=NB),
                            seqs(src[:, TP:T])[:, :, TQ - hist:TQ])

        def conv(dve, taps_done, it, tag, xp, y, taps, hist):
            pad = padded(xp, hist)
            for n in range(hist + 1):
                for part in "ps":
                    src = xp[:, n:n + TP] if part == "p" else pad[:, :, n:n + TQ]
                    dst = y[:, 0:TP] if part == "p" else seqs(y[:, TP:T])
                    if n == 0:
                        ins_ = dve.tensor_scalar(dst, src, taps(0), None, ALU.mult)
                    else:
                        dve.wait_ge(taps_done.sem, taps_done.count(f"{tag}t{n - 1}{part}", it))
                        ins_ = dve.scalar_tensor_tensor(out=dst, in0=src, scalar=taps(n), in1=dst,
                                                        op0=ALU.mult, op1=ALU.add)
                    ins_.then_inc(taps_done.sem, taps_done.step(f"{tag}t{n}{part}"))

        def conv_steps(tag, hist):
            return [f"{tag}t{n}{part}" for n in range(hist + 1) for part in "ps"]

        space.at = phase
        qkv = space.take(NCT, T)
        z = space.take(VH, T)
        core = space.at
        conv_rows = space.take(CONV_CH, parts=NB * GP + GP)
        BT = 8
        S3 = dict(pe=steps("gdn_tails_turned", ["tails"]),
                  act=steps("gdn_silu", [f"silu{j}" for j in range(BT)] + ["rows"], loop=True),
                  dve=steps("gdn_conv", [x for j in range(BT) for x in conv_steps(f"{j}", GP)]))
        ab_done = sem("ab_done")
        NQ = NCT // BT

        def pe_gdn_in(pe):
            with pe.Fori(0, NQ) as i:
                for j in range(4):
                    multiply_unit(pe, "gdn_in", i, j, pair_tile, hT, KD)
                pe.wait_ge(lane_free[1], read_count("gdn_in", i, 3, 1))
                for j in range(BT):
                    last = pe.transpose(psum[0:27, 4 + j // 4, (j % 4) * P:(j % 4 + 1) * P], tails[:, j, :], ident)
                last.then_inc(S3["pe"].sem, S3["pe"].step("tails"))
            with pe.Fori(NQ, 6) as i:
                for j in range(4):
                    multiply_unit(pe, "gdn_in", i, j, pair_tile, hT, KD)
            pe.wait_ge(small_in, 16 * 4)
            for half in range(2):
                for k in range(KD):
                    last = pe.matmul(psum[0:VH, 6 + half, 0:T], w_ab[:, k, half * VH:(half + 1) * VH], hT[:, k, :],
                                     start=(k == 0), stop=(k == KD - 1))
            last.then_inc(ab_done, 1)

        def act_gdn_in(act):
            act.sem_inc(S3["act"].sem, 1)

            def silu(i, j):
                act.wait_ge(S3["dve"].sem, S3["dve"].count(f"{j}t{GP}s", i))
                act.activation(one(qkv[:, bass.ds(8 * i + j, 1), :]), conv_y[j % 2], ACT.Silu).then_inc(S3["act"].sem, S3["act"].step(f"silu{j}"))
            with act.Fori(0, NQ) as i:
                for j in range(BT):
                    act.wait_ge(tile_done[j % 2], product_count("gdn_in", i, j // 2, j % 2))
                    state = gconv[:, bass.ds(8 * i + j, 1), 0:NB * GP].rearrange("p o (b c) -> p (o b) c", b=NB)
                    last = take_in(act, bank("gdn_in", j // 2, j % 2), xpg[j % 2], tails[:, j, :], state, GP)
                    last.then_inc(lane_free[j % 2], 1)
                    if j:
                        silu(i, j - 1)
                silu(i, BT - 1)
                act.wait_ge(S3["pe"].sem, S3["pe"].count("tails", i))
                act.copy(conv_rows[:, bass.ds(1024 * i, 1024)].rearrange("p (a b) -> p a b", a=2),
                                        psum[0:27, 4:6, :]).then_inc(S3["act"].sem, S3["act"].step("rows"))
            with act.Fori(NQ, 6) as i:
                for j in range(BT):
                    act.wait_ge(tile_done[j % 2], product_count("gdn_in", i, j // 2, j % 2))
                    act.activation(one(z[:, bass.ds(8 * i + j - NCT, 1), :]), bank("gdn_in", j // 2, j % 2)[:, 0:T],
                                   ACT.Silu).then_inc(lane_free[j % 2], 1)

        def dve_gdn_in(dve):
            with dve.Fori(0, NQ) as i:
                for j in range(BT):
                    dve.wait_ge(lane_free[j % 2], read_count("gdn_in", i, j // 2, j % 2))
                    if j >= 2:
                        dve.wait_ge(S3["act"].sem, S3["act"].count(f"silu{j - 2}", i))
                    else:
                        dve.wait_ge(S3["act"].sem, S3["act"].all_before(i))
                    conv(dve, S3["dve"], i, f"{j}", xpg[j % 2], conv_y[j % 2],
                         lambda n: one(gconv[:, bass.ds(8 * i + j, 1), NB * GP + n:NB * GP + n + 1]), GP)

        def pool_gdn_rows(pool):
            pool.wait_ge(S3["act"].sem, S3["act"].count("rows", NQ - 1))
            pool.dma_start(outs["gdn_conv_prompt"].rearrange("l b w c -> (l b w) c"), conv_rows[0:GP, :]).then_inc(stored, 16)
            pool.dma_start(outs["gdn_conv_sample"].rearrange("l b w c -> (l b w) c"), conv_rows[GP:27, :]).then_inc(stored, 16)
            n_stored[0] += 2
            pool.wait_ge(stored, 16 * n_stored[0])

        space.at = core
        rows4 = space.take(4, T, parts=VH)
        gtok = space.take(3, 4, VH)
        scratch = space.at
        gx = [space.take(T, parts=VH) for _ in range(4)]
        ea = space.take(1, parts=VH)
        sq = space.take(4, T)
        inv = space.take(4, T)
        C_G, C_B, C_E, C_N = range(4)
        S4 = dict(pe=steps("gates_pe", ["turned"] + [f"sum{g}" for g in range(4)]),
                  dve=steps("gates_dve", ["pad", "dt", "relu", "den", "beta", "soft", "g", "scan", "gap0", "gap", "nb", "tok", "toks"]
                            + [f"{x}{g}" for g in range(4) for x in ("eps", "inv", "out")]),
                  act=steps("gates_act", ["nbexp", "abs", "expn", "log", "ea", "egap", "eg"]
                            + [f"{x}{g}" for g in range(4) for x in ("sq", "root")]))

        def act_gates(act):
            act_steps, dve_steps = S4["act"], S4["dve"]
            act.wait_ge(ab_done, 1)
            act.wait_ge(small_in, 16 * 4)
            act.activation(gx[0], psum[0:VH, 7, 0:T], ACT.Exp, scale=-1.0).then_inc(act_steps.sem, act_steps.step("nbexp"))
            act.wait_ge(dve_steps.sem, dve_steps.count("dt"))
            act.activation(gx[2], gx[1], ACT.Abs).then_inc(act_steps.sem, act_steps.step("abs"))
            act.wait_ge(act_steps.sem, act_steps.count("abs"))
            act.activation(gx[2], gx[2], ACT.Exp, scale=-1.0).then_inc(act_steps.sem, act_steps.step("expn"))
            act.wait_ge(act_steps.sem, act_steps.count("expn"))
            act.activation(gx[2], gx[2], ACT.Ln, bias=1.0).then_inc(act_steps.sem, act_steps.step("log"))
            act.activation(ea, a_log, ACT.Exp).then_inc(act_steps.sem, act_steps.step("ea"))
            act.wait_ge(dve_steps.sem, dve_steps.count("gap"))
            act.activation(rows4[:, C_E, :], gx[3], ACT.Exp).then_inc(act_steps.sem, act_steps.step("egap"))
            act.activation(gx[1], rows4[:, C_G, :], ACT.Exp).then_inc(act_steps.sem, act_steps.step("eg"))
            for g in range(4):
                if g:
                    act.wait_ge(S4["pe"].sem, S4["pe"].count(f"sum{g - 1}"))
                act.activation(sq, qkv[:, 4 * g:4 * g + 4, :], ACT.Square).then_inc(act_steps.sem, act_steps.step(f"sq{g}"))
                act.wait_ge(dve_steps.sem, dve_steps.count(f"eps{g}"))
                act.activation(inv, inv, ACT.Sqrt).then_inc(act_steps.sem, act_steps.step(f"root{g}"))

        def dve_gates(dve):
            dve_steps, act_steps = S4["dve"], S4["act"]
            dve.memset(gtok, 0.0).then_inc(dve_steps.sem, dve_steps.step("pad"))
            dve.wait_ge(ab_done, 1)
            dve.wait_ge(small_in, 16 * 4)
            dve.tensor_scalar(gx[1], psum[0:VH, 6, 0:T], dt_bias, None, ALU.add).then_inc(dve_steps.sem, dve_steps.step("dt"))
            dve.wait_ge(dve_steps.sem, dve_steps.count("dt"))
            dve.tensor_scalar(gx[3], gx[1], 0.0, None, ALU.max).then_inc(dve_steps.sem, dve_steps.step("relu"))
            dve.wait_ge(act_steps.sem, act_steps.count("nbexp"))
            dve.tensor_scalar(gx[0], gx[0], 1.0, None, ALU.add).then_inc(dve_steps.sem, dve_steps.step("den"))
            dve.wait_ge(dve_steps.sem, dve_steps.count("den"))
            dve.reciprocal(rows4[:, C_B, :], gx[0]).then_inc(dve_steps.sem, dve_steps.step("beta"))
            dve.wait_ge(act_steps.sem, act_steps.count("ea"))
            dve.tensor_tensor(gx[3], gx[3], gx[2], ALU.add).then_inc(dve_steps.sem, dve_steps.step("soft"))
            dve.wait_ge(dve_steps.sem, dve_steps.count("soft"))
            dve.tensor_scalar(gx[3], gx[3], ea, -1.0, ALU.mult, ALU.mult).then_inc(dve_steps.sem, dve_steps.step("g"))
            dve.wait_ge(dve_steps.sem, dve_steps.count("g"))
            dve.tensor_tensor_scan(rows4[:, C_G, :], const("carry", VH), gx[3], 0.0, ALU.mult, ALU.add).then_inc(dve_steps.sem, dve_steps.step("scan"))
            dve.wait_ge(dve_steps.sem, dve_steps.count("scan"))
            g = rows4[:, C_G, :]
            dve.tensor_tensor(gx[3][:, 0:TP].rearrange("p (a b) -> p a b", a=2),
                                     g[:, P - 1:TP:P].unsqueeze(2).to_broadcast([VH, 2, P]),
                                     g[:, 0:TP].rearrange("p (a b) -> p a b", a=2), ALU.subtract).then_inc(dve_steps.sem, dve_steps.step("gap0"))
            dve.tensor_tensor(seqs(gx[3][:, TP:T]), g[:, TP + TQ - 1:T:TQ].unsqueeze(2).to_broadcast([VH, NB, TQ]),
                                     seqs(g[:, TP:T]), ALU.subtract).then_inc(dve_steps.sem, dve_steps.step("gap"))
            dve.wait_ge(act_steps.sem, act_steps.count("eg"))
            dve.scalar_tensor_tensor(out=rows4[:, C_N, :], in0=rows4[:, C_B, :], scalar=-1.0, in1=gx[1],
                                            op0=ALU.mult, op1=ALU.mult).then_inc(dve_steps.sem, dve_steps.step("nb"))
            dve.wait_ge(S4["pe"].sem, S4["pe"].count("turned"))
            turned = psum[:, 5, 0:3 * 4 * VH].rearrange("p (u c h) -> p u c h", u=3, c=4)
            dve.tensor_copy(gtok[:, 0:2], turned[:, 0:2]).then_inc(dve_steps.sem, dve_steps.step("tok"))
            dve.tensor_copy(gtok[0:TS, 2], turned[0:TS, 2]).then_inc(dve_steps.sem, dve_steps.step("toks"))
            for g in range(4):
                dve.wait_ge(S4["pe"].sem, S4["pe"].count(f"sum{g}"))
                if g:
                    dve.wait_ge(dve_steps.sem, dve_steps.count(f"out{g - 1}"))
                dve.tensor_scalar(inv, psum[:, 0:4, 0:T], EPS, None, ALU.add).then_inc(dve_steps.sem, dve_steps.step(f"eps{g}"))
                dve.wait_ge(act_steps.sem, act_steps.count(f"root{g}"))
                dve.reciprocal(inv, inv).then_inc(dve_steps.sem, dve_steps.step(f"inv{g}"))
                dve.wait_ge(dve_steps.sem, dve_steps.count(f"inv{g}"))
                t = qkv[:, 4 * g:4 * g + 4, :]
                dve.scalar_tensor_tensor(out=t, in0=inv, scalar=float(DK) ** -0.5 if g < 2 else 1.0, in1=t,
                                                op0=ALU.mult, op1=ALU.mult).then_inc(dve_steps.sem, dve_steps.step(f"out{g}"))

        def pe_gates(pe):
            act_steps, dve_steps = S4["act"], S4["dve"]
            pe.wait_ge(dve_steps.sem, dve_steps.count("nb"))
            for u, (c0, n) in enumerate(((0, P), (P, P), (TP, TS))):
                for c in range(4):
                    at = (u * 4 + c) * VH
                    last = pe.transpose(psum[0:n, 5, at:at + VH], rows4[:, c, c0:c0 + n], ident[0:VH, 0:VH])
            last.then_inc(S4["pe"].sem, S4["pe"].step("turned"))
            for g in range(4):
                pe.wait_ge(act_steps.sem, act_steps.count(f"sq{g}"))
                if g:
                    pe.wait_ge(dve_steps.sem, dve_steps.count(f"eps{g - 1}"))
                for j in range(4):
                    last = pe.matmul(psum[:, j, 0:T], ones, sq[:, j, :], start=True, stop=True)
                last.then_inc(S4["pe"].sem, S4["pe"].step(f"sum{g}"))

        space.at = scratch
        W3 = 3 * P
        kS = space.take(W3)
        qS = space.take(T)
        hd = []
        for _ in range(2):
            start = space.at
            h = dict(X=space.take(T), v=space.take(W3), at=space.take(W3), bts=space.take(W3), egc=space.take(T),
                     qkd=space.take(T), qd=space.take(T), kdec=space.take(3, P), S=space.take(2, P), S0=space.take(NB, P))
            h["spread"] = space.take(NB, P, off=start)
            h["rows"] = space.take(2, T, parts=VH, off=space.at)
            h["R"], h["vn"] = space.take(3, P), space.take(3, P)
            hd.append(h)
        ktok = space.take(3, P)
        kmask = kmask_space.rearrange("p (b c) -> p b c", b=NB)
        for h in hd:
            h["P"] = h["bts"]
            h["Y"] = space.take(W3)
            h["dec"] = h["Y"][:, 0:T]
        row_src = [h["rows"] for h in hd]
        o_heads = qkv[:, 2 * QKH:, :]
        LEVELS = 7
        width = lambda k: T if k < 3 else TP
        both = lambda names: [f"{x}{h}" for x in names for h in range(2)]
        S5 = dict(
            pe=steps("core_pe", ["gram", "ktok"] + both(["rows"]) + both(["at"])
                     + [f"{x}{k}{h}" for k in range(1, LEVELS) for x in "pxy" for h in range(2) if not (x == "x" and k == LEVELS - 1)]
                     + both(["vtok", "ks", "v0", "s1", "ks1", "v1", "s2", "o"]) + both(["snew"]), loop=True),
            dve=steps("core_dve", both(["row", "bts", "d", "cd", "at1", "at2", "qkd", "qd", "ya", "yb", "xa", "xb"])
                      + [f"{x}{k}{h}" for k in range(1, LEVELS) for x in "pxy" for h in range(2) if not (x == "x" and k == LEVELS - 1)]
                      + both(["rs", "vn0", "vns", "s1", "r1", "vn1", "s2"]) + both(["snew"]), loop=True),
            act=steps("core_act", ["k", "q"] + both(["v"]) + ["ktok"] + both(["egc", "dec", "kdec", "r"]) + both(["o"]), loop=True),
            pool=steps("core_pool", ["kmask", "s0g0", "spread0", "s0g1", "spread1"], loop=True))
        state_in, state_out, pads = sem("states_in"), sem("states_out"), sem("core_pads")
        PB = [(2, 3, 4), (5, 6, 7)]

        STATES = 64

        def pe_core(pe):
            pe_steps, dve_steps, act_steps, pool_steps = S5["pe"], S5["dve"], S5["act"], S5["pool"]
            chunk = [(0, P), (P, P), (TP, TS)]
            pe.sem_inc(pe_steps.sem, 1)
            pe.wait_ge(pads, 9)
            with pe.Fori(0, QKH) as i:
                pe.wait_ge(act_steps.sem, act_steps.count("v1", i))
                pe.wait_ge(dve_steps.sem, dve_steps.all_before(i))
                for rhs, b in ((kS, 0), (qS, 1)):
                    for c0, n in chunk:
                        last = pe.matmul(psum[:, b, c0:c0 + n], kS[:, c0:c0 + P], rhs[:, c0:c0 + n], start=True, stop=True)
                last.then_inc(pe_steps.sem, pe_steps.step("gram"))
                for u in range(3):
                    last = pe.transpose(psum[:, 4, u * P:(u + 1) * P], kS[:, u * P:(u + 1) * P], ident)
                last.then_inc(pe_steps.sem, pe_steps.step("ktok"))
                for h in range(2):
                    if h == 0:
                        pe.wait_ge(act_steps.sem, act_steps.all_before(i))
                    pe.wait_ge(dve_steps.sem, dve_steps.count(f"row{h}", i))
                    for q in range(2):
                        last = pe.matmul(psum[:, PB[h][q], 0:T], ones[0:VH, :], row_src[h][:, q, :], start=True, stop=True)
                    last.then_inc(pe_steps.sem, pe_steps.step(f"rows{h}"))
                for h in range(2):
                    pe.wait_ge(dve_steps.sem, dve_steps.count(f"at2{h}", i))
                    if h == 0:
                        pe.wait_ge(act_steps.sem, act_steps.count("ktok", i))
                    for u in range(3):
                        last = pe.transpose(psum[:, PB[h][2], u * P:(u + 1) * P], hd[h]["at"][:, u * P:(u + 1) * P], ident)
                    last.then_inc(pe_steps.sem, pe_steps.step(f"at{h}"))
                for k in range(1, LEVELS):
                    cs = chunk if k < 3 else chunk[:2]
                    for h in range(2):
                        d = hd[h]
                        pe.wait_ge(dve_steps.sem, dve_steps.count(f"xb{h}" if k == 1 else f"x{k - 1}{h}", i))
                        for c0, n in cs:
                            last = pe.matmul(psum[:, PB[h][0], c0:c0 + n], d["at"][:, c0:c0 + P], d["X"][:, c0:c0 + n], start=True, stop=True)
                        last.then_inc(pe_steps.sem, pe_steps.step(f"p{k}{h}"))
                    if k < LEVELS - 1:
                        for h in range(2):
                            d = hd[h]
                            pe.wait_ge(dve_steps.sem, dve_steps.count(f"p{k}{h}", i))
                            if k > 1:
                                pe.wait_ge(dve_steps.sem, dve_steps.count(f"y{k - 1}{h}", i))
                            for c0, n in cs:
                                last = pe.matmul(psum[:, PB[h][1], c0:c0 + n], d["Y"][:, c0:c0 + P], d["P"][:, c0:c0 + n], start=True, stop=True)
                            last.then_inc(pe_steps.sem, pe_steps.step(f"x{k}{h}"))
                    for h in range(2):
                        d = hd[h]
                        pe.wait_ge(dve_steps.sem, dve_steps.count(f"p{k}{h}", i))
                        if k == LEVELS - 1:
                            pe.wait_ge(dve_steps.sem, dve_steps.count(f"y{k - 1}{h}", i))
                        for c0, n in cs:
                            last = pe.matmul(psum[:, PB[h][2], c0:c0 + n], d["P"][:, c0:c0 + P], d["Y"][:, c0:c0 + n], start=True, stop=True)
                        last.then_inc(pe_steps.sem, pe_steps.step(f"y{k}{h}"))
                for h in range(2):
                    pe.wait_ge(dve_steps.sem, dve_steps.count(f"p{LEVELS - 1}{h}", i))
                    for u in range(3):
                        last = pe.transpose(psum[:, PB[h][0], u * P:(u + 1) * P], hd[h]["v"][:, u * P:(u + 1) * P], ident)
                    last.then_inc(pe_steps.sem, pe_steps.step(f"vtok{h}"))
                for h in range(2):
                    pe.wait_ge(pool_steps.sem, pool_steps.count("kmask", i))
                    pe.wait_ge(state_in, 32 * (i + 1))
                    for b in range(NB):
                        last = pe.matmul(psum[0:TS, PB[h][1], 0:P], kmask[:, b, :], hd[h]["S0"][:, b, :], start=(b == 0), stop=(b == NB - 1))
                    last.then_inc(pe_steps.sem, pe_steps.step(f"ks{h}"))
                for h in range(2):
                    d = hd[h]
                    pe.wait_ge(dve_steps.sem, dve_steps.count(f"rs{h}", i))
                    pe.wait_ge(dve_steps.sem, dve_steps.count(f"y{LEVELS - 1}{h}", i))
                    pe.wait_ge(act_steps.sem, act_steps.count(f"r{h}", i))
                    pe.matmul(psum[:, PB[h][1], P:2 * P], d["Y"][:, 0:P], d["R"][:, 0, :], start=True, stop=True)
                    last = pe.matmul(psum[0:TS, PB[h][1], 2 * P:3 * P], d["Y"][0:TS, TP:T], d["R"][0:TS, 2, :], start=True, stop=True)
                    last.then_inc(pe_steps.sem, pe_steps.step(f"v0{h}"))
                for h in range(2):
                    d = hd[h]
                    pe.wait_ge(dve_steps.sem, dve_steps.count(f"vn0{h}", i))
                    pe.matmul(psum[:, PB[h][2], 0:P], d["kdec"][:, 0, :], d["vn"][:, 0, :], start=True, stop=True).then_inc(pe_steps.sem, pe_steps.step(f"s1{h}"))
                for h in range(2):
                    d = hd[h]
                    pe.wait_ge(dve_steps.sem, dve_steps.count(f"s1{h}", i))
                    pe.matmul(psum[:, PB[h][2], P:2 * P], kS[:, P:2 * P], d["S"][:, 0, :], start=True, stop=True).then_inc(pe_steps.sem, pe_steps.step(f"ks1{h}"))
                for h in range(2):
                    d = hd[h]
                    pe.wait_ge(dve_steps.sem, dve_steps.count(f"r1{h}", i))
                    pe.matmul(psum[:, PB[h][2], 2 * P:3 * P], d["Y"][:, P:2 * P], d["R"][:, 1, :], start=True, stop=True).then_inc(pe_steps.sem, pe_steps.step(f"v1{h}"))
                for h in range(2):
                    d = hd[h]
                    pe.wait_ge(dve_steps.sem, dve_steps.count(f"vn1{h}", i))
                    pe.matmul(psum[:, PB[h][2], 3 * P:4 * P], d["kdec"][:, 1, :], d["vn"][:, 1, :], start=True, stop=True).then_inc(pe_steps.sem, pe_steps.step(f"s2{h}"))
                for h in range(2):
                    d, o = hd[h], psum[:, PB[h][0], :]
                    pe.matmul(o[:, 0:P], d["vn"][:, 0, :], d["qkd"][:, 0:P], start=True, stop=True)
                    pe.matmul(o[:, P:TP], d["vn"][:, 1, :], d["qkd"][:, P:TP], start=True, stop=False)
                    pe.matmul(o[:, P:TP], d["S"][:, 0, :], d["qd"][:, P:TP], start=False, stop=True)
                    pe.matmul(o[:, TP:T], d["vn"][0:TS, 2, :], d["qkd"][0:TS, TP:T], start=True, stop=True, skip_group_check=True)
                    for b in range(NB):
                        c = TP + b * TQ
                        last = pe.matmul(o[:, c:c + TQ], d["S0"][:, b, :], d["qd"][:, c:c + TQ], start=False, stop=True,
                                         skip_group_check=True)
                    last.then_inc(pe_steps.sem, pe_steps.step(f"o{h}"))
                for h in range(2):
                    d = hd[h]
                    pe.wait_ge(pool_steps.sem, pool_steps.count(f"spread{h}", i))
                    if h:
                        pe.wait_ge(dve_steps.sem, dve_steps.count("snew0", i))
                    for x in range(2):
                        last = pe.matmul(psum[:, x, :], d["kdec"][0:TS, 2, :],
                                         d["spread"][0:TS, 4 * x:4 * x + 4, :].rearrange("p a b -> p (a b)"), start=True, stop=True)
                    last.then_inc(pe_steps.sem, pe_steps.step(f"snew{h}"))

        def act_core(act):
            act_steps, dve_steps, pe_steps = S5["act"], S5["dve"], S5["pe"]
            new = outs["gdn_s_sample"].rearrange("l b h k v -> (l h) k b v")
            first = outs["gdn_s_prompt"].rearrange("l b h k v -> (l b h) k v")
            act.sem_inc(act_steps.sem, 1)
            act.sem_inc(state_out, 16)
            with act.Fori(0, QKH) as i:
                act.wait_ge(pe_steps.sem, pe_steps.all_before(i))
                act.copy(kS[:, 0:T], one(qkv[:, bass.ds(QKH + i, 1), :])).then_inc(act_steps.sem, act_steps.step("k"))
                act.copy(qS, one(qkv[:, bass.ds(i, 1), :])).then_inc(act_steps.sem, act_steps.step("q"))
                for h in range(2):
                    act.copy(hd[h]["v"][:, 0:T], one(qkv[:, bass.ds(2 * QKH + 2 * i + h, 1), :])).then_inc(act_steps.sem, act_steps.step(f"v{h}"))
                act.wait_ge(pe_steps.sem, pe_steps.count("ktok", i))
                act.copy(ktok, psum[:, 4, 0:W3].rearrange("p (u c) -> p u c", u=3)).then_inc(act_steps.sem, act_steps.step("ktok"))
                for h in range(2):
                    act.wait_ge(pe_steps.sem, pe_steps.count(f"rows{h}", i))
                    act.wait_ge(S5["pool"].sem, S5["pool"].all_before(i))
                    act.activation(hd[h]["egc"], psum[:, PB[h][0], 0:T], ACT.Exp).then_inc(act_steps.sem, act_steps.step(f"egc{h}"))
                for h in range(2):
                    act.wait_ge(dve_steps.sem, dve_steps.count(f"d{h}", i))
                    act.activation(hd[h]["dec"], hd[h]["dec"], ACT.Exp).then_inc(act_steps.sem, act_steps.step(f"dec{h}"))
                act.wait_ge(act_steps.sem, act_steps.count("ktok", i))
                for h in range(2):
                    for u in range(3):
                        last = act.activation(hd[h]["kdec"][:, u, :], ktok[:, u, :], ACT.Copy, scale=gtok[:, u, C_E, bass.ds(2 * i + h, 1)])
                    last.then_inc(act_steps.sem, act_steps.step(f"kdec{h}"))
                for h in range(2):
                    act.wait_ge(pe_steps.sem, pe_steps.count(f"vtok{h}", i))
                    for u in range(3):
                        r = P if u < 2 else TS
                        last = act.activation(hd[h]["R"][0:r, u, :], psum[0:r, PB[h][0], u * P:(u + 1) * P], ACT.Copy,
                                              scale=gtok[0:r, u, C_B, bass.ds(2 * i + h, 1)])
                    last.then_inc(act_steps.sem, act_steps.step(f"r{h}"))
                for h in range(2):
                    act.wait_ge(pe_steps.sem, pe_steps.count(f"o{h}", i))
                    act.copy(one(o_heads[:, bass.ds(2 * i + h, 1), :]), psum[:, PB[h][0], 0:T]).then_inc(act_steps.sem, act_steps.step(f"o{h}"))
                for h in range(2):
                    act.wait_ge(dve_steps.sem, dve_steps.count(f"snew{h}", i))
                    act.dma_start(new[bass.ds(2 * i + h, 1)].rearrange("o k b v -> (o k) b v"), hd[h]["S0"]).then_inc(state_out, 16)
                    act.dma_start(first[bass.ds(2 * i + h, 1)].rearrange("o k v -> (o k) v"), hd[h]["S"][:, 1, :]).then_inc(state_out, 16)

        def dve_core(dve):
            dve_steps, pe_steps, act_steps, pool_steps = S5["dve"], S5["pe"], S5["act"], S5["pool"]
            dve.sem_inc(dve_steps.sem, 1)
            dve.memset(kS[:, T:W3], 0.0).then_inc(pads, 1)
            for h in hd:
                for name in ("v", "at", "bts", "Y"):
                    dve.memset(h[name][:, T:W3], 0.0).then_inc(pads, 1)
            dve.wait_ge(pads, 9)
            w3 = lambda ap, w: ap[:, 0:w]
            col = lambda parts, u, c, i, h: gtok[0:parts, u, c, bass.ds(2 * i + h, 1)]
            with dve.Fori(0, QKH) as i:
                for h in range(2):
                    dve.wait_ge(pe_steps.sem, pe_steps.all_before(i))
                    dve.tensor_scalar(row_src[h], rows4[:, 0:2, :], ident[0:VH, bass.ds(2 * i + h, 1)], None, ALU.mult).then_inc(dve_steps.sem, dve_steps.step(f"row{h}"))
                for h in range(2):
                    dve.wait_ge(pe_steps.sem, pe_steps.count(f"rows{h}", i))
                    dve.tensor_tensor(hd[h]["bts"][:, 0:T], psum[:, PB[h][1], 0:T], const("strict3"), ALU.mult).then_inc(dve_steps.sem, dve_steps.step(f"bts{h}"))
                for h in range(2):
                    dve.wait_ge(act_steps.sem, act_steps.count(f"egc{h}", i))
                    for u, (c0, n) in enumerate(((0, P), (P, P), (TP, TS))):
                        last = dve.tensor_scalar(hd[h]["dec"][:, c0:c0 + n], psum[:, PB[h][0], c0:c0 + n], col(P, u, C_G, i, h), 0.0,
                                                 ALU.subtract, ALU.min)
                    last.then_inc(dve_steps.sem, dve_steps.step(f"d{h}"))
                for h in range(2):
                    dve.wait_ge(act_steps.sem, act_steps.count(f"dec{h}", i))
                    dve.tensor_tensor(hd[h]["dec"], hd[h]["dec"], const("causal3"), ALU.mult).then_inc(dve_steps.sem, dve_steps.step(f"cd{h}"))
                for h in range(2):
                    dve.wait_ge(dve_steps.sem, dve_steps.count(f"cd{h}", i))
                    dve.tensor_tensor(hd[h]["at"][:, 0:T], psum[:, 0, 0:T], hd[h]["dec"], ALU.mult).then_inc(dve_steps.sem, dve_steps.step(f"at1{h}"))
                for h in range(2):
                    dve.wait_ge(dve_steps.sem, dve_steps.count(f"at1{h}", i))
                    dve.tensor_tensor(hd[h]["at"][:, 0:T], hd[h]["at"][:, 0:T], hd[h]["bts"][:, 0:T], ALU.mult).then_inc(dve_steps.sem, dve_steps.step(f"at2{h}"))
                for h in range(2):
                    dve.tensor_tensor(hd[h]["qkd"], psum[:, 1, 0:T], hd[h]["dec"], ALU.mult).then_inc(dve_steps.sem, dve_steps.step(f"qkd{h}"))
                for h in range(2):
                    dve.wait_ge(act_steps.sem, act_steps.count(f"egc{h}", i))
                    dve.tensor_tensor(hd[h]["qd"], qS, hd[h]["egc"], ALU.mult).then_inc(dve_steps.sem, dve_steps.step(f"qd{h}"))
                for h in range(2):
                    dve.wait_ge(dve_steps.sem, dve_steps.count(f"qkd{h}", i))
                    dve.tensor_tensor(hd[h]["Y"][:, 0:T], hd[h]["at"][:, 0:T], const("level0T"), ALU.mult).then_inc(dve_steps.sem, dve_steps.step(f"ya{h}"))
                for h in range(2):
                    dve.wait_ge(dve_steps.sem, dve_steps.count(f"ya{h}", i))
                    dve.tensor_tensor(hd[h]["Y"][:, 0:T], const("eye3"), hd[h]["Y"][:, 0:T], ALU.subtract).then_inc(dve_steps.sem, dve_steps.step(f"yb{h}"))
                for h in range(2):
                    dve.wait_ge(pe_steps.sem, pe_steps.count(f"at{h}", i))
                    dve.tensor_tensor(hd[h]["X"], psum[:, PB[h][2], 0:T], const("level0"), ALU.mult).then_inc(dve_steps.sem, dve_steps.step(f"xa{h}"))
                for h in range(2):
                    dve.wait_ge(dve_steps.sem, dve_steps.count(f"xa{h}", i))
                    dve.tensor_tensor(hd[h]["X"], const("eye3"), hd[h]["X"], ALU.subtract).then_inc(dve_steps.sem, dve_steps.step(f"xb{h}"))
                for k in range(1, LEVELS):
                    n = width(k)
                    for h in range(2):
                        dve.wait_ge(pe_steps.sem, pe_steps.count(f"p{k}{h}", i))
                        if k < 3:
                            dve.tensor_tensor(hd[h]["P"][:, 0:n], psum[:, PB[h][0], 0:n], const(f"level{k}"), ALU.mult).then_inc(dve_steps.sem, dve_steps.step(f"p{k}{h}"))
                        else:
                            pair = lambda ap: ap.rearrange("p (a b) -> p a b", a=2)
                            dve.tensor_tensor(pair(hd[h]["P"][:, 0:n]), pair(psum[:, PB[h][0], 0:n]),
                                                     const(f"level{k}").unsqueeze(1).to_broadcast([P, 2, P]), ALU.mult).then_inc(dve_steps.sem, dve_steps.step(f"p{k}{h}"))
                    for x, nm, b in (("x", "X", 1), ("y", "Y", 2)):
                        if x == "x" and k == LEVELS - 1:
                            continue
                        for h in range(2):
                            dve.wait_ge(pe_steps.sem, pe_steps.count(f"{x}{k}{h}", i))
                            dve.tensor_tensor(hd[h][nm][:, 0:n], hd[h][nm][:, 0:n], psum[:, PB[h][b], 0:n], ALU.subtract).then_inc(dve_steps.sem, dve_steps.step(f"{x}{k}{h}"))
                for h in range(2):
                    dve.wait_ge(pe_steps.sem, pe_steps.count(f"ks{h}", i))
                    dve.wait_ge(act_steps.sem, act_steps.count(f"r{h}", i))
                    dve.scalar_tensor_tensor(out=hd[h]["R"][0:TS, 2, :], in0=psum[0:TS, PB[h][1], 0:P], scalar=col(TS, 2, C_N, i, h),
                                                    in1=hd[h]["R"][0:TS, 2, :], op0=ALU.mult, op1=ALU.add).then_inc(dve_steps.sem, dve_steps.step(f"rs{h}"))
                for h in range(2):
                    dve.wait_ge(pe_steps.sem, pe_steps.count(f"v0{h}", i))
                    dve.tensor_copy(hd[h]["vn"][:, 0, :], psum[:, PB[h][1], P:2 * P]).then_inc(dve_steps.sem, dve_steps.step(f"vn0{h}"))
                for h in range(2):
                    dve.tensor_copy(hd[h]["vn"][0:TS, 2, :], psum[0:TS, PB[h][1], 2 * P:3 * P]).then_inc(dve_steps.sem, dve_steps.step(f"vns{h}"))
                for h in range(2):
                    dve.wait_ge(pe_steps.sem, pe_steps.count(f"s1{h}", i))
                    dve.tensor_copy(hd[h]["S"][:, 0, :], psum[:, PB[h][2], 0:P]).then_inc(dve_steps.sem, dve_steps.step(f"s1{h}"))
                for h in range(2):
                    dve.wait_ge(pe_steps.sem, pe_steps.count(f"ks1{h}", i))
                    dve.scalar_tensor_tensor(out=hd[h]["R"][:, 1, :], in0=psum[:, PB[h][2], P:2 * P], scalar=col(P, 1, C_N, i, h),
                                                    in1=hd[h]["R"][:, 1, :], op0=ALU.mult, op1=ALU.add).then_inc(dve_steps.sem, dve_steps.step(f"r1{h}"))
                for h in range(2):
                    dve.wait_ge(pe_steps.sem, pe_steps.count(f"v1{h}", i))
                    dve.tensor_copy(hd[h]["vn"][:, 1, :], psum[:, PB[h][2], 2 * P:3 * P]).then_inc(dve_steps.sem, dve_steps.step(f"vn1{h}"))
                for h in range(2):
                    dve.wait_ge(pe_steps.sem, pe_steps.count(f"s2{h}", i))
                    dve.wait_ge(dve_steps.sem, dve_steps.count(f"s1{h}", i))
                    dve.wait_ge(state_out, STATES * i + 16)
                    dve.scalar_tensor_tensor(out=hd[h]["S"][:, 1, :], in0=hd[h]["S"][:, 0, :], scalar=hd[h]["egc"][:, TP - 1:TP],
                                                    in1=psum[:, PB[h][2], 3 * P:4 * P], op0=ALU.mult, op1=ALU.add).then_inc(dve_steps.sem, dve_steps.step(f"s2{h}"))
                for h in range(2):
                    dve.wait_ge(pe_steps.sem, pe_steps.count(f"snew{h}", i))
                    dve.wait_ge(pool_steps.sem, pool_steps.count(f"s0g{h}", i))
                    x = hd[h]["S0"].rearrange("p (x a) b -> p x (a b)", x=2)
                    dve.tensor_tensor(x, x, psum[:, 0:2, :], ALU.add).then_inc(dve_steps.sem, dve_steps.step(f"snew{h}"))

        def pool_core(pool):
            pool_steps, dve_steps, pe_steps, act_steps = S5["pool"], S5["dve"], S5["pe"], S5["act"]
            st = ins["state_gdn_s"].rearrange("l b h k v -> (l h) k b v")
            pool.sem_inc(pool_steps.sem, 1)
            with pool.Fori(0, QKH) as i:
                pool.wait_ge(state_out, STATES * i + 16)
                for h in range(2):
                    pool.dma_start(hd[h]["S0"], st[bass.ds(2 * i + h, 1)].rearrange("o k b v -> (o k) b v")).then_inc(state_in, 16)
                pool.wait_ge(act_steps.sem, act_steps.count("k", i))
                pool.tensor_tensor(kmask, const("col_seq").rearrange("p (b c) -> p b c", b=NB),
                                          kS[:, TP:T].unsqueeze(1).to_broadcast([P, NB, TS]), ALU.mult).then_inc(pool_steps.sem, pool_steps.step("kmask"))
                for h in range(2):
                    pool.wait_ge(pe_steps.sem, pe_steps.count(f"o{h}", i))
                    pool.tensor_tensor(hd[h]["S0"], hd[h]["S0"],
                                              hd[h]["egc"][:, TP + TQ - 1:T:TQ].unsqueeze(2).to_broadcast([P, NB, P]), ALU.mult).then_inc(pool_steps.sem, pool_steps.step(f"s0g{h}"))
                    pool.wait_ge(dve_steps.sem, dve_steps.count(f"vns{h}", i))
                    pool.tensor_tensor(hd[h]["spread"][0:TS], hd[h]["vn"][0:TS, 2, :].unsqueeze(1).to_broadcast([TS, NB, P]),
                                              const("tok_seq", TS).unsqueeze(2).to_broadcast([TS, NB, P]), ALU.mult).then_inc(pool_steps.sem, pool_steps.step(f"spread{h}"))
            pool.wait_ge(state_out, STATES * QKH + 16)

        space.at = scratch
        sq6 = space.take(4, T)
        inv6 = space.take(4, T)
        S6 = dict(pe=steps("gate_norm_pe", [f"sum{g}" for g in range(4)]),
                  act=steps("gate_norm_act", [f"{x}{g}" for g in range(4) for x in ("sq", "root")]),
                  dve=steps("gate_norm_dve", [f"{x}{g}" for g in range(4) for x in ("inv", "w", "out")]))

        def act_gate_norm(act):
            for g in range(4):
                if g:
                    act.wait_ge(S6["pe"].sem, S6["pe"].count(f"sum{g - 1}"))
                act.activation(sq6, o_heads[:, 4 * g:4 * g + 4, :], ACT.Square).then_inc(S6["act"].sem, S6["act"].step(f"sq{g}"))
                act.wait_ge(S6["pe"].sem, S6["pe"].count(f"sum{g}"))
                if g:
                    act.wait_ge(S6["dve"].sem, S6["dve"].count(f"w{g - 1}"))
                act.activation(inv6, psum[:, 0:4, 0:T], ACT.Sqrt, bias=eps_col, scale=1.0 / DK).then_inc(S6["act"].sem, S6["act"].step(f"root{g}"))

        def pe_gate_norm(pe):
            for g in range(4):
                pe.wait_ge(S6["act"].sem, S6["act"].count(f"sq{g}"))
                if g:
                    pe.wait_ge(S6["act"].sem, S6["act"].count(f"root{g - 1}"))
                for j in range(4):
                    last = pe.matmul(psum[:, j, 0:T], ones, sq6[:, j, :], start=True, stop=True)
                last.then_inc(S6["pe"].sem, S6["pe"].step(f"sum{g}"))

        def dve_gate_norm(dve):
            dve_steps = S6["dve"]
            for g in range(4):
                dve.wait_ge(S6["act"].sem, S6["act"].count(f"root{g}"))
                dve.reciprocal(inv6, inv6).then_inc(dve_steps.sem, dve_steps.step(f"inv{g}"))
                dve.wait_ge(dve_steps.sem, dve_steps.count(f"inv{g}"))
                t = o_heads[:, 4 * g:4 * g + 4, :]
                dve.scalar_tensor_tensor(out=t, in0=t, scalar=out_norm, in1=inv6, op0=ALU.mult, op1=ALU.mult).then_inc(dve_steps.sem, dve_steps.step(f"w{g}"))
                dve.wait_ge(dve_steps.sem, dve_steps.count(f"w{g}"))
                dve.tensor_tensor(t, t, z[:, 4 * g:4 * g + 4, :], ALU.mult).then_inc(dve_steps.sem, dve_steps.step(f"out{g}"))

        def pe_add(pe, name, act_in, kn):
            w0, n = UNITS[name]
            with pe.Fori(0, n // 4) as i:
                for j in range(4):
                    multiply_unit(pe, name, i, j, single_tile(kn), act_in, kn, lanes=(1,))

        def dve_add(dve, name):
            w0, n = UNITS[name]
            with dve.Fori(0, n // 4) as i:
                for j in range(4):
                    dve.wait_ge(unit_done, product_count(name, i, j, 1))
                    x = one(xT[:, bass.ds(4 * i + j, 1), :])
                    dve.tensor_tensor(x, x, bank(name, j, 1)[:, 0:T], ALU.add).then_inc(lane_free[1], 1)

        def ffn_up(l):
            name = f"ffn_up{l}"
            space.at = phase
            hid = space.take(NFT, T)
            rows = space.take(FF, parts=18)
            sil = [space.take(T) for _ in range(2)]
            nt = NB * FP + FP
            s = dict(pe=steps(f"ffn{l}_tails_turned", ["tails"]),
                     act=steps(f"ffn{l}_silu", [f"silu{j}" for j in range(4)] + ["rows"], loop=True),
                     dve=steps(f"ffn{l}_conv", [x for j in range(4) for x in conv_steps(f"{j}", FP)]))
            full, rest = NFT // 4, NFT % 4

            def tile(sl, k, lane):
                return sl[:, 0:KD * 256].rearrange("p (k g n) -> p k g n", k=KD, g=2)[:, k, lane, :]

            def source(n, sl):
                v = ins["ffn_w_up"][l].rearrange("(k p) (g n) -> p k g n", p=P, g=2)
                dst = sl[:, 0:KD * 256].rearrange("p (k g n) -> p k g n", k=KD, g=2)
                return [(dst[:, :, g, :], v[:, :, g, bass.ds(n * P, P)]) for g in range(2)]

            def pe(eng):
                def body(i, n):
                    for j in range(n):
                        multiply_unit(eng, name, i, j, tile, hT, KD)
                    eng.wait_ge(lane_free[0], read_count(name, i, n - 1, 0))
                    eng.wait_ge(s["act"].sem, s["act"].all_before(i))
                    for j in range(n):
                        last = eng.transpose(psum[0:nt, 4, j * P:(j + 1) * P], tails[:, j, 0:nt], ident)
                    last.then_inc(s["pe"].sem, 1)
                with eng.Fori(0, full) as i:
                    body(i, 4)
                body(full, rest)

            def act(eng):
                eng.sem_inc(s["act"].sem, 1)

                def body(i, n):
                    def silu(j):
                        eng.wait_ge(s["dve"].sem, s["dve"].count(f"{j}t{FP}s", i))
                        if j >= 2:
                            eng.wait_ge(lane_free[1], read_count(name, i, j - 2, 1))
                        else:
                            eng.wait_ge(lane_free[1], lane_before[1][name] + 4 * i + j + 1)
                        eng.activation(sil[j % 2], conv_y[j % 2], ACT.Silu).then_inc(s["act"].sem, 1)
                    for j in range(n):
                        eng.wait_ge(half_done, product_count(name, i, j, 0))
                        state = fconv[l][:, bass.ds(4 * i + j, 1), 0:NB * FP].rearrange("p o (b c) -> p (o b) c", b=NB)
                        last = take_in(eng, bank(name, j, 0), xpf[j % 2], tails[:, j, :], state, FP)
                        last.then_inc(lane_free[0], 1)
                        if j:
                            silu(j - 1)
                    silu(n - 1)
                    eng.wait_ge(s["pe"].sem, i + 1)
                    eng.copy(rows[:, bass.ds(512 * i, n * P)], psum[0:nt, 4, 0:n * P]).then_inc(s["act"].sem, 1)
                with eng.Fori(0, full) as i:
                    body(i, 4)
                body(full, rest)

            def dve(eng):
                def body(i, n):
                    def product(j):
                        eng.wait_ge(s["act"].sem, s["act"].all_before(i, j + 1))
                        eng.wait_ge(unit_done, product_count(name, i, j, 1))
                        eng.tensor_tensor(one(hid[:, bass.ds(4 * i + j, 1), :]), sil[j % 2], bank(name, j, 1)[:, 0:T],
                                          ALU.mult).then_inc(lane_free[1], 1)
                    for j in range(n):
                        eng.wait_ge(lane_free[0], read_count(name, i, j, 0))
                        if j >= 2:
                            eng.wait_ge(s["act"].sem, s["act"].all_before(i, j - 1))
                        else:
                            eng.wait_ge(s["act"].sem, s["act"].all_before(i))
                        conv(eng, s["dve"], i, f"{j}", xpf[j % 2], conv_y[j % 2],
                             lambda t: one(fconv[l][:, bass.ds(4 * i + j, 1), NB * FP + t:NB * FP + t + 1]), FP)
                        if j:
                            product(j - 1)
                    product(n - 1)
                with eng.Fori(0, full) as i:
                    body(i, 4)
                body(full, rest)

            def pool(eng):
                eng.wait_ge(s["act"].sem, s["act"].all_before(full, rest + 1))
                eng.dma_start(outs["ffn_conv_prompt"][l].rearrange("b w c -> (b w) c"), rows[0:FP, :]).then_inc(stored, 16)
                eng.dma_start(outs["ffn_conv_sample"][l].rearrange("b w c -> (b w) c"), rows[FP:nt, :]).then_inc(stored, 16)
                n_stored[0] += 2
                eng.wait_ge(stored, 16 * n_stored[0])
            return dict(pe=pe, act=act, dve=dve, pool=pool, source=source, hid=hid)

        def nsa_stages():
            space.at = phase
            n_tab = sum(n for at, n in where.values() if at >= base_cols)
            att = space.take(n_tab)

            def table(name, *dims):
                at, n = where[name]
                ap = att[:, at - base_cols:at - base_cols + n]
                if dims:
                    ap = ap.rearrange("p (a b) -> p a b", a=dims[0])
                return ap

            w2 = space.take(4, DH)
            pe_bias = space.take(4)
            ckT = space.take(2, NB * NCMP)
            cv = space.take(NB, KV_DIM, parts=NCMP)
            ckT_p = space.take(2, PCMP)
            cv_p = space.take(KV_DIM, parts=PCMP)
            past_projection = space.at
            att_in, w1_in, raw_in = sem("attention_tables_in"), sem("w1_in"), sem("raw_pages_in")

            w1 = space.take(2, 16, CHID)
            raw = space.take(STRIDE, 2 * KV_DIM)
            turned = space.take(8, 4 * P)
            NC2 = 2 * NCMP
            hid = space.take(2, 4 * NC2, off=xpg_at)
            tb_names = [f"t{v}{m}" for v in range(2) for m in range(8)]
            C = dict(
                pe=steps("cmp_pe", [x for v in range(2) for x in [f"t{v}{m}" for m in range(8)] + [f"h{v}0", f"h{v}1", f"o{v}"]], loop=True),
                dve=steps("cmp_dve", [x for v in range(2) for x in [f"t{v}{m}" for m in range(0, 8, 2)]] + ["k", "v"], loop=True),
                act=steps("cmp_act", [x for v in range(2) for x in [f"t{v}{m}" for m in range(1, 8, 2)] + [f"h{v}0", f"h{v}1"]], loop=True))
            bias_pe, bias_dve = sem("pe_bias_product"), sem("pe_bias_copied")
            kv_pages = ins["cache_nsa_kv"].rearrange("l g (n s) c j d -> (l g) n s (c j d)", s=STRIDE)

            def load_w1(pool):
                for v in range(2):
                    pool.dma_start(w1[:, v], ins["nsa_cmp_w1"][0, v].rearrange("s d h -> (s d) h").rearrange("(c p) h -> p c h", p=P)).then_inc(w1_in, 16)

            def pool_cmp(pool):
                pool.dma_start(att, ins["tables"][:, base_cols:base_cols + n_tab]).then_inc(att_in, 16)
                pool.dma_start(w2, ins["nsa_cmp_w2"][0].rearrange("v (t p) d -> p (v t) d", p=P)).then_inc(att_in, 16)
                load_w1(pool)
                with pool.Fori(0, NB // 2) as i:
                    pool.wait_ge(C["pe"].sem, C["pe"].all_before(i))
                    for b in range(2):
                        for g in range(NPG):
                            page = pool.value_load(pages_sb[0:1, bass.ds(2 * NPG * i + NPG * b + g, 1)], min_val=0, max_val=NPOOL - 1)
                            at = 64 * b + 8 * g
                            pool.dma_start(raw[at:at + 8], kv_pages[bass.ds(page, 1)].rearrange("o n s c -> (o n) s c")[:, :, 0:2 * KV_DIM]).then_inc(raw_in, 16)

            def hidden_products(pe, v, t, out, rhs):
                for half in range(2):
                    for m in range(8):
                        last = pe.matmul(out, w1[:, v, 8 * half + m, t * P:(t + 1) * P], rhs(m, half),
                                         start=(half == 0 and m == 0), stop=(half == 1 and m == 7))
                return last

            def pe_cmp(pe):
                pe_steps, dve_steps, act_steps = C["pe"], C["dve"], C["act"]
                pe.sem_inc(pe_steps.sem, 1)
                pe.wait_ge(w1_in, 32)
                for v in range(2):
                    for t in range(2):
                        for c in range(16):
                            last = pe.matmul(psum[:, 7, 2 * v + t:2 * v + t + 1], w1[:, v, c, t * P:(t + 1) * P], embed[:, 16 * v + c:16 * v + c + 1],
                                             start=(c == 0), stop=(c == 15))
                last.then_inc(bias_pe, 1)
                pe.wait_ge(bias_dve, 1)
                pe.wait_ge(att_in, 32)
                with pe.Fori(0, NB // 2) as i:
                    pe.wait_ge(raw_in, 256 * (i + 1))
                    for v in range(2):
                        for m in range(8):
                            if m >= 4:
                                pe.wait_ge((dve_steps if m % 2 == 0 else act_steps).sem, (dve_steps if m % 2 == 0 else act_steps).count(f"t{v}{m - 4}", i))
                            elif v:
                                pe.wait_ge((dve_steps if m % 2 == 0 else act_steps).sem, (dve_steps if m % 2 == 0 else act_steps).count(f"t{v - 1}{m + 4}", i))
                            else:
                                pe.wait_ge((dve_steps if m % 2 == 0 else act_steps).sem, (dve_steps if m % 2 == 0 else act_steps).all_before(i))
                            for j in range(4):
                                c0 = v * KV_DIM + (j % 2) * P
                                last = pe.transpose(psum[:, m % 4, j * P:(j + 1) * P], raw[:, 2 * m + j // 2, c0:c0 + P], ident)
                            last.then_inc(pe_steps.sem, pe_steps.step(f"t{v}{m}"))
                        pe.wait_ge(dve_steps.sem, dve_steps.count(f"t{v}6", i))
                        pe.wait_ge(act_steps.sem, act_steps.count(f"t{v}7", i))
                        blocks = lambda m, half: turned[:, m, :].rearrange("p (x n) -> p x n", x=8)[:, :, half:half + NCMP]
                        for t in range(2):
                            if v:
                                pe.wait_ge(act_steps.sem, act_steps.count(f"h{v - 1}{t}", i))
                            hidden_products(pe, v, t, psum[:, 4 + t, 0:4 * NC2], blocks).then_inc(pe_steps.sem, pe_steps.step(f"h{v}{t}"))
                        pe.wait_ge(act_steps.sem, act_steps.count(f"h{v}1", i))
                        pe.wait_ge(dve_steps.sem, dve_steps.all_before(i))
                        for g in range(4):
                            for t in range(2):
                                if v == 0:
                                    h0 = 64 * (g % 2)
                                    last = pe.matmul(psum[h0:h0 + DH, 6, (g // 2) * NC2:(g // 2 + 1) * NC2], w2[:, t, :],
                                                     hid[:, t, g * NC2:(g + 1) * NC2], start=(t == 0), stop=(t == 1))
                        if v == 1:
                            for b in range(2):
                                for g in range(4):
                                    for t in range(2):
                                        c0 = g * NC2 + b * NCMP
                                        last = pe.matmul(psum[0:NCMP, 7, b * KV_DIM + g * DH:b * KV_DIM + (g + 1) * DH], hid[:, t, c0:c0 + NCMP],
                                                         w2[:, 2 + t, :], start=(t == 0), stop=(t == 1))
                        last.then_inc(pe_steps.sem, pe_steps.step(f"o{v}"))

            def copy_batches(eng, kind, v, i):
                own, pe_steps = C[kind], C["pe"]
                for m in range(8):
                    if m % 2 == (kind == "act"):
                        eng.wait_ge(pe_steps.sem, pe_steps.count(f"t{v}{m}", i))
                        if v:
                            eng.wait_ge(pe_steps.sem, pe_steps.count("h01", i))
                        for s2 in range(2):
                            for g2 in range(2):
                                src = psum[64 * g2:64 * g2 + DH, m % 4, 256 * s2:256 * (s2 + 1)].rearrange("p (a b) -> p a b", a=2)
                                dst = turned[64 * s2:64 * s2 + DH, m, :].rearrange("p (a g b) -> p a g b", a=2, g=2)[:, :, g2, :]
                                last = (eng.tensor_copy if kind == "dve" else eng.copy)(dst, src)
                        last.then_inc(own.sem, own.step(f"t{v}{m}"))

            def dve_cmp(dve):
                dve_steps, pe_steps = C["dve"], C["pe"]
                dve.sem_inc(dve_steps.sem, 1)
                dve.wait_ge(bias_pe, 1)
                dve.tensor_copy(pe_bias, psum[:, 7, 0:4]).then_inc(bias_dve, 1)
                with dve.Fori(0, NB // 2) as i:
                    for v in range(2):
                        copy_batches(dve, "dve", v, i)
                    dve.wait_ge(pe_steps.sem, pe_steps.count("o0", i))
                    dve.tensor_copy(ckT[:, :, bass.ds(NC2 * i, NC2)], psum[:, 6, 0:2 * NC2].rearrange("p (a b) -> p a b", a=2)).then_inc(dve_steps.sem, dve_steps.step("k"))
                    dve.wait_ge(pe_steps.sem, pe_steps.count("o1", i))
                    dve.tensor_copy(cv[:, bass.ds(2 * i, 2), :], psum[0:NCMP, 7, :].rearrange("p (a b) -> p a b", a=2)).then_inc(dve_steps.sem, dve_steps.step("v"))

            def act_cmp(act):
                act_steps, pe_steps = C["act"], C["pe"]
                act.sem_inc(act_steps.sem, 1)
                act.wait_ge(bias_dve, 1)
                with act.Fori(0, NB // 2) as i:
                    for v in range(2):
                        copy_batches(act, "act", v, i)
                        for t in range(2):
                            act.wait_ge(pe_steps.sem, pe_steps.count(f"h{v}{t}", i))
                            if v:
                                act.wait_ge(pe_steps.sem, pe_steps.count("o0", i))
                            act.activation(hid[:, t, :], psum[:, 4 + t, 0:4 * NC2], ACT.Silu, bias=pe_bias[:, 2 * v + t:2 * v + t + 1]).then_inc(act_steps.sem, act_steps.step(f"h{v}{t}"))

            space.at = past_projection
            gates48 = space.take(T, parts=3 * HEADS)
            w_gate = space.take(KD, 3 * HEADS)
            gate_p = space.take(3, 3 * HEADS)
            gate_wide = space.take(NB, 3 * HEADS, parts=TS)
            gate_pick = space.take(NB, 3 * HEADS)
            gate_s = space.take(NB, 3)
            qT = space.take(8, T)
            kvT = space.take(12, T)
            rows_s = space.take(NKV * KV_DIM, parts=TS)
            after_rows_s = space.at
            rows_p = space.take(2, NKV * KV_DIM)
            work = space.at
            gate_done, wg_in = sem("gates_product"), sem("gate_columns_in")
            K_SEL, V_SEL, K_WIN, V_WIN = (slice(x * KV_DIM, (x + 1) * KV_DIM) for x in (2, 3, 4, 5))

            def stream_in(sp):
                w0 = UNITS["nsa_in"][0]
                w = ins["nsa_w_in"][0].rearrange("(k p) n -> p k n", p=P)
                for n in range(10):
                    sp.wait_ge(unit_done, w0 + n - RING + 1)
                    sl = slot(w0 + n)[:, 0:KD * 256]
                    if n < 4:
                        c0 = (n // 2) * 512 + (n % 2) * P
                        views = [(sl.rearrange("p (k r h d) -> p k r h d", k=KD, r=2, h=2)[:, :, r, h, :],
                                  w[:, :, c0 + 256 * h + DH * r:c0 + 256 * h + DH * (r + 1)]) for h in range(2) for r in range(2)]
                    else:
                        c0 = Q_DIM + (n - 4) * 256
                        views = [(sl.rearrange("p (k n) -> p k n", k=KD)[:, h:h + 4, :], w[:, h:h + 4, c0:c0 + 256]) for h in (0, 4)]
                    for dst, src in views:
                        sp.dma_start(dst, src).then_inc(w_in[(w0 + n) % RING], 16)

            def pe_in(pe):
                for n in range(10):
                    multiply_unit(pe, "nsa_in", n // 4, n % 4, pair_tile, hT, KD)
                pe.wait_ge(wg_in, 16)
                for k in range(KD):
                    last = pe.matmul(psum[0:3 * HEADS, 6, 0:T], w_gate[:, k, :], hT[:, k, :], start=(k == 0), stop=(k == KD - 1))
                last.then_inc(gate_done, 1)

            def act_in(act):
                for n in range(10):
                    for l in range(2):
                        act.wait_ge(tile_done[l], product_count("nsa_in", n // 4, n % 4, l))
                        src = bank("nsa_in", n % 4, l)[:, 0:T]
                        if n < 4:
                            ins_ = act.activation(qT[:, 2 * n + l, :], src, ACT.Copy, scale=float(DH) ** -0.5)
                        else:
                            ins_ = act.copy(kvT[:, 2 * (n - 4) + l, :], src)
                        ins_.then_inc(lane_free[l], 1)

            def pool_in(pool):
                pool.dma_start(w_gate, ins["nsa_w_in"][0].rearrange("(k p) n -> p k n", p=P)[:, :, Q_DIM + NKV * KV_DIM:]).then_inc(wg_in, 16)

            space.at = work
            w1_again = space.take(2, 16, CHID)
            sub = space.take(2, 8, 4 * PSUB)
            hid_p = space.take(2, 2 * 4 * PCMP, off=xpg_at)
            groups = [(tb, rows, q) for tb, rows in ((0, P), (1, P), (2, TS)) for q in range(3)]
            R = dict(pe=steps("rows_pe", [f"g{n}" for n in range(9)] + ["gt", "gw", "hk", "hv", "ok", "ov"]),
                     dve=steps("rows_dve", ["g0", "g2", "g4", "g6", "g8", "den", "gate", "gtok", "gwide", "gpick", "gsum"]
                               + [f"sub{n}" for n in range(8)] + ["k", "v"]),
                     act=steps("rows_act", ["g1", "g3", "g5", "g7", "gexp"] + [f"sub{n}" for n in range(8)] + ["hk", "hv"]))
            same_q = table("same_q")

            def rows_dst(tb, rows, q):
                return (rows_p[:, tb, 512 * q:512 * (q + 1)] if tb < 2 else rows_s[:, 512 * q:512 * (q + 1)])

            def pe_rows(pe):
                pe_steps, dve_steps, act_steps = R["pe"], R["dve"], R["act"]
                for n, (tb, rows, q) in enumerate(groups):
                    if n >= 4:
                        pe.wait_ge((dve_steps if n % 2 == 0 else act_steps).sem, (dve_steps if n % 2 == 0 else act_steps).count(f"g{n - 4}"))
                    for j in range(4):
                        last = pe.transpose(psum[0:rows, n % 4, j * P:(j + 1) * P], kvT[:, 4 * q + j, tb * P:tb * P + rows], ident)
                    last.then_inc(pe_steps.sem, pe_steps.step(f"g{n}"))
                pe.wait_ge(dve_steps.sem, dve_steps.count("gate"))
                for tb, rows in ((0, P), (1, P), (2, TS)):
                    last = pe.transpose(psum[0:rows, 4, tb * 48:(tb + 1) * 48], gates48[:, tb * P:tb * P + rows], ident[0:48, 0:48])
                last.then_inc(pe_steps.sem, pe_steps.step("gt"))
                pe.wait_ge(dve_steps.sem, dve_steps.count("gwide"))
                pe.matmul(psum[:, 5, 0:NB * 48], same_q[0:TS, :], gate_wide.rearrange("p b c -> p (b c)"), start=True, stop=True).then_inc(pe_steps.sem, pe_steps.step("gw"))
                pe.wait_ge(w1_in, 64)
                pe.wait_ge(dve_steps.sem, dve_steps.count("sub7"))
                pe.wait_ge(act_steps.sem, act_steps.count("sub7"))
                for kv, name in enumerate(("hk", "hv")):
                    for t in range(2):
                        blocks = lambda m, half: sub[:, kv, m, :].rearrange("p (x n) -> p x n", x=4)[:, :, half:half + PCMP]
                        last = hidden_products_again(pe, kv, t, psum[:, 6 + kv, t * 60:(t + 1) * 60], blocks)
                    last.then_inc(pe_steps.sem, pe_steps.step(name))
                pe.wait_ge(act_steps.sem, act_steps.count("hk"))
                for g in range(4):
                    for t in range(2):
                        h0 = 64 * (g % 2)
                        last = pe.matmul(psum[h0:h0 + DH, 0, (g // 2) * PCMP:(g // 2 + 1) * PCMP], w2[:, t, :],
                                         hid_p[:, 0, t * 60 + g * PCMP:t * 60 + (g + 1) * PCMP], start=(t == 0), stop=(t == 1))
                last.then_inc(pe_steps.sem, pe_steps.step("ok"))
                pe.wait_ge(act_steps.sem, act_steps.count("hv"))
                for g in range(4):
                    for t in range(2):
                        last = pe.matmul(psum[0:PCMP, 1, g * DH:(g + 1) * DH], hid_p[:, 1, t * 60 + g * PCMP:t * 60 + (g + 1) * PCMP],
                                         w2[:, 2 + t, :], start=(t == 0), stop=(t == 1))
                last.then_inc(pe_steps.sem, pe_steps.step("ov"))

            def hidden_products_again(pe, v, t, out, rhs):
                for half in range(2):
                    for m in range(8):
                        last = pe.matmul(out, w1_again[:, v, 8 * half + m, t * P:(t + 1) * P], rhs(m, half),
                                         start=(half == 0 and m == 0), stop=(half == 1 and m == 7))
                return last

            def sub_copies(eng, kind):
                n = 0
                for kv in range(2):
                    for g in range(4):
                        for s2 in range(2):
                            if s2 == (kind == "act"):
                                src = kvT[64 * (g % 2):64 * (g % 2) + DH, 2 * kv + g // 2, 0:TP].rearrange("p (n m s) -> p m n s", m=8, s=2)[:, :, :, s2]
                                dst = sub[64 * s2:64 * s2 + DH, kv, :, g * PSUB:(g + 1) * PSUB]
                                (eng.tensor_copy if kind == "dve" else eng.copy)(dst, src).then_inc(R[kind].sem, R[kind].step(f"sub{n}"))
                                n += 1

            def act_rows(act):
                act_steps, pe_steps = R["act"], R["pe"]
                for n, (tb, rows, q) in enumerate(groups):
                    if n % 2:
                        act.wait_ge(pe_steps.sem, pe_steps.count(f"g{n}"))
                        act.copy(rows_dst(tb, rows, q), psum[0:rows, n % 4, :]).then_inc(act_steps.sem, act_steps.step(f"g{n}"))
                act.wait_ge(gate_done, 1)
                act.activation(gates48, psum[0:48, 6, 0:T], ACT.Exp, scale=-1.0).then_inc(act_steps.sem, act_steps.step("gexp"))
                sub_copies(act, "act")
                for kv, name in enumerate(("hk", "hv")):
                    act.wait_ge(pe_steps.sem, pe_steps.count(name))
                    for t in range(2):
                        last = act.activation(hid_p[:, kv, t * 60:(t + 1) * 60], psum[:, 6 + kv, t * 60:(t + 1) * 60], ACT.Silu,
                                              bias=pe_bias[:, 2 * kv + t:2 * kv + t + 1])
                    last.then_inc(act_steps.sem, act_steps.step(name))

            def dve_rows(dve):
                dve_steps, pe_steps, act_steps = R["dve"], R["pe"], R["act"]
                for n, (tb, rows, q) in enumerate(groups):
                    if n % 2 == 0:
                        dve.wait_ge(pe_steps.sem, pe_steps.count(f"g{n}"))
                        dve.tensor_copy(rows_dst(tb, rows, q), psum[0:rows, n % 4, :]).then_inc(dve_steps.sem, dve_steps.step(f"g{n}"))
                dve.wait_ge(act_steps.sem, act_steps.count("gexp"))
                dve.tensor_scalar(gates48, gates48, 1.0, None, ALU.add).then_inc(dve_steps.sem, dve_steps.step("den"))
                dve.wait_ge(dve_steps.sem, dve_steps.count("den"))
                dve.reciprocal(gates48, gates48).then_inc(dve_steps.sem, dve_steps.step("gate"))
                dve.wait_ge(pe_steps.sem, pe_steps.count("gt"))
                gt = psum[:, 4, 0:3 * 48].rearrange("p (a b) -> p a b", a=3)
                dve.tensor_copy(gate_p[:, 0:2, :], gt[:, 0:2, :])
                dve.tensor_copy(gate_p[0:TS, 2, :], gt[0:TS, 2, :]).then_inc(dve_steps.sem, dve_steps.step("gtok"))
                dve.wait_ge(dve_steps.sem, dve_steps.count("gtok"))
                dve.tensor_tensor(gate_wide, gate_p[0:TS, 2, :].unsqueeze(1).to_broadcast([TS, NB, 48]),
                                         const("tok_seq", TS).unsqueeze(2).to_broadcast([TS, NB, 48]), ALU.mult).then_inc(dve_steps.sem, dve_steps.step("gwide"))
                dve.wait_ge(pe_steps.sem, pe_steps.count("gw"))
                dve.tensor_tensor(gate_pick, psum[:, 5, 0:NB * 48].rearrange("p (b c) -> p b c", b=NB),
                                         table("own_head").unsqueeze(1).to_broadcast([P, NB, 48]), ALU.mult).then_inc(dve_steps.sem, dve_steps.step("gpick"))
                dve.wait_ge(dve_steps.sem, dve_steps.count("gpick"))
                dve.tensor_reduce(gate_s, gate_pick.rearrange("p b (h c) -> p b c h", c=3), AX.X, ALU.add).then_inc(dve_steps.sem, dve_steps.step("gsum"))
                sub_copies(dve, "dve")
                dve.wait_ge(pe_steps.sem, pe_steps.count("ok"))
                dve.tensor_copy(ckT_p, psum[:, 0, 0:2 * PCMP].rearrange("p (a b) -> p a b", a=2)).then_inc(dve_steps.sem, dve_steps.step("k"))
                dve.wait_ge(pe_steps.sem, pe_steps.count("ov"))
                dve.tensor_copy(cv_p, psum[0:PCMP, 1, 0:KV_DIM]).then_inc(dve_steps.sem, dve_steps.step("v"))

            def pool_rows(pool):
                for v in range(2):
                    pool.dma_start(w1_again[:, v], ins["nsa_cmp_w1"][0, v].rearrange("s d h -> (s d) h").rearrange("(c p) h -> p c h", p=P)).then_inc(w1_in, 16)
                pool.wait_ge(R["dve"].sem, R["dve"].count("g8"))
                pool.wait_ge(R["act"].sem, R["act"].count("g7"))
                kvp = outs["kv_rows_prompt"].rearrange("l b (t p) c g d -> p (l b t) (c g d)", p=P)
                wp = outs["win_prompt"].rearrange("l b (t p) c g d -> p (l b t) (c g d)", p=P)
                pool.dma_start(kvp, rows_p[:, :, 0:4 * KV_DIM]).then_inc(stored, 16)
                pool.dma_start(wp, rows_p[:, :, 4 * KV_DIM:]).then_inc(stored, 16)
                pool.dma_start(outs["kv_rows_sample"].rearrange("l b q c g d -> (l b q) (c g d)"), rows_s[:, 0:4 * KV_DIM]).then_inc(stored, 16)
                for b in range(NB):
                    pool.dma_start(outs["win_sample"][0, b].rearrange("w c g d -> w (c g d)")[WIN - TQ:, :],
                                   rows_s[b * TQ:(b + 1) * TQ, 4 * KV_DIM:]).then_inc(stored, 16)
                n_stored[0] += 11

            space.at = work
            o_tok = space.take(2, Q_DIM)
            qs = space.take(TP)
            hs = [dict(s0=space.take(2, P), s1=space.take(2, TP), sc=space.take(2, PCMP), mx=space.take(2, 3), sm=space.take(2, 3),
                       c=space.take(2, 3), p0=space.take(2 * P), pc=space.take(2 * P, parts=PCMP), p1=space.take(4 * P)) for _ in range(2)]
            B2 = lambda names: [f"{x}{h}" for x in names for h in range(2)]
            A = dict(pe=steps("prompt_pe", B2(["s"]) + B2(["t"]) + B2(["o"]), loop=True),
                     dve=steps("prompt_dve", B2(["s0", "sc", "s1", "m0", "mc", "m1", "pc", "inv", "c", "p0", "o0", "o1", "o2"])),
                     act=steps("prompt_act", ["q"] + B2(["e", "p1"])))
            AO = dict(pe=steps("prompt_out_pe", [f"g{n}" for n in range(4)]),
                      dve=steps("prompt_out_dve", ["g0", "g2"]), act=steps("prompt_out_act", ["g1", "g3"]))

            def pe_prompt(pe):
                pe_steps, dve_steps, act_steps = A["pe"], A["dve"], A["act"]
                pe.sem_inc(pe_steps.sem, 1)
                for gp in range(2):
                    with pe.Fori(4 * gp, 4 * gp + 4) as i:
                        pe.wait_ge(act_steps.sem, act_steps.count("q", i))
                        for h in range(2):
                            lo = slice(64 * h, 64 * h + DH)
                            b0, b1 = psum[:, 3 * h, :], psum[:, 3 * h + 1, :]
                            q0, q1 = qs[lo, 0:P], qs[lo, P:TP]
                            ks, kw, kc = kvT[lo, 4 + gp, :], kvT[lo, 8 + gp, :], ckT_p[lo, gp, :]
                            pe.matmul(b0[:, 0:P], q0, ks[:, 0:P], start=True, stop=True)
                            pe.matmul(b0[:, P:2 * P], q0, kw[:, 0:P], start=True, stop=True)
                            pe.matmul(b0[:, 256:256 + PCMP], q0, kc, start=True, stop=True)
                            pe.matmul(b0[:, 272:272 + PCMP], q1, kc, start=True, stop=True)
                            pe.matmul(b1[:, 0:TP], q1, ks[:, 0:TP], start=True, stop=True)
                            pe.matmul(b1[:, TP:2 * TP], q1, kw[:, 0:TP], start=True, stop=True).then_inc(pe_steps.sem, pe_steps.step(f"s{h}"))
                        for h in range(2):
                            d = hs[h]
                            b0, b1 = psum[:, 3 * h, :], psum[:, 3 * h + 1, :]
                            pe.wait_ge(act_steps.sem, act_steps.count(f"e{h}", i))
                            pe.wait_ge(dve_steps.sem, dve_steps.count(f"pc{h}", i))
                            for x in range(2):
                                pe.transpose(b0[:, x * P:(x + 1) * P], d["s0"][:, x, :], ident)
                                pe.transpose(b0[0:PCMP, (2 + x) * P:(3 + x) * P], d["sc"][:, x, :], ident)
                                for y in range(2):
                                    last = pe.transpose(b1[:, (2 * x + y) * P:(2 * x + y + 1) * P], d["s1"][:, x, y * P:(y + 1) * P], ident)
                            last.then_inc(pe_steps.sem, pe_steps.step(f"t{h}"))
                        for h in range(2):
                            d, g = hs[h], 2 * gp + h
                            pe.wait_ge(dve_steps.sem, dve_steps.count(f"p0{h}", i))
                            pe.wait_ge(act_steps.sem, act_steps.count(f"p1{h}", i))
                            o = psum[:, 3 * h + 2, 0:384].rearrange("p (t b d) -> p t b d", t=2, b=3)
                            cols = lambda x: slice(x.start + g * DH, x.start + (g + 1) * DH)
                            for t in range(2):
                                pe.matmul(o[:, t, 0, :], d["pc"][:, t * P:(t + 1) * P], cv_p[:, g * DH:(g + 1) * DH], start=True, stop=True)
                            for x, vc in ((0, V_SEL), (1, V_WIN)):
                                pe.matmul(o[:, 0, 1 + x, :], d["p0"][:, x * P:(x + 1) * P], rows_p[:, 0, cols(vc)], start=True, stop=True)
                                for y in range(2):
                                    last = pe.matmul(o[:, 1, 1 + x, :], d["p1"][:, (2 * x + y) * P:(2 * x + y + 1) * P], rows_p[:, y, cols(vc)],
                                                     start=(y == 0), stop=(y == 1))
                            last.then_inc(pe_steps.sem, pe_steps.step(f"o{h}"))

            def act_prompt(act):
                act_steps, dve_steps, pe_steps = A["act"], A["dve"], A["pe"]
                for gp in range(2):
                    with act.Fori(4 * gp, 4 * gp + 4) as i:
                        act.wait_ge(pe_steps.sem, pe_steps.all_before(i))
                        act.copy(qs, one(qT[:, bass.ds(i, 1), 0:TP])).then_inc(act_steps.sem, act_steps.step("q"))
                        for h in range(2):
                            d = hs[h]
                            act.wait_ge(dve_steps.sem, dve_steps.count(f"m1{h}", i))
                            for x in range(2):
                                act.activation(d["s0"][:, x, :], d["s0"][:, x, :], ACT.Exp, bias=d["mx"][:, 0, 1 + x:2 + x], accum_out=d["sm"][:, 0, 1 + x:2 + x])
                                act.activation(d["sc"][:, x, :], d["sc"][:, x, :], ACT.Exp, bias=d["mx"][:, x, 0:1], accum_out=d["sm"][:, x, 0:1])
                                last = act.activation(d["s1"][:, x, :], d["s1"][:, x, :], ACT.Exp, bias=d["mx"][:, 1, 1 + x:2 + x], accum_out=d["sm"][:, 1, 1 + x:2 + x])
                            last.then_inc(act_steps.sem, act_steps.step(f"e{h}"))
                        for h in range(2):
                            act.wait_ge(pe_steps.sem, pe_steps.count(f"t{h}", i))
                            act.copy(hs[h]["p1"], psum[:, 3 * h + 1, :]).then_inc(act_steps.sem, act_steps.step(f"p1{h}"))

            def dve_prompt(dve):
                dve_steps, pe_steps, act_steps = A["dve"], A["pe"], A["act"]
                dve.wait_ge(att_in, 32)
                for gp in range(2):
                    with dve.Fori(4 * gp, 4 * gp + 4) as i:
                        for h in range(2):
                            d = hs[h]
                            slope = table("slopes")[:, bass.ds(i + 4 * gp + 4 * h, 1)]
                            b0 = psum[:, 3 * h, :]
                            dve.wait_ge(pe_steps.sem, pe_steps.count(f"s{h}", i))
                            dve.scalar_tensor_tensor(out=d["s0"], in0=table("dist0").unsqueeze(1).to_broadcast([P, 2, P]), scalar=slope,
                                                            in1=b0[:, 0:256].rearrange("p (a b) -> p a b", a=2), op0=ALU.mult, op1=ALU.add).then_inc(dve_steps.sem, dve_steps.step(f"s0{h}"))
                        for h in range(2):
                            d = hs[h]
                            slope = table("slopes")[:, bass.ds(i + 4 * gp + 4 * h, 1)]
                            dve.scalar_tensor_tensor(out=d["sc"], in0=table("cdist", 2), scalar=slope,
                                                            in1=psum[:, 3 * h, 256:288].rearrange("p (a b) -> p a b", a=2)[:, :, 0:PCMP], op0=ALU.mult, op1=ALU.add).then_inc(dve_steps.sem, dve_steps.step(f"sc{h}"))
                        for h in range(2):
                            d = hs[h]
                            slope = table("slopes")[:, bass.ds(i + 4 * gp + 4 * h, 1)]
                            dve.scalar_tensor_tensor(out=d["s1"], in0=table("dist1").unsqueeze(1).to_broadcast([P, 2, TP]), scalar=slope,
                                                            in1=psum[:, 3 * h + 1, :].rearrange("p (a b) -> p a b", a=2), op0=ALU.mult, op1=ALU.add).then_inc(dve_steps.sem, dve_steps.step(f"s1{h}"))
                        for h in range(2):
                            dve.wait_ge(dve_steps.sem, dve_steps.count(f"s0{h}", i))
                            dve.tensor_reduce(hs[h]["mx"][:, 0, 1:3], hs[h]["s0"], AX.X, ALU.max, negate=True).then_inc(dve_steps.sem, dve_steps.step(f"m0{h}"))
                        for h in range(2):
                            dve.wait_ge(dve_steps.sem, dve_steps.count(f"sc{h}", i))
                            dve.tensor_reduce(hs[h]["mx"][:, :, 0], hs[h]["sc"], AX.X, ALU.max, negate=True).then_inc(dve_steps.sem, dve_steps.step(f"mc{h}"))
                        for h in range(2):
                            dve.wait_ge(dve_steps.sem, dve_steps.count(f"s1{h}", i))
                            dve.tensor_reduce(hs[h]["mx"][:, 1, 1:3], hs[h]["s1"], AX.X, ALU.max, negate=True).then_inc(dve_steps.sem, dve_steps.step(f"m1{h}"))
                        for h in range(2):
                            dve.wait_ge(act_steps.sem, act_steps.count(f"e{h}", i))
                            dve.tensor_tensor(hs[h]["sc"], hs[h]["sc"], table("cvalid", 2), ALU.mult).then_inc(dve_steps.sem, dve_steps.step(f"pc{h}"))
                        for h in range(2):
                            dve.reciprocal(hs[h]["sm"], hs[h]["sm"]).then_inc(dve_steps.sem, dve_steps.step(f"inv{h}"))
                        for h in range(2):
                            dve.wait_ge(dve_steps.sem, dve_steps.count(f"inv{h}", i))
                            dve.tensor_tensor(hs[h]["c"], hs[h]["sm"], gate_p[:, 0:2, bass.ds(3 * i + 12 * gp + 12 * h, 3)], ALU.mult).then_inc(dve_steps.sem, dve_steps.step(f"c{h}"))
                        for h in range(2):
                            dve.wait_ge(pe_steps.sem, pe_steps.count(f"t{h}", i))
                            dve.tensor_copy(hs[h]["p0"], psum[:, 3 * h, 0:256])
                            dve.tensor_copy(hs[h]["pc"], psum[0:PCMP, 3 * h, 256:512]).then_inc(dve_steps.sem, dve_steps.step(f"p0{h}"))
                        for br in range(3):
                            for h in range(2):
                                if br == 0:
                                    dve.wait_ge(pe_steps.sem, pe_steps.count(f"o{h}", i))
                                    dve.wait_ge(dve_steps.sem, dve_steps.count(f"c{h}", i))
                                else:
                                    dve.wait_ge(dve_steps.sem, dve_steps.count(f"o{br - 1}{h}", i))
                                for t in range(2):
                                    src = psum[:, 3 * h + 2, 0:384].rearrange("p (t b d) -> p t b d", t=2, b=3)[:, t, br, :]
                                    dst = o_tok[:, t, bass.ds(DH * i + 256 * gp + 256 * h, DH)]
                                    c = hs[h]["c"][:, t, br:br + 1]
                                    if br == 0:
                                        last = dve.tensor_scalar(dst, src, c, None, ALU.mult)
                                    else:
                                        last = dve.scalar_tensor_tensor(out=dst, in0=src, scalar=c, in1=dst, op0=ALU.mult, op1=ALU.add)
                                last.then_inc(dve_steps.sem, dve_steps.step(f"o{br}{h}"))

            out_blocks = [(tb, half) for tb in range(2) for half in range(2)]

            def pe_prompt_out(pe):
                for n, (tb, half) in enumerate(out_blocks):
                    for j in range(4):
                        c0 = (4 * half + j) * P
                        last = pe.transpose(psum[:, n, j * P:(j + 1) * P], o_tok[:, tb, c0:c0 + P], ident)
                    last.then_inc(AO["pe"].sem, AO["pe"].step(f"g{n}"))

            def prompt_out(eng, kind):
                for n, (tb, half) in enumerate(out_blocks):
                    if n % 2 == (kind == "act"):
                        eng.wait_ge(AO["pe"].sem, AO["pe"].count(f"g{n}"))
                        (eng.tensor_copy if kind == "dve" else eng.copy)(
                            hT[:, 4 * half:4 * half + 4, tb * P:(tb + 1) * P], psum[:, n, :].rearrange("p (a b) -> p a b", a=4)).then_inc(AO[kind].sem, AO[kind].step(f"g{n}"))

            space.at = after_rows_s
            k_sel = space.take(NPG, KV_DIM)
            v_sel = space.take(NPG, KV_DIM)
            k_win = space.take(WIN // P, KV_DIM)
            v_win = space.take(WIN // P, KV_DIM)
            kT = space.take(2, PAST)
            kTw = space.take(2, WIN, off=xpg_at)
            q2 = space.take(2, P)
            ss = space.take(PAST + TS)
            sw = space.take(WIN + TS)
            sc_wide = space.take(P)
            sc = sc_wide[:, 0:NCMP]
            mx, sm, cc = space.take(3), space.take(3), space.take(3)
            imp_r, imp, rank, pen = (space.take(FREE_BLKS) for _ in range(4))
            pcT = space.take(P, parts=NCMP)
            cmpg = space.take(FREE_BLKS, FREE_BLKS, off=space.at)
            cmpe = space.take(FREE_BLKS, FREE_BLKS, off=space.at + FREE_BLKS ** 2)
            pT = space.take(12, P)
            pTn = space.take(2 * P, parts=TS)
            o_wide = space.take(P)
            o_s = o_wide[:, 0:DH]
            assert space.at <= size
            F = dict(
                pe=steps("sample_pe", [f"t{n}" for n in range(6)] + ["cmp", "sel", "win", "pc", "ir", "is", "ptw", "pts", "ptn", "o", "ot"], loop=True),
                dve=steps("sample_dve", ["t0", "t2", "t4", "scmp", "mcmp", "icmp", "pcmp", "pc", "swin", "swn", "mwin", "ssel", "ssn",
                                         "ir", "is", "gt", "eq", "eqe", "gte", "rank", "pen", "spen", "msel", "pts1", "ptn", "inv", "c",
                                         "o0", "o1", "o2", "oT0", "oT1"], loop=True),
                act=steps("sample_act", ["q", "t1", "t3", "t5", "ecmp", "ewin", "ptw", "esel", "pts0"]))
            k_in, v_in, k_out, zeroed = sem("sample_k_in"), sem("sample_v_in"), sem("window_stored"), sem("q2_zeroed")
            kv_rows = ins["cache_nsa_kv"].rearrange("l g s c j d -> (l g) s (c j d)")
            win_rows = ins["cache_nsa_win"].rearrange("l b (t p) c j d -> (l b) p t (c j d)", p=P)
            win_out = outs["win_sample"].rearrange("l b w c j d -> (l b) w (c j d)")

            def store_window(eng, i, c0, src):
                dst = win_out[bass.ds(i, 1)].rearrange("o w c -> (o w) c")[:, c0:c0 + KV_DIM]
                eng.dma_start(dst[0:P - TQ, :], src[TQ:P, 0, :]).then_inc(k_out, 16)
                eng.dma_start(dst[P - TQ:WIN - TQ, :].rearrange("(t p) c -> p t c", p=P), src[:, 1:, :]).then_inc(k_out, 16)

            def pool_sample(pool):
                with pool.Fori(0, NB) as i:
                    pool.wait_ge(F["pe"].sem, F["pe"].all_before(i))
                    pool.wait_ge(k_out, 64 * i + 16)
                    pages = [pool.value_load(pages_sb[0:1, bass.ds(NPG * i + g, 1)], min_val=0, max_val=NPOOL - 1) for g in range(NPG)]
                    for g in range(NPG):
                        src = kv_rows[bass.ds(pages[g], 1)].rearrange("o s c -> (o s) c")
                        pool.dma_start(k_sel[:, g, :], src[:, K_SEL]).then_inc(k_in, 16)
                    w = win_rows[bass.ds(i, 1)].rearrange("o p t c -> (o p) t c")
                    pool.dma_start(k_win, w[:, :, 0:KV_DIM]).then_inc(k_in, 16)
                    for g in range(NPG):
                        src = kv_rows[bass.ds(pages[g], 1)].rearrange("o s c -> (o s) c")
                        pool.dma_start(v_sel[:, g, :], src[:, V_SEL]).then_inc(v_in, 16)
                    pool.dma_start(v_win, w[:, :, KV_DIM:]).then_inc(v_in, 16)
                pool.wait_ge(k_out, 64 * NB + 16)

            def pe_sample(pe):
                pe_steps, dve_steps, act_steps = F["pe"], F["dve"], F["act"]
                pe.sem_inc(pe_steps.sem, 1)
                pe.wait_ge(zeroed, 3)
                with pe.Fori(0, NB) as i:
                    pe.wait_ge(dve_steps.sem, dve_steps.all_before(i))
                    pe.wait_ge(k_in, 144 * (i + 1))
                    for n in range(6):
                        gp = n % 2
                        for j in range(4):
                            src = k_sel[:, 4 * (n // 2) + j, :] if n < 4 else k_win[:, j, :]
                            last = pe.transpose(psum[:, n, j * P:(j + 1) * P], src[:, gp * P:(gp + 1) * P], ident)
                        last.then_inc(pe_steps.sem, pe_steps.step(f"t{n}"))
                    pe.wait_ge(act_steps.sem, act_steps.count("q", i))
                    for c0, k in ((0, lambda gp: ckT[:, gp, bass.ds(NCMP * i, NCMP)]), (64, lambda gp: kvT[:, 4 + gp, TP:T]),
                                  (128, lambda gp: kvT[:, 8 + gp, TP:T])):
                        for gp in range(2):
                            last = pe.matmul(psum[:, 7, c0:c0 + (TS if c0 else NCMP)], q2[:, gp, :], k(gp), start=(gp == 0), stop=(gp == 1))
                    last.then_inc(pe_steps.sem, pe_steps.step("cmp"))
                    pe.wait_ge(dve_steps.sem, dve_steps.count("t4", i))
                    pe.wait_ge(act_steps.sem, act_steps.count("t5", i))
                    for x in range(2):
                        for gp in range(2):
                            last = pe.matmul(psum[:, x, :], q2[:, gp, :], kT[:, gp, x * 512:(x + 1) * 512], start=(gp == 0), stop=(gp == 1))
                    last.then_inc(pe_steps.sem, pe_steps.step("sel"))
                    for gp in range(2):
                        last = pe.matmul(psum[:, 2, :], q2[:, gp, :], kTw[:, gp, :], start=(gp == 0), stop=(gp == 1))
                    last.then_inc(pe_steps.sem, pe_steps.step("win"))
                    pe.wait_ge(dve_steps.sem, dve_steps.count("pcmp", i))
                    pe.transpose(psum[:, 3, 0:P], sc_wide, ident).then_inc(pe_steps.sem, pe_steps.step("pc"))
                    pe.wait_ge(dve_steps.sem, dve_steps.count("pc", i))
                    pe.matmul(psum[:, 4, 0:FREE_BLKS], pcT, table("overlap")[0:NCMP, :], start=True, stop=True).then_inc(pe_steps.sem, pe_steps.step("ir"))
                    pe.wait_ge(dve_steps.sem, dve_steps.count("ir", i))
                    pe.matmul(psum[:, 5, 0:FREE_BLKS], table("group_sum"), imp_r, start=True, stop=True).then_inc(pe_steps.sem, pe_steps.step("is"))
                    pe.wait_ge(act_steps.sem, act_steps.count("ewin", i))
                    for j in range(4):
                        last = pe.transpose(psum[:, 2, j * P:(j + 1) * P], sw[:, j * P:(j + 1) * P], ident)
                    last.then_inc(pe_steps.sem, pe_steps.step("ptw"))
                    pe.wait_ge(act_steps.sem, act_steps.count("esel", i))
                    for j in range(8):
                        last = pe.transpose(psum[:, j // 4, (j % 4) * P:(j % 4 + 1) * P], ss[:, j * P:(j + 1) * P], ident)
                    last.then_inc(pe_steps.sem, pe_steps.step("pts"))
                    pe.transpose(psum[0:TS, 3, 0:P], ss[:, PAST:], ident)
                    pe.transpose(psum[0:TS, 3, P:2 * P], sw[:, WIN:], ident).then_inc(pe_steps.sem, pe_steps.step("ptn"))
                    pe.wait_ge(v_in, 144 * (i + 1))
                    pe.matmul(psum[:, 5, 0:KV_DIM], pcT, cv[:, bass.ds(i, 1), :].rearrange("p o c -> p (o c)"), start=True, stop=True)
                    pe.wait_ge(act_steps.sem, act_steps.count("ptw", i))
                    pe.wait_ge(dve_steps.sem, dve_steps.count("ptn", i))
                    for j in range(4):
                        pe.matmul(psum[:, 6, KV_DIM:], pT[:, 8 + j, :], v_win[:, j, :], start=(j == 0), stop=False)
                    pe.matmul(psum[:, 6, KV_DIM:], pTn[:, P:], rows_s[:, V_WIN], start=False, stop=True)
                    pe.wait_ge(act_steps.sem, act_steps.count("pts0", i))
                    for j in range(8):
                        pe.matmul(psum[:, 6, 0:KV_DIM], pT[:, j, :], v_sel[:, j, :], start=(j == 0), stop=False)
                    pe.matmul(psum[:, 6, 0:KV_DIM], pTn[:, 0:P], rows_s[:, V_SEL], start=False, stop=True).then_inc(pe_steps.sem, pe_steps.step("o"))
                    pe.wait_ge(dve_steps.sem, dve_steps.count("o2", i))
                    pe.transpose(psum[:, 7, 0:P], o_wide, ident).then_inc(pe_steps.sem, pe_steps.step("ot"))

            def act_sample(act):
                act_steps, dve_steps, pe_steps = F["act"], F["dve"], F["pe"]
                act.sem_inc(k_out, 16)
                act.wait_ge(zeroed, 3)
                with act.Fori(0, NB) as i:
                    act.wait_ge(pe_steps.sem, pe_steps.all_before(i))
                    for h in range(2):
                        lo = slice(64 * h, 64 * h + 64)
                        for gp in range(2):
                            last = act.copy(q2[lo, gp, 64 * gp + 32 * h:64 * gp + 32 * h + 32].rearrange("p (r q) -> p r q", r=4), qT[lo, 4 * gp:4 * gp + 4, bass.ds(TP + TQ * i, TQ)])
                    last.then_inc(act_steps.sem, act_steps.step("q"))
                    for n in (1, 3, 5):
                        act.wait_ge(pe_steps.sem, pe_steps.count(f"t{n}", i))
                        dst = kT[:, 1, 512 * (n // 2):512 * (n // 2 + 1)] if n < 4 else kTw[:, 1, :]
                        act.copy(dst, psum[:, n, :]).then_inc(act_steps.sem, act_steps.step(f"t{n}"))
                    act.wait_ge(dve_steps.sem, dve_steps.count("mcmp", i))
                    act.activation(sc, sc, ACT.Exp, bias=mx[:, 0:1], accum_out=sm[:, 0:1]).then_inc(act_steps.sem, act_steps.step("ecmp"))
                    act.wait_ge(dve_steps.sem, dve_steps.count("mwin", i))
                    act.activation(sw, sw, ACT.Exp, bias=mx[:, 2:3], accum_out=sm[:, 2:3]).then_inc(act_steps.sem, act_steps.step("ewin"))
                    act.wait_ge(pe_steps.sem, pe_steps.count("ptw", i))
                    act.copy(pT[:, 8:12, :], psum[:, 2, :].rearrange("p (a b) -> p a b", a=4)).then_inc(act_steps.sem, act_steps.step("ptw"))
                    act.wait_ge(dve_steps.sem, dve_steps.count("msel", i))
                    act.activation(ss, ss, ACT.Exp, bias=mx[:, 1:2], accum_out=sm[:, 1:2]).then_inc(act_steps.sem, act_steps.step("esel"))
                    act.wait_ge(pe_steps.sem, pe_steps.count("pts", i))
                    act.copy(pT[:, 0:4, :], psum[:, 0, :].rearrange("p (a b) -> p a b", a=4)).then_inc(act_steps.sem, act_steps.step("pts0"))
                    act.wait_ge(k_in, 144 * (i + 1))
                    act.wait_ge(v_in, 144 * (i + 1))
                    store_window(act, i, 0, k_win)
                    store_window(act, i, KV_DIM, v_win)

            def dve_sample(dve):
                dve_steps, pe_steps, act_steps = F["dve"], F["pe"], F["act"]
                dve.sem_inc(dve_steps.sem, 1)
                for t in (q2, sc_wide, o_wide):
                    dve.memset(t, 0.0).then_inc(zeroed, 1)
                dve.wait_ge(zeroed, 3)
                n14 = FREE_BLKS
                with dve.Fori(0, NB) as i:
                    for n in (0, 2, 4):
                        dve.wait_ge(pe_steps.sem, pe_steps.count(f"t{n}", i))
                        dst = kT[:, 0, 512 * (n // 2):512 * (n // 2 + 1)] if n < 4 else kTw[:, 0, :]
                        dve.tensor_copy(dst, psum[:, n, :]).then_inc(dve_steps.sem, dve_steps.step(f"t{n}"))
                    dve.wait_ge(pe_steps.sem, pe_steps.count("cmp", i))
                    dve.tensor_tensor(sc, psum[:, 7, 0:NCMP], table("bias_cmp"), ALU.add).then_inc(dve_steps.sem, dve_steps.step("scmp"))
                    dve.wait_ge(dve_steps.sem, dve_steps.count("scmp", i))
                    dve.tensor_reduce(mx[:, 0:1], sc, AX.X, ALU.max, negate=True).then_inc(dve_steps.sem, dve_steps.step("mcmp"))
                    dve.wait_ge(act_steps.sem, act_steps.count("ecmp", i))
                    dve.reciprocal(sm[:, 0:1], sm[:, 0:1]).then_inc(dve_steps.sem, dve_steps.step("icmp"))
                    dve.wait_ge(dve_steps.sem, dve_steps.count("icmp", i))
                    dve.tensor_scalar(sc, sc, sm[:, 0:1], None, ALU.mult).then_inc(dve_steps.sem, dve_steps.step("pcmp"))
                    dve.wait_ge(pe_steps.sem, pe_steps.count("pc", i))
                    dve.tensor_copy(pcT, psum[0:NCMP, 3, 0:P]).then_inc(dve_steps.sem, dve_steps.step("pc"))
                    new = one(table("bias_new", NB)[:, bass.ds(i, 1), :])
                    dve.wait_ge(pe_steps.sem, pe_steps.count("win", i))
                    dve.tensor_tensor(sw[:, 0:WIN], psum[:, 2, :], table("bias_win"), ALU.add).then_inc(dve_steps.sem, dve_steps.step("swin"))
                    dve.tensor_tensor(sw[:, WIN:], psum[:, 7, 128:128 + TS], new, ALU.add).then_inc(dve_steps.sem, dve_steps.step("swn"))
                    dve.wait_ge(dve_steps.sem, dve_steps.count("swn", i))
                    dve.tensor_reduce(mx[:, 2:3], sw, AX.X, ALU.max, negate=True).then_inc(dve_steps.sem, dve_steps.step("mwin"))
                    dve.tensor_tensor(ss[:, 0:PAST].rearrange("p (a b) -> p a b", a=2), psum[:, 0:2, :], table("bias_sel", 2), ALU.add).then_inc(dve_steps.sem, dve_steps.step("ssel"))
                    dve.tensor_tensor(ss[:, PAST:], psum[:, 7, 64:64 + TS], new, ALU.add).then_inc(dve_steps.sem, dve_steps.step("ssn"))
                    dve.wait_ge(pe_steps.sem, pe_steps.count("ir", i))
                    dve.tensor_copy(imp_r, psum[:, 4, 0:n14]).then_inc(dve_steps.sem, dve_steps.step("ir"))
                    dve.wait_ge(pe_steps.sem, pe_steps.count("is", i))
                    dve.tensor_copy(imp, psum[:, 5, 0:n14]).then_inc(dve_steps.sem, dve_steps.step("is"))
                    dve.wait_ge(dve_steps.sem, dve_steps.count("is", i))
                    other = imp.unsqueeze(1).to_broadcast([P, n14, n14])
                    this = imp.unsqueeze(2).to_broadcast([P, n14, n14])
                    dve.tensor_tensor(cmpg, other, this, ALU.is_gt).then_inc(dve_steps.sem, dve_steps.step("gt"))
                    dve.tensor_tensor(cmpe, other, this, ALU.is_equal).then_inc(dve_steps.sem, dve_steps.step("eq"))
                    dve.wait_ge(dve_steps.sem, dve_steps.count("eq", i))
                    dve.tensor_tensor(cmpe, cmpe, table("earlier", n14), ALU.mult).then_inc(dve_steps.sem, dve_steps.step("eqe"))
                    dve.wait_ge(dve_steps.sem, dve_steps.count("eqe", i))
                    dve.tensor_tensor(cmpg, cmpg, cmpe, ALU.add).then_inc(dve_steps.sem, dve_steps.step("gte"))
                    dve.wait_ge(dve_steps.sem, dve_steps.count("gte", i))
                    dve.tensor_reduce(rank, cmpg, AX.X, ALU.add).then_inc(dve_steps.sem, dve_steps.step("rank"))
                    dve.wait_ge(dve_steps.sem, dve_steps.count("rank", i))
                    dve.tensor_scalar(pen, rank, FREE_TOP - 0.5, MASKED, ALU.is_ge, ALU.mult).then_inc(dve_steps.sem, dve_steps.step("pen"))
                    dve.wait_ge(dve_steps.sem, dve_steps.count("pen", i))
                    blocks = ss[:, SELB:SELB * (1 + n14)].rearrange("p (a b) -> p a b", a=n14)
                    dve.tensor_tensor(blocks, blocks, pen.unsqueeze(2).to_broadcast([P, n14, SELB]), ALU.add).then_inc(dve_steps.sem, dve_steps.step("spen"))
                    dve.wait_ge(dve_steps.sem, dve_steps.count("spen", i))
                    dve.tensor_reduce(mx[:, 1:2], ss, AX.X, ALU.max, negate=True).then_inc(dve_steps.sem, dve_steps.step("msel"))
                    dve.wait_ge(pe_steps.sem, pe_steps.count("pts", i))
                    dve.tensor_copy(pT[:, 4:8, :], psum[:, 1, :].rearrange("p (a b) -> p a b", a=4)).then_inc(dve_steps.sem, dve_steps.step("pts1"))
                    dve.wait_ge(pe_steps.sem, pe_steps.count("ptn", i))
                    dve.tensor_copy(pTn, psum[0:TS, 3, 0:2 * P]).then_inc(dve_steps.sem, dve_steps.step("ptn"))
                    dve.wait_ge(act_steps.sem, act_steps.count("esel", i))
                    dve.reciprocal(sm[:, 1:3], sm[:, 1:3]).then_inc(dve_steps.sem, dve_steps.step("inv"))
                    dve.wait_ge(dve_steps.sem, dve_steps.count("inv", i))
                    gate = one(gate_s[:, bass.ds(i, 1), :])
                    dve.tensor_copy(cc[:, 0:1], gate[:, 0:1])
                    dve.tensor_tensor(cc[:, 1:3], sm[:, 1:3], gate[:, 1:3], ALU.mult).then_inc(dve_steps.sem, dve_steps.step("c"))
                    dve.wait_ge(pe_steps.sem, pe_steps.count("o", i))
                    dve.wait_ge(dve_steps.sem, dve_steps.count("c", i))
                    for br, (b, c0) in enumerate(((5, 0), (6, 0), (6, KV_DIM))):
                        if br:
                            dve.wait_ge(dve_steps.sem, dve_steps.count(f"o{br - 1}", i))
                        for g in range(4):
                            r = slice(32 * g, 32 * g + 32)
                            src = psum[r, b, c0 + g * DH:c0 + (g + 1) * DH]
                            if br == 0:
                                last = dve.tensor_scalar(o_s[r, :], src, cc[r, 0:1], None, ALU.mult)
                            else:
                                last = dve.scalar_tensor_tensor(out=o_s[r, :], in0=src, scalar=cc[r, br:br + 1], in1=o_s[r, :], op0=ALU.mult, op1=ALU.add)
                        last.then_inc(dve_steps.sem, dve_steps.step(f"o{br}"))
                    dve.wait_ge(pe_steps.sem, pe_steps.count("ot", i))
                    ot = psum[0:DH, 7, 0:P].rearrange("p (t e q) -> p t e q", t=8, e=2)
                    for e in range(2):
                        dve.tensor_copy(hT[64 * e:64 * e + DH, :, bass.ds(TP + TQ * i, TQ)], ot[:, :, e, :]).then_inc(dve_steps.sem, dve_steps.step(f"oT{e}"))

            def pe_out(pe):
                for n in range(4):
                    multiply_unit(pe, "nsa_out", 0, n, pair_tile, hT, KD)

            def dve_out(dve):
                for xp in xpg:
                    dve.memset(xp[:, 0:GP], 0.0)
                for n in range(4):
                    for l in range(2):
                        dve.wait_ge(tile_done[l], product_count("nsa_out", 0, n, l))
                        x = xT[:, 2 * n + l, :]
                        dve.tensor_tensor(x, x, bank("nsa_out", n, l)[:, 0:T], ALU.add).then_inc(lane_free[l], 1)

            return dict(stream_in=stream_in,
                        pe=(pe_cmp, pe_in, pe_rows, pe_prompt, pe_prompt_out, pe_sample, pe_out),
                        act=(act_cmp, act_in, act_rows, act_prompt, lambda e: prompt_out(e, "act"), act_sample),
                        dve=(dve_cmp, dve_rows, dve_prompt, lambda e: prompt_out(e, "dve"), dve_sample, dve_out),
                        pool=(pool_cmp, pool_in, pool_rows, pool_sample))

        def final_stage():
            space.at = phase
            y = space.take(3, D)
            blocks = [(tb, rows, half) for tb, rows in ((0, P), (1, P), (2, TS)) for half in range(2)]
            s = dict(pe=steps("y_turned", [f"g{n}" for n in range(6)]),
                     dve=steps("y_copied_dve", ["g0", "g2", "g4"]), act=steps("y_copied_act", ["g1", "g3", "g5"]))

            def pe(eng):
                for n, (tb, rows, half) in enumerate(blocks):
                    for j in range(4):
                        last = eng.transpose(psum[0:rows, n, j * P:(j + 1) * P], hT[:, 4 * half + j, tb * P:tb * P + rows], ident)
                    last.then_inc(s["pe"].sem, s["pe"].step(f"g{n}"))

            def copy(eng, kind):
                for n, (tb, rows, half) in enumerate(blocks):
                    if n % 2 == (kind == "act"):
                        eng.wait_ge(s["pe"].sem, s["pe"].count(f"g{n}"))
                        dst = y[0:rows, tb, 512 * half:512 * half + 512]
                        (eng.tensor_copy if kind == "dve" else eng.copy)(dst, psum[0:rows, n, :]).then_inc(s[kind].sem, s[kind].step(f"g{n}"))

            def pool(eng):
                v = outs["y_prompt"].rearrange("b (t p) d -> p (b t) d", p=P)
                for tb in range(3):
                    eng.wait_ge(s["dve"].sem, s["dve"].count(f"g{2 * tb}"))
                    eng.wait_ge(s["act"].sem, s["act"].count(f"g{2 * tb + 1}"))
                    if tb < 2:
                        eng.dma_start(v[:, tb, :], y[:, tb, :]).then_inc(stored, 16)
                    else:
                        eng.dma_start(outs["y_sample"].rearrange("b q d -> (b q) d"), y[0:TS, 2, :]).then_inc(stored, 16)
                n_stored[0] += 3
                eng.wait_ge(stored, 16 * n_stored[0])
            return dict(pe=pe, copy=copy, pool=pool)

        norms = [norm_stage(f"norm{n}", w) for n, w in enumerate((0, 2, 1, 3, 4))]
        ffns = [ffn_up(l) for l in range(2)]
        nsa = nsa_stages()
        fin = final_stage()
        block = ctx.enter_context(nc.Block())

        @block.sync
        def _(sp):
            sp.dma_start(x_tok[:, 0:2, :], ins["x_prompt"].rearrange("b (t p) d -> p (b t) d", p=P)).then_inc(x_in, 16)
            sp.dma_start(x_tok[0:TS, 2, :], ins["x_sample"].rearrange("b q d -> (b q) d")).then_inc(x_in, 16)
            sp.dma_start(tables, ins["tables"][:, 0:base_cols]).then_inc(const_in, 16)
            flat = "l w c -> (l w) c"
            sp.dma_start(norm_rows[0:1, :], ins["gdn_norm"]).then_inc(rows_in, 16)
            sp.dma_start(norm_rows[1:2, :], ins["nsa_norm"]).then_inc(rows_in, 16)
            sp.dma_start(norm_rows[2:4, :], ins["ffn_norm"]).then_inc(rows_in, 16)
            sp.dma_start(norm_rows[4:5, :], ins["final_norm"].rearrange("(o d) -> o d", o=1)).then_inc(rows_in, 16)
            sp.dma_start(g_rows[0:NB * GP, :], ins["state_gdn_conv"].rearrange("l b w c -> (l b w) c")).then_inc(rows_in, 16)
            sp.dma_start(g_rows[NB * GP:, :], ins["gdn_conv_w"].rearrange(flat)).then_inc(rows_in, 16)
            for l in range(2):
                sp.dma_start(f_rows[l][0:NB * FP, :], ins["state_ffn_conv"][l].rearrange("b w c -> (b w) c")).then_inc(rows_in, 16)
                sp.dma_start(f_rows[l][NB * FP:, :], ins["ffn_conv_w"][l]).then_inc(rows_in, 16)
            sp.dma_start(e_rows, ins["nsa_cmp_pe"].rearrange("l v (c s) d -> (l v c) (s d)", s=2)).then_inc(rows_in, 16)
            sp.dma_start(pages_sb[:], ins["page_table"].rearrange("(o b) n -> o (b n)", o=1)).then_inc(rows_in, 16)
            sp.dma_start(out_norm, ins["gdn_out_norm"].rearrange("l d -> d l")).then_inc(small_in, 16)
            sp.dma_start(a_log, ins["gdn_a_log"].rearrange("l d -> d l")).then_inc(small_in, 16)
            sp.dma_start(dt_bias, ins["gdn_dt_bias"].rearrange("l d -> d l")).then_inc(small_in, 16)
            sp.dma_start(w_ab, ins["gdn_w_in"][0].rearrange("(k p) n -> p k n", p=P)[:, :, CONV_CH + V_DIM:]).then_inc(small_in, 16)
            stream(sp, "gdn_in", pair_source(ins["gdn_w_in"][0]))
            stream(sp, "gdn_out", single_source(ins["gdn_w_out"][0], VH))
            stream(sp, "ffn_up0", ffns[0]["source"])
            stream(sp, "ffn_down0", single_source(ins["ffn_w_down"][0], NFT))
            nsa["stream_in"](sp)
            stream(sp, "nsa_out", pair_source(ins["nsa_w_out"][0]))
            stream(sp, "ffn_up1", ffns[1]["source"])
            stream(sp, "ffn_down1", single_source(ins["ffn_w_down"][1], NFT))

        @block.tensor
        def _(pe):
            compress, project, rows, prompt, prompt_turn, sample, project_out = nsa["pe"]
            pe_turns(pe)
            pe.drain().then_inc(stage_closed, 1)
            pe.wait_ge(stage_closed, 4 * 1)
            norms[0][0](pe)
            pe.drain().then_inc(stage_closed, 1)
            pe.wait_ge(stage_closed, 4 * 2)
            pe_gdn_in(pe)
            pe.drain().then_inc(stage_closed, 1)
            pe.wait_ge(stage_closed, 4 * 3)
            pe_gates(pe)
            pe.drain().then_inc(stage_closed, 1)
            pe.wait_ge(stage_closed, 4 * 4)
            pe_core(pe)
            pe.drain().then_inc(stage_closed, 1)
            pe.wait_ge(stage_closed, 4 * 5)
            pe_gate_norm(pe)
            pe.drain().then_inc(stage_closed, 1)
            pe.wait_ge(stage_closed, 4 * 6)
            pe_add(pe, "gdn_out", o_heads, VH)
            pe.drain().then_inc(stage_closed, 1)
            pe.wait_ge(stage_closed, 4 * 7)
            norms[1][0](pe)
            pe.drain().then_inc(stage_closed, 1)
            pe.wait_ge(stage_closed, 4 * 8)
            ffns[0]["pe"](pe)
            pe.drain().then_inc(stage_closed, 1)
            pe.wait_ge(stage_closed, 4 * 9)
            pe_add(pe, "ffn_down0", ffns[0]["hid"], NFT)
            pe.drain().then_inc(stage_closed, 1)
            pe.wait_ge(stage_closed, 4 * 10)
            compress(pe)
            pe.drain().then_inc(stage_closed, 1)
            pe.wait_ge(stage_closed, 4 * 11)
            norms[2][0](pe)
            pe.drain().then_inc(stage_closed, 1)
            pe.wait_ge(stage_closed, 4 * 12)
            project(pe)
            pe.drain().then_inc(stage_closed, 1)
            pe.wait_ge(stage_closed, 4 * 13)
            rows(pe)
            pe.drain().then_inc(stage_closed, 1)
            pe.wait_ge(stage_closed, 4 * 14)
            prompt(pe)
            pe.drain().then_inc(stage_closed, 1)
            pe.wait_ge(stage_closed, 4 * 15)
            prompt_turn(pe)
            pe.drain().then_inc(stage_closed, 1)
            pe.wait_ge(stage_closed, 4 * 16)
            sample(pe)
            pe.drain().then_inc(stage_closed, 1)
            pe.wait_ge(stage_closed, 4 * 17)
            project_out(pe)
            pe.drain().then_inc(stage_closed, 1)
            pe.wait_ge(stage_closed, 4 * 18)
            norms[3][0](pe)
            pe.drain().then_inc(stage_closed, 1)
            pe.wait_ge(stage_closed, 4 * 19)
            ffns[1]["pe"](pe)
            pe.drain().then_inc(stage_closed, 1)
            pe.wait_ge(stage_closed, 4 * 20)
            pe_add(pe, "ffn_down1", ffns[1]["hid"], NFT)
            pe.drain().then_inc(stage_closed, 1)
            pe.wait_ge(stage_closed, 4 * 21)
            norms[4][0](pe)
            pe.drain().then_inc(stage_closed, 1)
            pe.wait_ge(stage_closed, 4 * 22)
            fin["pe"](pe)

        @block.scalar
        def _(act):
            compress, project, rows, prompt, prompt_turn, sample = nsa["act"]
            copy_turned(act, "act")
            act.drain().then_inc(stage_closed, 1)
            act.wait_ge(stage_closed, 4 * 1)
            norms[0][1](act)
            act.drain().then_inc(stage_closed, 1)
            act.wait_ge(stage_closed, 4 * 2)
            act_gdn_in(act)
            act.drain().then_inc(stage_closed, 1)
            act.wait_ge(stage_closed, 4 * 3)
            act_gates(act)
            act.drain().then_inc(stage_closed, 1)
            act.wait_ge(stage_closed, 4 * 4)
            act_core(act)
            act.drain().then_inc(stage_closed, 1)
            act.wait_ge(stage_closed, 4 * 5)
            act_gate_norm(act)
            act.drain().then_inc(stage_closed, 1)
            act.wait_ge(stage_closed, 4 * 6)
            act.drain().then_inc(stage_closed, 1)
            act.wait_ge(stage_closed, 4 * 7)
            norms[1][1](act)
            act.drain().then_inc(stage_closed, 1)
            act.wait_ge(stage_closed, 4 * 8)
            ffns[0]["act"](act)
            act.drain().then_inc(stage_closed, 1)
            act.wait_ge(stage_closed, 4 * 9)
            act.drain().then_inc(stage_closed, 1)
            act.wait_ge(stage_closed, 4 * 10)
            compress(act)
            act.drain().then_inc(stage_closed, 1)
            act.wait_ge(stage_closed, 4 * 11)
            norms[2][1](act)
            act.drain().then_inc(stage_closed, 1)
            act.wait_ge(stage_closed, 4 * 12)
            project(act)
            act.drain().then_inc(stage_closed, 1)
            act.wait_ge(stage_closed, 4 * 13)
            rows(act)
            act.drain().then_inc(stage_closed, 1)
            act.wait_ge(stage_closed, 4 * 14)
            prompt(act)
            act.drain().then_inc(stage_closed, 1)
            act.wait_ge(stage_closed, 4 * 15)
            prompt_turn(act)
            act.drain().then_inc(stage_closed, 1)
            act.wait_ge(stage_closed, 4 * 16)
            sample(act)
            act.drain().then_inc(stage_closed, 1)
            act.wait_ge(stage_closed, 4 * 17)
            act.drain().then_inc(stage_closed, 1)
            act.wait_ge(stage_closed, 4 * 18)
            norms[3][1](act)
            act.drain().then_inc(stage_closed, 1)
            act.wait_ge(stage_closed, 4 * 19)
            ffns[1]["act"](act)
            act.drain().then_inc(stage_closed, 1)
            act.wait_ge(stage_closed, 4 * 20)
            act.drain().then_inc(stage_closed, 1)
            act.wait_ge(stage_closed, 4 * 21)
            norms[4][1](act)
            act.drain().then_inc(stage_closed, 1)
            act.wait_ge(stage_closed, 4 * 22)
            fin["copy"](act, "act")

        @block.vector
        def _(dve):
            compress, rows, prompt, prompt_turn, sample, project_out = nsa["dve"]
            dve_prepare(dve)
            copy_turned(dve, "dve")
            dve.drain().then_inc(stage_closed, 1)
            dve.wait_ge(stage_closed, 4 * 1)
            norms[0][2](dve)
            dve.drain().then_inc(stage_closed, 1)
            dve.wait_ge(stage_closed, 4 * 2)
            dve_gdn_in(dve)
            dve.drain().then_inc(stage_closed, 1)
            dve.wait_ge(stage_closed, 4 * 3)
            dve_gates(dve)
            dve.drain().then_inc(stage_closed, 1)
            dve.wait_ge(stage_closed, 4 * 4)
            dve_core(dve)
            dve.drain().then_inc(stage_closed, 1)
            dve.wait_ge(stage_closed, 4 * 5)
            dve_gate_norm(dve)
            dve.drain().then_inc(stage_closed, 1)
            dve.wait_ge(stage_closed, 4 * 6)
            dve_add(dve, "gdn_out")
            dve.drain().then_inc(stage_closed, 1)
            dve.wait_ge(stage_closed, 4 * 7)
            norms[1][2](dve)
            dve.drain().then_inc(stage_closed, 1)
            dve.wait_ge(stage_closed, 4 * 8)
            ffns[0]["dve"](dve)
            dve.drain().then_inc(stage_closed, 1)
            dve.wait_ge(stage_closed, 4 * 9)
            dve_add(dve, "ffn_down0")
            dve.drain().then_inc(stage_closed, 1)
            dve.wait_ge(stage_closed, 4 * 10)
            compress(dve)
            dve.drain().then_inc(stage_closed, 1)
            dve.wait_ge(stage_closed, 4 * 11)
            norms[2][2](dve)
            dve.drain().then_inc(stage_closed, 1)
            dve.wait_ge(stage_closed, 4 * 12)
            dve.drain().then_inc(stage_closed, 1)
            dve.wait_ge(stage_closed, 4 * 13)
            rows(dve)
            dve.drain().then_inc(stage_closed, 1)
            dve.wait_ge(stage_closed, 4 * 14)
            prompt(dve)
            dve.drain().then_inc(stage_closed, 1)
            dve.wait_ge(stage_closed, 4 * 15)
            prompt_turn(dve)
            dve.drain().then_inc(stage_closed, 1)
            dve.wait_ge(stage_closed, 4 * 16)
            sample(dve)
            dve.drain().then_inc(stage_closed, 1)
            dve.wait_ge(stage_closed, 4 * 17)
            project_out(dve)
            dve.drain().then_inc(stage_closed, 1)
            dve.wait_ge(stage_closed, 4 * 18)
            norms[3][2](dve)
            dve.drain().then_inc(stage_closed, 1)
            dve.wait_ge(stage_closed, 4 * 19)
            ffns[1]["dve"](dve)
            dve.drain().then_inc(stage_closed, 1)
            dve.wait_ge(stage_closed, 4 * 20)
            dve_add(dve, "ffn_down1")
            dve.drain().then_inc(stage_closed, 1)
            dve.wait_ge(stage_closed, 4 * 21)
            norms[4][2](dve)
            dve.drain().then_inc(stage_closed, 1)
            dve.wait_ge(stage_closed, 4 * 22)
            fin["copy"](dve, "dve")

        @block.gpsimd
        def _(pool):
            compress, project, rows, sample = nsa["pool"]
            pool.drain().then_inc(stage_closed, 1)
            pool.wait_ge(stage_closed, 4 * 1)
            pool.drain().then_inc(stage_closed, 1)
            pool.wait_ge(stage_closed, 4 * 2)
            pool_gdn_rows(pool)
            pool.drain().then_inc(stage_closed, 1)
            pool.wait_ge(stage_closed, 4 * 3)
            pool.drain().then_inc(stage_closed, 1)
            pool.wait_ge(stage_closed, 4 * 4)
            pool_core(pool)
            pool.drain().then_inc(stage_closed, 1)
            pool.wait_ge(stage_closed, 4 * 5)
            pool.drain().then_inc(stage_closed, 1)
            pool.wait_ge(stage_closed, 4 * 6)
            pool.drain().then_inc(stage_closed, 1)
            pool.wait_ge(stage_closed, 4 * 7)
            pool.drain().then_inc(stage_closed, 1)
            pool.wait_ge(stage_closed, 4 * 8)
            ffns[0]["pool"](pool)
            pool.drain().then_inc(stage_closed, 1)
            pool.wait_ge(stage_closed, 4 * 9)
            pool.drain().then_inc(stage_closed, 1)
            pool.wait_ge(stage_closed, 4 * 10)
            compress(pool)
            pool.drain().then_inc(stage_closed, 1)
            pool.wait_ge(stage_closed, 4 * 11)
            pool.drain().then_inc(stage_closed, 1)
            pool.wait_ge(stage_closed, 4 * 12)
            project(pool)
            pool.drain().then_inc(stage_closed, 1)
            pool.wait_ge(stage_closed, 4 * 13)
            rows(pool)
            pool.drain().then_inc(stage_closed, 1)
            pool.wait_ge(stage_closed, 4 * 14)
            pool.drain().then_inc(stage_closed, 1)
            pool.wait_ge(stage_closed, 4 * 15)
            pool.drain().then_inc(stage_closed, 1)
            pool.wait_ge(stage_closed, 4 * 16)
            sample(pool)
            pool.drain().then_inc(stage_closed, 1)
            pool.wait_ge(stage_closed, 4 * 17)
            pool.drain().then_inc(stage_closed, 1)
            pool.wait_ge(stage_closed, 4 * 18)
            pool.drain().then_inc(stage_closed, 1)
            pool.wait_ge(stage_closed, 4 * 19)
            ffns[1]["pool"](pool)
            pool.drain().then_inc(stage_closed, 1)
            pool.wait_ge(stage_closed, 4 * 20)
            pool.drain().then_inc(stage_closed, 1)
            pool.wait_ge(stage_closed, 4 * 21)
            pool.drain().then_inc(stage_closed, 1)
            pool.wait_ge(stage_closed, 4 * 22)
            fin["pool"](pool)


_INS = ['x_prompt', 'x_sample', 'cache_nsa_kv', 'cache_nsa_win', 'state_gdn_s', 'state_gdn_conv', 'state_ffn_conv',
        'page_table', 'gdn_norm', 'gdn_w_in', 'gdn_conv_w', 'gdn_a_log', 'gdn_dt_bias', 'gdn_out_norm', 'gdn_w_out',
        'nsa_norm', 'nsa_w_in', 'nsa_cmp_pe', 'nsa_cmp_w1', 'nsa_cmp_w2', 'nsa_w_out',
        'ffn_norm', 'ffn_w_up', 'ffn_conv_w', 'ffn_w_down', 'final_norm']
_OUTS = [('y_prompt', (1, TP, D)), ('y_sample', (NB, TQ, D)),
         ('kv_rows_prompt', (1, 1, TP, 4, GROUPS, DH)), ('kv_rows_sample', (1, NB, TQ, 4, GROUPS, DH)),
         ('win_prompt', (1, 1, TP, 2, GROUPS, DH)), ('win_sample', (1, NB, WIN, 2, GROUPS, DH)),
         ('gdn_s_prompt', (1, 1, VH, DK, DK)), ('gdn_s_sample', (1, NB, VH, DK, DK)),
         ('gdn_conv_prompt', (1, 1, GP, CONV_CH)), ('gdn_conv_sample', (1, NB, GP, CONV_CH)),
         ('ffn_conv_prompt', (2, 1, FP, FF)), ('ffn_conv_sample', (2, NB, FP, FF))]


def kernel(**inputs):
    import numpy as _np
    import concourse.bacc as _bacc
    from concourse import mybir as _mybir
    from concourse.bass_utils import run_bass_kernel_spmd as _run

    nc = _bacc.Bacc("TRN2", target_bir_lowering=False, num_devices=1)
    tables, where, base_cols = constants()
    arrays, args = {"tables_dram": tables}, {}
    args["tables"] = nc.dram_tensor("tables_dram", tables.shape, _mybir.dt.float32, kind="ExternalInput").ap()
    for name in _INS:
        a = _np.ascontiguousarray(inputs[name])
        arrays[f"in_{name}_dram"] = a
        args[name] = nc.dram_tensor(f"in_{name}_dram", a.shape, _mybir.dt.from_np(a.dtype), kind="ExternalInput").ap()
    outs = {name: nc.dram_tensor(f"out_{name}_dram", shape, _mybir.dt.float32, kind="ExternalOutput").ap()
            for name, shape in _OUTS}
    build(nc, args, outs, where, base_cols)
    r = _run(nc, [arrays], core_ids=[0])
    return tuple(r.results[0][f"out_{name}_dram"] for name, _ in _OUTS)
```

```python
from contextlib import ExitStack

import numpy as np

import concourse.bass as bass
from concourse import mybir

ALU = mybir.AluOpType
ACT = mybir.ActivationFunctionType
F32 = mybir.dt.float32
F32R = mybir.dt.float32r
I32 = mybir.dt.int32
AX = mybir.AxisListType

P = 128
D = 1024
KD = D // P
TP, NB, TQ = 256, 8, 8
TS = NB * TQ
T = TP + TS
EPS = 1e-6

QKH, VH, DK = 8, 16, 128
CONV_CH = (2 * QKH + VH) * DK
V_DIM = VH * DK
NCT = CONV_CH // P
GW = 4
GP = GW - 1
FF = 2816
NFT = FF // P
FW = 3
FP = FW - 1

HEADS, GROUPS, DH = 16, 4, 64
REP = HEADS // GROUPS
Q_DIM = HEADS * DH
KV_DIM = GROUPS * DH
NKV = 6
PAST, PAGE, NPOOL = 1024, 128, 80
NPG = PAST // PAGE
WIN = 512
STRIDE, CLEN, CHID = 16, 32, 256
NSUB = PAST // STRIDE
NCMP = NSUB - 1
PSUB = TP // STRIDE
PCMP = PSUB - 1
SELB, TOPN = 64, 8
NPB = PAST // SELB
FREE_BLKS = NPB - 2
FREE_TOP = TOPN - 3
MASKED = -1e30

RING = 4
SLOT = NFT * P

UNITS = {}
_at = 0
for _name, _n in (("gdn_in", 24), ("gdn_out", 8), ("ffn_up0", 22), ("ffn_down0", 8),
                  ("nsa_in", 10), ("nsa_out", 4), ("ffn_up1", 22), ("ffn_down1", 8)):
    UNITS[_name] = (_at, _n)
    _at += _n


SPLITS = {}
_at = 0
for _name, _n in (("gdn_in", KD), ("gdn_out", 4), ("ffn_up0", KD), ("ffn_down0", 4), ("nsa_in", KD), ("nsa_out", 1),
                  ("ffn_up1", KD), ("ffn_down1", 4)):
    SPLITS[_name] = (_at, _n)
    _at += _n


def split_count(name):
    return sum(SPLITS[name])


def constants():
    parts, where, at = [], {}, 0

    def put(name, a):
        nonlocal at
        a = np.asarray(a, np.float32).reshape(a.shape[0], -1)
        full = np.zeros((P, a.shape[1]), np.float32)
        full[:a.shape[0]] = a
        parts.append(full)
        where[name] = (at, a.shape[1])
        at += a.shape[1]

    eye = np.eye(P)
    t = np.arange(P)
    up = (t[:, None] <= t[None, :]) * 1.0
    same8 = (t[:64, None] // TQ == t[None, :64] // TQ) * 1.0
    pad = lambda a: np.concatenate([a, np.zeros((P - a.shape[0], a.shape[1]))])
    put("ident", eye)
    put("ones", np.ones((P, P)))
    causal3 = np.concatenate([up, up, pad(up[:64, :64] * same8)], 1)
    eye3 = np.concatenate([eye, eye, pad(eye[:64, :64])], 1)
    put("causal3", causal3)
    put("strict3", causal3 - eye3)
    put("eye3", eye3)
    low = [((t[:, None] >> k) % 2 == 1) & ((t[None, :] >> k) == (t[:, None] >> k) - 1) for k in range(7)]
    for k in range(3):
        m = low[k] * 1.0
        put(f"level{k}", np.concatenate([m, m, pad(m[:64, :64])], 1))
    for k in range(3, 7):
        put(f"level{k}", low[k] * 1.0)
    m = low[0].T * 1.0
    put("level0T", np.concatenate([m, m, pad(m[:64, :64])], 1))
    b = np.arange(NB)
    put("tok_seq", (t[:64, None] // TQ == b[None, :]) * 1.0)
    put("col_seq", np.broadcast_to((np.arange(TS)[None, :] // TQ == b[:, None]) * 1.0, (P, NB, TS)))
    carry = np.ones(T)
    carry[[0, 128]] = 0
    carry[TP::TQ] = 0
    put("carry", np.broadcast_to(carry, (VH, T)))
    base = at

    slopes = 2.0 ** (-8.0 * np.arange(1, HEADS + 1) / HEADS)
    put("slopes", np.broadcast_to(slopes, (P, HEADS)))
    pos = np.arange(TP)
    dist = lambda q, k: np.where(q[:, None] >= k[None, :], -(q[:, None] - k[None, :]) * 1.0, -1e33)
    put("dist0", dist(t, pos[:P]))
    put("dist1", dist(t + P, pos))
    ce = np.arange(PCMP) * STRIDE + CLEN - 1
    put("cdist", np.stack([dist(t, ce), dist(t + P, ce)], 1))
    put("cvalid", np.stack([t[:, None] >= ce, t[:, None] + P >= ce], 1) * 1.0)
    row_slope = slopes[t // TQ]
    tq = PAST + t % TQ
    past = np.arange(PAST)
    put("bias_sel", -row_slope[:, None] * (tq[:, None] - past[None, :]))
    k = np.arange(TS)
    new = np.full((P, NB, TS), MASKED)
    for s in range(NB):
        ok = (k[None, :] // TQ == s) & (k[None, :] % TQ <= t[:, None] % TQ)
        new[:, s] = np.where(ok, -row_slope[:, None] * (t[:, None] % TQ - k[None, :] % TQ), MASKED)
    put("bias_new", new)
    dw = tq[:, None] - past[None, PAST - WIN:]
    put("bias_win", np.where(dw < WIN, -row_slope[:, None] * dw, MASKED))
    ce = np.arange(NCMP) * STRIDE + CLEN - 1
    put("bias_cmp", -row_slope[:, None] * (tq[:, None] - ce[None, :]))
    put("group_sum", (t[:, None] // 32 == t[None, :] // 32) & (t[:, None] % TQ == t[None, :] % TQ))
    st = np.arange(NCMP)[:, None] * STRIDE
    bs = (1 + np.arange(FREE_BLKS))[None, :] * SELB
    put("same_q", (t[:64, None] % TQ == t[None, :] % TQ))
    put("own_head", np.repeat(t[:, None] // TQ == np.arange(HEADS)[None, :], 3, axis=1))
    put("overlap", (st < bs + SELB) & (st + CLEN > bs))
    j = np.arange(FREE_BLKS)
    put("earlier", np.broadcast_to(j[None, None, :] < j[None, :, None], (P, FREE_BLKS, FREE_BLKS)))
    return np.concatenate(parts, 1), where, base


class Steps:

    def __init__(self, sem, order, loop, lag):
        self.sem, self.order, self.at, self.first = sem, order, 0, len(order) if lag else 1 if loop else 0
        self.index = {name: n for n, name in enumerate(order)}
        assert len(self.index) == len(order)

    def step(self, name):
        assert self.order[self.at] == name, (name, self.order[self.at])
        self.at = (self.at + 1) % len(self.order)
        return 1

    def count(self, name, it=0):
        return it * len(self.order) + self.index[name] + 1 + self.first

    def all_before(self, it, extra=0):
        return it * len(self.order) + extra + self.first


class Space:

    def __init__(self, low, high, cut, size):
        self.low, self.high, self.cut, self.size, self.at = low, high, cut, size, 0

    def take(self, *dims, parts=P, off=None):
        n = int(np.prod(dims))
        if off is None:
            off = self.at
            self.at += n
        assert off + n <= self.size and (off >= self.cut or off + n <= self.cut), (off, n)
        ap = self.high[0:parts, off - self.cut:off - self.cut + n] if off >= self.cut else self.low[0:parts, off:off + n]
        return shaped(ap, dims)


def shaped(ap, dims):
    if len(dims) > 1:
        names = "abcd"[:len(dims)]
        ap = ap.rearrange(f"p ({' '.join(names)}) -> p {' '.join(names)}", **dict(zip(names, dims)))
    return ap


def seqs(ap):
    return ap.rearrange("p (b q) -> p b q", b=NB)


def build(nc, ins, outs, where, base_cols):
    ctx = ExitStack()
    with ctx:
        def sem(name):
            return ctx.enter_context(nc.semaphore(name))

        def steps(name, order, loop=False, lag=False):
            return Steps(sem(name), order, loop, lag)

        size, cut = 53072, 22840
        sbuf_low = ctx.enter_context(nc.sbuf_tensor("sbuf_resident", [P, cut], F32))
        sbuf_high = ctx.enter_context(nc.sbuf_tensor("sbuf_stages", [P, size - cut], F32))
        sbuf_at = nc._sbuf_addr_for_side(None) - 4 * size
        pages_sb = ctx.enter_context(nc.sbuf_tensor("page_rows", [1, 2 * NB * NPG], I32))
        psum = ctx.enter_context(nc.psum_tensor("psum", [P, 8, 512], F32))
        space = Space(sbuf_low, sbuf_high, cut, size)

        def rounded(name, ap):
            at = ap.offset + (cut if ap.tensor.name == sbuf_high.name else 0)
            dims = ap.shape[1:]
            n = int(np.prod(dims))
            twin = nc.alloc_sbuf_tensor_at(name, [P, n], F32R, offset=sbuf_at + 4 * at, align_bytes=4)
            return shaped(twin[:, 0:n], dims)

        tables = space.take(base_cols)

        def const(name, parts=P):
            at, n = where[name]
            return tables[0:parts, at:at + n]

        ident, ones = const("ident"), const("ones")
        norm_w = space.take(KD, 5)
        gconv = space.take(NCT, NB * GP + GW)
        fconv = [space.take(NFT, NB * FP + FW) for _ in range(2)]
        out_norm = space.take(1)
        a_log = space.take(1, parts=VH)
        dt_bias = space.take(1, parts=VH)
        xT = space.take(KD, T)
        hT = space.take(KD, T)
        rinv = space.take(T)
        w_ab = space.take(KD, 2 * VH)
        w_ab_hi = space.take(KD, 2 * VH)
        ring = [space.take(SLOT) for _ in range(RING)]
        assert space.at <= cut
        xpg_at = space.at = cut
        xpg = [space.take(GP + TP + NB * (GP + TQ)) for _ in range(2)]
        xpf = [v[:, 0:FP + TP + NB * (FP + TQ)] for v in xpg]
        conv_y = [space.take(T) for _ in range(2)]
        kmask_space = space.take(NB * TS, off=space.at - 2 * T)
        tails = space.take(8, 27)
        eps_col = space.take(1)
        embed = space.take(32)
        phase = space.at
        ring_lo = [rounded(f"weights_low{j}", ring[j]) for j in range(RING)]
        hi_at = size - RING * KD * 256
        hi_ring = [rounded(f"weights_high{j}", space.take(KD * 256, off=hi_at + j * KD * 256)) for j in range(RING)]
        wide_at = size - RING * SLOT
        hi_wide = [rounded(f"weights_high_wide{j}", space.take(SLOT, off=wide_at + j * SLOT)) for j in range(RING)]
        hT_rounded = rounded("h_rounded", hT)
        w_ab_lo = rounded("w_ab_low", w_ab)
        w_ab_hi = rounded("w_ab_high", w_ab_hi)

        hi_done, lo_done = sem("weights_high_part_done"), sem("weights_low_part_done")
        x_hi, x_lo = sem("activations_high_part_done"), sem("activations_low_part_done")
        ab_split = sem("ab_columns_split")
        w_in = [sem(f"weights_in_slot{j}") for j in range(RING)]
        half_done = sem("unit_first_tile_done")
        unit_done = sem("unit_done")
        lane_free = [sem(f"lane{l}_banks_free") for l in range(2)]
        stage_closed = sem("stage_closed")
        const_in, rows_in, x_in, small_in = sem("const_in"), sem("rows_in"), sem("x_in"), sem("small_in")
        stored = sem("stored")
        n_stored = [0]

        def slot(w):
            return ring[w % RING]

        space.at = phase
        x_tok = space.take(3, D)
        norm_rows = space.take(D, parts=5)
        g_rows = space.take(CONV_CH, parts=NB * GP + GW)
        f_rows = [space.take(FF, parts=NB * FP + FW) for _ in range(2)]

        e_rows = space.take(P, parts=32)
        turns = []
        for tb, rows in ((0, P), (1, P), (2, TS)):
            for half in range(2):
                turns.append((4 * P, [xT[:, 4 * half:4 * half + 4, tb * P:tb * P + rows]],
                              [(x_tok[0:rows, tb, (4 * half + j) * P:(4 * half + j + 1) * P], rows, j * P)
                               for j in range(4)], rows))
        turns.append((0, [norm_w], [(norm_rows[:, k * P:(k + 1) * P], 5, 5 * k) for k in range(KD)], 5))
        n = NB * GP + GW
        for half in range(2):
            turns.append((0, [gconv[:, 16 * half:16 * half + 16, :]],
                          [(g_rows[:, (16 * half + j) * P:(16 * half + j + 1) * P], n, n * j)
                           for j in range(16)], n))
        n = NB * FP + FW
        for l in range(2):
            turns.append((0, [fconv[l]], [(f_rows[l][:, k * P:(k + 1) * P], n, n * k) for k in range(NFT)], n))
        turns.append((0, [embed.rearrange("p (a b) -> p a b", a=1)], [(e_rows, 32, 0)], 32))
        NTURN = len(turns)
        S1 = dict(pe=steps("turned", [f"g{n}" for n in range(NTURN)]),
                  dve=steps("turned_copied_dve", [f"g{n}" for n in range(0, NTURN, 2)]),
                  act=steps("turned_copied_act", [f"g{n}" for n in range(1, NTURN, 2)]))

        def pe_turns(pe):
            pe.wait_ge(const_in, 16)
            for n, (_, dst, items, rows) in enumerate(turns):
                if n == 0:
                    pe.wait_ge(x_in, 32)
                if n == 6:
                    pe.wait_ge(rows_in, 16 * 13)
                if n >= 8:
                    pe.wait_ge(S1["dve" if n % 2 == 0 else "act"].sem, S1["dve" if n % 2 == 0 else "act"].count(f"g{n - 8}"))
                for src, r, col in items:
                    last = pe.transpose(psum[:, n % 8, col:col + r], src, ident[0:r, 0:r])
                last.then_inc(S1["pe"].sem, S1["pe"].step(f"g{n}"))

        def copy_turned(eng, kind):
            for n, (pitch, dst, items, rows) in enumerate(turns):
                if n % 2 != (kind == "act"):
                    continue
                eng.wait_ge(S1["pe"].sem, S1["pe"].count(f"g{n}"))
                a, b = dst[0].shape[1], dst[0].shape[2]
                if pitch:
                    src = psum[:, n % 8, :].rearrange("p (a b) -> p a b", a=4)[:, :, 0:rows]
                else:
                    src = psum[:, n % 8, 0:a * b].rearrange("p (a b) -> p a b", a=a)
                ins_ = eng.tensor_copy(dst[0], src) if kind == "dve" else eng.copy(dst[0], src)
                ins_.then_inc(S1[kind].sem, S1[kind].step(f"g{n}"))

        def dve_prepare(dve):
            dve.memset(eps_col, EPS)
            dve.memset(xpg[0][:, 0:GP], 0.0).then_inc(lane_free[0], 2)
            dve.memset(xpg[1][:, 0:GP], 0.0).then_inc(lane_free[1], 2)

        def norm_stage(name, which, low=None, low_rounded=None, units=None):
            steps_of = dict(act=steps(f"{name}_act", ["square", "root"]),
                            pe=steps(f"{name}_pe", ["sum"]),
                            dve=steps(f"{name}_dve", ["inverse"] + [f"scaled{k}" for k in range(KD)]))
            pe_steps, act_steps, dve_steps = steps_of["pe"], steps_of["act"], steps_of["dve"]

            def act(eng):
                eng.activation(hT, xT, ACT.Square).then_inc(act_steps.sem, act_steps.step("square"))
                for j in range(2 if low else 0):
                    high_part(eng, units, 0, j, KD * 2, free=True)
                eng.wait_ge(pe_steps.sem, pe_steps.count("sum"))
                eng.activation(rinv, psum[:, 0, 0:T], ACT.Sqrt, bias=eps_col, scale=1.0 / D).then_inc(act_steps.sem, act_steps.step("root"))
                if low:
                    for k in range(KD):
                        eng.wait_ge(dve_steps.sem, dve_steps.count(f"scaled{k}"))
                        eng.copy(hT_rounded[:, k, :], low(k)).then_inc(x_hi, 1)

            def pe(eng):
                eng.wait_ge(act_steps.sem, act_steps.count("square"))
                for k in range(KD):
                    last = eng.matmul(psum[:, 0, 0:T], ones, hT[:, k, :], start=(k == 0), stop=(k == KD - 1))
                last.then_inc(pe_steps.sem, pe_steps.step("sum"))

            def dve(eng):
                eng.wait_ge(act_steps.sem, act_steps.count("root"))
                eng.reciprocal(rinv, rinv).then_inc(dve_steps.sem, dve_steps.step("inverse"))
                eng.wait_ge(dve_steps.sem, dve_steps.count("inverse"))
                for k in range(KD):
                    out = low(k) if low else hT[:, k, :]
                    eng.scalar_tensor_tensor(out=out, in0=xT[:, k, :], scalar=norm_w[:, k, which:which + 1], in1=rinv,
                                             op0=ALU.mult, op1=ALU.mult).then_inc(dve_steps.sem, dve_steps.step(f"scaled{k}"))
                if low:
                    for k in range(KD):
                        eng.wait_ge(x_hi, SPLITS[units][0] + k + 1)
                        eng.tensor_tensor(low_rounded(k), low(k), hT_rounded[:, k, :], ALU.subtract).then_inc(x_lo, 1)
            return dict(pe=pe, act=act, dve=dve)

        half_before, lane_before = {}, [{}, {}]
        h, ln = 0, [0, 0]
        for name, (w0, n) in UNITS.items():
            two = not ("out" in name and name == "gdn_out" or "down" in name)
            half_before[name] = h
            lane_before[0][name], lane_before[1][name] = ln
            h += n * two
            ln = [ln[0] + n * two, ln[1] + n]

        def stream(sp, name, source):
            w0, n = UNITS[name]

            def load(i, j, fresh=False):
                if not fresh:
                    sp.wait_ge(unit_done, w0 + 4 * i + j - RING + 1)
                for dst, src in source(4 * i + j, slot(w0 + j)):
                    sp.dma_start(dst, src).then_inc(w_in[(w0 + j) % RING], 16)

            first = 1 if w0 == 0 else 0
            for j in range(4 * first):
                load(0, j, fresh=True)
            with sp.Fori(first, n // 4) as i:
                for j in range(4):
                    load(i, j)
            for j in range(n % 4):
                load(n // 4, j)

        tile_done = (half_done, unit_done)

        def landed_count(name, i, j):
            w = UNITS[name][0] + j
            more = 32 if w >= UNITS["nsa_in"][0] else 0
            return 32 * (w // RING + i + 1) + more

        def high_part(act, name, i, j, kn, free=False):
            w = UNITS[name][0] + j
            dst = (hi_wide if "down" in name else hi_ring)[w % RING]
            act.wait_ge(w_in[w % RING], landed_count(name, i, j))
            if not free:
                act.wait_ge(unit_done, w + 4 * i - RING + 1)
            act.copy(dst[:, 0:kn * P], slot(w)[:, 0:kn * P]).then_inc(hi_done, 1)

        def high_parts(act, name, kn):
            n = UNITS[name][1]
            with act.Fori(0, n // 4) as i:
                for j in range(4):
                    high_part(act, name, i, j, kn)

        def low_part(pool, name, i, j, kn):
            w = UNITS[name][0] + j
            hi = (hi_wide if "down" in name else hi_ring)[w % RING]
            pool.wait_ge(hi_done, w + 4 * i + 1)
            sl = slot(w)[:, 0:kn * P]
            pool.tensor_tensor(ring_lo[w % RING][:, 0:kn * P], sl, hi[:, 0:kn * P], ALU.subtract).then_inc(lo_done, 1)

        def low_parts(pool, name, kn):
            n = UNITS[name][1]
            with pool.Fori(0, n // 4) as i:
                for j in range(4):
                    low_part(pool, name, i, j, kn)
            for j in range(n % 4):
                low_part(pool, name, n // 4, j, kn)

        def free_count(name, i, j, l):
            return lane_before[l][name] + 4 * i + j + 1

        def read_count(name, i, j, l):
            return lane_before[l][name] + 4 * i + j + 3

        def product_count(name, i, j, l):
            if l == 0:
                return half_before[name] + 4 * i + j + 1
            return UNITS[name][0] + 4 * i + j + 1

        def bank(name, j, l):
            return psum[:, 2 * l + (UNITS[name][0] + j) % 2, :]

        def one(ap):
            return ap.rearrange("p o t -> p (o t)")

        def three_products(pe, out, w_hi, w_lo, x_hi_tile, x_lo_tile, first, last):
            pe.matmul(out, w_lo, x_hi_tile, start=first, stop=False)
            pe.matmul(out, w_hi, x_lo_tile, start=False, stop=False)
            return pe.matmul(out, w_hi, x_hi_tile, start=False, stop=last)

        def multiply_unit(pe, name, i, j, tile, high, low, kn, lanes=(0, 1)):
            w = UNITS[name][0] + j
            pe.wait_ge(lo_done, w + 4 * i + 1)
            lo, hi = ring_lo[w % RING], (hi_wide if "down" in name else hi_ring)[w % RING]
            for l in lanes:
                pe.wait_ge(lane_free[l], free_count(name, i, j, l))
                for k in range(kn):
                    last = three_products(pe, bank(name, j, l)[:, 0:T], tile(hi, k, l), tile(lo, k, l), high(k), low(k),
                                          k == 0, k == kn - 1)
                last.then_inc(half_done if l == 0 else unit_done, 1)

        def pair_tile(sl, k, l):
            return sl[:, 0:KD * 256].rearrange("p (k n) -> p k n", k=KD)[:, k, l * P:(l + 1) * P]

        def pair_source(w):
            v = w.rearrange("(k p) n -> p k n", p=P)

            def source(n, sl):
                dst = sl[:, 0:KD * 256].rearrange("p (k n) -> p k n", k=KD)
                return [(dst[:, h:h + 4, :], v[:, h:h + 4, bass.ds(n * 256, 256)]) for h in (0, 4)]
            return source

        def single_source(w, kn):
            v = w.rearrange("(k p) n -> p k n", p=P)
            m = kn // 2

            def source(n, sl):
                dst = sl[:, 0:kn * P].rearrange("p (k n) -> p k n", k=kn)
                return [(dst[:, a:b, :], v[:, a:b, bass.ds(n * P, P)]) for a, b in ((0, m), (m, kn))]
            return source

        def single_tile(kn):
            return lambda sl, k, l: sl[:, 0:kn * P].rearrange("p (k n) -> p k n", k=kn)[:, k, :]

        def padded(xp, hist):
            return xp[:, hist + TP:hist + TP + NB * (hist + TQ)].rearrange("p (b c) -> p b c", b=NB)

        def take_in(act, src, xp, tail, state, hist):
            pad = padded(xp, hist)
            act.copy(pad[:, :, 0:hist], state)
            act.copy(xp[:, hist:hist + TP], src[:, 0:TP])
            act.copy(tail[:, 0:hist], src[:, TP - hist:TP])
            act.copy(pad[:, :, hist:hist + TQ], seqs(src[:, TP:T]))
            return act.copy(tail[:, hist:hist + NB * hist].rearrange("p (b c) -> p b c", b=NB),
                            seqs(src[:, TP:T])[:, :, TQ - hist:TQ])

        def conv(dve, taps_done, it, tag, xp, y, taps, hist):
            pad = padded(xp, hist)
            for n in range(hist + 1):
                for part in "ps":
                    src = xp[:, n:n + TP] if part == "p" else pad[:, :, n:n + TQ]
                    dst = y[:, 0:TP] if part == "p" else seqs(y[:, TP:T])
                    if n == 0:
                        ins_ = dve.tensor_scalar(dst, src, taps(0), None, ALU.mult)
                    else:
                        dve.wait_ge(taps_done.sem, taps_done.count(f"{tag}t{n - 1}{part}", it))
                        ins_ = dve.scalar_tensor_tensor(out=dst, in0=src, scalar=taps(n), in1=dst,
                                                        op0=ALU.mult, op1=ALU.add)
                    ins_.then_inc(taps_done.sem, taps_done.step(f"{tag}t{n}{part}"))

        def conv_steps(tag, hist):
            return [f"{tag}t{n}{part}" for n in range(hist + 1) for part in "ps"]

        space.at = phase
        qkv = space.take(NCT, T)
        z = space.take(VH, T)
        core = space.at
        conv_rows = space.take(CONV_CH, parts=NB * GP + GP)
        BT = 8
        S3 = dict(pe=steps("gdn_tails_turned", ["tails"]),
                  act=steps("gdn_silu", [f"silu{j}" for j in range(BT)] + ["rows"], loop=True),
                  dve=steps("gdn_conv", [x for j in range(BT) for x in conv_steps(f"{j}", GP)]))
        ab_done, conv_rows_stored = sem("ab_done"), sem("gdn_conv_rows_stored")
        NQ = NCT // BT
        g_low = lambda k: ring[k // 2][:, KD * 256 + (k % 2) * T:KD * 256 + (k % 2 + 1) * T]
        g_low_rounded = lambda k: ring_lo[k // 2][:, KD * 256 + (k % 2) * T:KD * 256 + (k % 2 + 1) * T]
        h_high = lambda k: hT_rounded[:, k, :]

        def pe_gdn_in(pe):
            pe.wait_ge(x_lo, split_count("gdn_in"))
            with pe.Fori(0, NQ) as i:
                for j in range(4):
                    multiply_unit(pe, "gdn_in", i, j, pair_tile, h_high, g_low_rounded, KD)
                pe.wait_ge(lane_free[1], read_count("gdn_in", i, 3, 1))
                for j in range(BT):
                    last = pe.transpose(psum[0:27, 4 + j // 4, (j % 4) * P:(j % 4 + 1) * P], tails[:, j, :], ident)
                last.then_inc(S3["pe"].sem, S3["pe"].step("tails"))
            with pe.Fori(NQ, 6) as i:
                for j in range(4):
                    multiply_unit(pe, "gdn_in", i, j, pair_tile, h_high, g_low_rounded, KD)
            pe.wait_ge(ab_split, 2)
            for half in range(2):
                for k in range(KD):
                    cols = slice(half * VH, (half + 1) * VH)
                    last = three_products(pe, psum[0:VH, 6 + half, 0:T], w_ab_hi[:, k, cols], w_ab_lo[:, k, cols], h_high(k), g_low_rounded(k),
                                          k == 0, k == KD - 1)
            last.then_inc(ab_done, 1)

        def act_gdn_in(act):
            act.sem_inc(S3["act"].sem, 1)

            def silu(i, j):
                act.wait_ge(S3["dve"].sem, S3["dve"].count(f"{j}t{GP}s", i))
                act.activation(one(qkv[:, bass.ds(8 * i + j, 1), :]), conv_y[j % 2], ACT.Silu).then_inc(
                    S3["act"].sem, S3["act"].step(f"silu{j}"))

            def z_tiles(i, ahead):
                for j in range(BT):
                    act.wait_ge(tile_done[j % 2], product_count("gdn_in", i, j // 2, j % 2))
                    if j % 2 == 0 and j // 2 < ahead:
                        high_part(act, "gdn_in", i, j // 2 + 2, KD * 2, free=True)
                    act.activation(one(z[:, bass.ds(8 * i + j - NCT, 1), :]), bank("gdn_in", j // 2, j % 2)[:, 0:T],
                                   ACT.Silu).then_inc(lane_free[j % 2], 1)
            act.wait_ge(small_in, 16 * 4)
            act.copy(w_ab_hi, w_ab).then_inc(ab_split, 1)
            with act.Fori(0, NQ) as i:
                for j in range(BT):
                    act.wait_ge(tile_done[j % 2], product_count("gdn_in", i, j // 2, j % 2))
                    if j % 2 == 0:
                        high_part(act, "gdn_in", i, j // 2 + 2, KD * 2, free=True)
                    state = gconv[:, bass.ds(8 * i + j, 1), 0:NB * GP].rearrange("p o (b c) -> p (o b) c", b=NB)
                    last = take_in(act, bank("gdn_in", j // 2, j % 2), xpg[j % 2], tails[:, j, :], state, GP)
                    last.then_inc(lane_free[j % 2], 1)
                    if j:
                        silu(i, j - 1)
                silu(i, BT - 1)
                act.wait_ge(S3["pe"].sem, S3["pe"].count("tails", i))
                act.copy(conv_rows[:, bass.ds(1024 * i, 1024)].rearrange("p (a b) -> p a b", a=2),
                         psum[0:27, 4:6, :]).then_inc(S3["act"].sem, S3["act"].step("rows"))
            act.wait_ge(S3["act"].sem, S3["act"].count("rows", NQ - 1))
            act.dma_start(outs["gdn_conv_prompt"].rearrange("l b w c -> (l b w) c"), conv_rows[0:GP, :]).then_inc(conv_rows_stored, 16)
            act.dma_start(outs["gdn_conv_sample"].rearrange("l b w c -> (l b w) c"), conv_rows[GP:27, :]).then_inc(conv_rows_stored, 16)
            for i, ahead in ((4, 4), (5, 2)):
                z_tiles(i, ahead)

        def pool_gdn_in(pool):
            pool.wait_ge(ab_split, 1)
            pool.tensor_tensor(w_ab_lo, w_ab, w_ab_hi, ALU.subtract).then_inc(ab_split, 1)
            low_parts(pool, "gdn_in", KD * 2)
            pool.wait_ge(conv_rows_stored, 32)

        def dve_gdn_in(dve):
            with dve.Fori(0, NQ) as i:
                for j in range(BT):
                    dve.wait_ge(lane_free[j % 2], read_count("gdn_in", i, j // 2, j % 2))
                    if j >= 2:
                        dve.wait_ge(S3["act"].sem, S3["act"].count(f"silu{j - 2}", i))
                    else:
                        dve.wait_ge(S3["act"].sem, S3["act"].all_before(i))
                    conv(dve, S3["dve"], i, f"{j}", xpg[j % 2], conv_y[j % 2],
                         lambda n: one(gconv[:, bass.ds(8 * i + j, 1), NB * GP + n:NB * GP + n + 1]), GP)

        space.at = core
        rows4 = space.take(4, T, parts=VH)
        gtok = space.take(3, 4, VH)
        scratch = space.at
        gx = [space.take(T, parts=VH) for _ in range(4)]
        ea = space.take(1, parts=VH)
        sq = space.take(4, T)
        inv = space.take(4, T)
        C_G, C_B, C_E, C_N = range(4)
        S4 = dict(pe=steps("gates_pe", ["turned"] + [f"sum{g}" for g in range(4)]),
                  dve=steps("gates_dve", ["pad", "dt", "relu", "den", "beta", "soft", "g", "scan", "gap0", "gap", "nb", "tok", "toks"]
                            + [f"{x}{g}" for g in range(4) for x in ("eps", "inv", "out")]),
                  act=steps("gates_act", ["nbexp", "abs", "expn", "log", "ea", "egap", "eg"]
                            + [f"{x}{g}" for g in range(4) for x in ("sq", "root")]))

        def act_gates(act):
            act_steps, dve_steps = S4["act"], S4["dve"]
            act.wait_ge(ab_done, 1)
            act.wait_ge(small_in, 16 * 4)
            act.activation(gx[0], psum[0:VH, 7, 0:T], ACT.Exp, scale=-1.0).then_inc(act_steps.sem, act_steps.step("nbexp"))
            act.wait_ge(dve_steps.sem, dve_steps.count("dt"))
            act.activation(gx[2], gx[1], ACT.Abs).then_inc(act_steps.sem, act_steps.step("abs"))
            act.wait_ge(act_steps.sem, act_steps.count("abs"))
            act.activation(gx[2], gx[2], ACT.Exp, scale=-1.0).then_inc(act_steps.sem, act_steps.step("expn"))
            act.wait_ge(act_steps.sem, act_steps.count("expn"))
            act.activation(gx[2], gx[2], ACT.Ln, bias=1.0).then_inc(act_steps.sem, act_steps.step("log"))
            act.activation(ea, a_log, ACT.Exp).then_inc(act_steps.sem, act_steps.step("ea"))
            act.wait_ge(dve_steps.sem, dve_steps.count("gap"))
            act.activation(rows4[:, C_E, :], gx[3], ACT.Exp).then_inc(act_steps.sem, act_steps.step("egap"))
            act.activation(gx[1], rows4[:, C_G, :], ACT.Exp).then_inc(act_steps.sem, act_steps.step("eg"))
            for g in range(4):
                if g:
                    act.wait_ge(S4["pe"].sem, S4["pe"].count(f"sum{g - 1}"))
                act.activation(sq, qkv[:, 4 * g:4 * g + 4, :], ACT.Square).then_inc(act_steps.sem, act_steps.step(f"sq{g}"))
                act.wait_ge(dve_steps.sem, dve_steps.count(f"eps{g}"))
                act.activation(inv, inv, ACT.Sqrt).then_inc(act_steps.sem, act_steps.step(f"root{g}"))

        def dve_gates(dve):
            dve_steps, act_steps = S4["dve"], S4["act"]
            dve.memset(gtok, 0.0).then_inc(dve_steps.sem, dve_steps.step("pad"))
            dve.wait_ge(ab_done, 1)
            dve.wait_ge(small_in, 16 * 4)
            dve.tensor_scalar(gx[1], psum[0:VH, 6, 0:T], dt_bias, None, ALU.add).then_inc(dve_steps.sem, dve_steps.step("dt"))
            dve.wait_ge(dve_steps.sem, dve_steps.count("dt"))
            dve.tensor_scalar(gx[3], gx[1], 0.0, None, ALU.max).then_inc(dve_steps.sem, dve_steps.step("relu"))
            dve.wait_ge(act_steps.sem, act_steps.count("nbexp"))
            dve.tensor_scalar(gx[0], gx[0], 1.0, None, ALU.add).then_inc(dve_steps.sem, dve_steps.step("den"))
            dve.wait_ge(dve_steps.sem, dve_steps.count("den"))
            dve.reciprocal(rows4[:, C_B, :], gx[0]).then_inc(dve_steps.sem, dve_steps.step("beta"))
            dve.wait_ge(act_steps.sem, act_steps.count("ea"))
            dve.tensor_tensor(gx[3], gx[3], gx[2], ALU.add).then_inc(dve_steps.sem, dve_steps.step("soft"))
            dve.wait_ge(dve_steps.sem, dve_steps.count("soft"))
            dve.tensor_scalar(gx[3], gx[3], ea, -1.0, ALU.mult, ALU.mult).then_inc(dve_steps.sem, dve_steps.step("g"))
            dve.wait_ge(dve_steps.sem, dve_steps.count("g"))
            dve.tensor_tensor_scan(rows4[:, C_G, :], const("carry", VH), gx[3], 0.0, ALU.mult, ALU.add).then_inc(dve_steps.sem, dve_steps.step("scan"))
            dve.wait_ge(dve_steps.sem, dve_steps.count("scan"))
            g = rows4[:, C_G, :]
            dve.tensor_tensor(gx[3][:, 0:TP].rearrange("p (a b) -> p a b", a=2),
                                     g[:, P - 1:TP:P].unsqueeze(2).to_broadcast([VH, 2, P]),
                                     g[:, 0:TP].rearrange("p (a b) -> p a b", a=2), ALU.subtract).then_inc(dve_steps.sem, dve_steps.step("gap0"))
            dve.tensor_tensor(seqs(gx[3][:, TP:T]), g[:, TP + TQ - 1:T:TQ].unsqueeze(2).to_broadcast([VH, NB, TQ]),
                                     seqs(g[:, TP:T]), ALU.subtract).then_inc(dve_steps.sem, dve_steps.step("gap"))
            dve.wait_ge(act_steps.sem, act_steps.count("eg"))
            dve.scalar_tensor_tensor(out=rows4[:, C_N, :], in0=rows4[:, C_B, :], scalar=-1.0, in1=gx[1],
                                            op0=ALU.mult, op1=ALU.mult).then_inc(dve_steps.sem, dve_steps.step("nb"))
            dve.wait_ge(S4["pe"].sem, S4["pe"].count("turned"))
            turned = psum[:, 5, 0:3 * 4 * VH].rearrange("p (u c h) -> p u c h", u=3, c=4)
            dve.tensor_copy(gtok[:, 0:2], turned[:, 0:2]).then_inc(dve_steps.sem, dve_steps.step("tok"))
            dve.tensor_copy(gtok[0:TS, 2], turned[0:TS, 2]).then_inc(dve_steps.sem, dve_steps.step("toks"))
            for g in range(4):
                dve.wait_ge(S4["pe"].sem, S4["pe"].count(f"sum{g}"))
                if g:
                    dve.wait_ge(dve_steps.sem, dve_steps.count(f"out{g - 1}"))
                dve.tensor_scalar(inv, psum[:, 0:4, 0:T], EPS, None, ALU.add).then_inc(dve_steps.sem, dve_steps.step(f"eps{g}"))
                dve.wait_ge(act_steps.sem, act_steps.count(f"root{g}"))
                dve.reciprocal(inv, inv).then_inc(dve_steps.sem, dve_steps.step(f"inv{g}"))
                dve.wait_ge(dve_steps.sem, dve_steps.count(f"inv{g}"))
                t = qkv[:, 4 * g:4 * g + 4, :]
                dve.scalar_tensor_tensor(out=t, in0=inv, scalar=float(DK) ** -0.5 if g < 2 else 1.0, in1=t,
                                                op0=ALU.mult, op1=ALU.mult).then_inc(dve_steps.sem, dve_steps.step(f"out{g}"))

        def pe_gates(pe):
            act_steps, dve_steps = S4["act"], S4["dve"]
            pe.wait_ge(dve_steps.sem, dve_steps.count("nb"))
            for u, (c0, n) in enumerate(((0, P), (P, P), (TP, TS))):
                for c in range(4):
                    at = (u * 4 + c) * VH
                    last = pe.transpose(psum[0:n, 5, at:at + VH], rows4[:, c, c0:c0 + n], ident[0:VH, 0:VH])
            last.then_inc(S4["pe"].sem, S4["pe"].step("turned"))
            for g in range(4):
                pe.wait_ge(act_steps.sem, act_steps.count(f"sq{g}"))
                if g:
                    pe.wait_ge(dve_steps.sem, dve_steps.count(f"eps{g - 1}"))
                for j in range(4):
                    last = pe.matmul(psum[:, j, 0:T], ones, sq[:, j, :], start=True, stop=True)
                last.then_inc(S4["pe"].sem, S4["pe"].step(f"sum{g}"))

        space.at = scratch
        W3 = 3 * P
        kS = space.take(W3)
        qS = space.take(T)
        hd = []
        for _ in range(2):
            start = space.at
            h = dict(X=space.take(T), v=space.take(W3), at=space.take(W3), bts=space.take(W3), egc=space.take(T),
                     qkd=space.take(T), qd=space.take(T), kdec=space.take(3, P), S=space.take(2, P), S0=space.take(NB, P))
            h["spread"] = space.take(NB, P, off=start)
            h["rows"] = space.take(2, T, parts=VH, off=space.at)
            h["R"], h["vn"] = space.take(3, P), space.take(3, P)
            hd.append(h)
        ktok = space.take(3, P)
        kmask = kmask_space.rearrange("p (b c) -> p b c", b=NB)
        for h in hd:
            h["P"] = h["bts"]
            h["Y"] = space.take(W3)
            h["dec"] = h["Y"][:, 0:T]
        row_src = [h["rows"] for h in hd]
        o_heads = qkv[:, 2 * QKH:, :]
        LEVELS = 7
        width = lambda k: T if k < 3 else TP
        both = lambda names: [f"{x}{h}" for x in names for h in range(2)]
        S5 = dict(
            pe=steps("core_pe", ["gram", "ktok"] + both(["rows"]) + both(["at"])
                     + [f"{x}{k}{h}" for k in range(1, LEVELS) for x in "pxy" for h in range(2) if not (x == "x" and k == LEVELS - 1)]
                     + both(["vtok", "ks", "v0", "s1", "ks1", "v1", "s2", "o"]) + both(["snew"]), loop=True),
            dve=steps("core_dve", both(["row", "bts", "d", "cd", "at1", "at2", "qkd", "qd", "ya", "yb", "xa", "xb"])
                      + [f"{x}{k}{h}" for k in range(1, LEVELS) for x in "pxy" for h in range(2) if not (x == "x" and k == LEVELS - 1)]
                      + both(["rs", "vn0", "vns", "s1", "r1", "vn1", "s2"]) + both(["snew"]), loop=True),
            act=steps("core_act", ["k", "q"] + both(["v"]) + ["ktok"] + both(["egc", "dec", "kdec", "r"]) + both(["o"]), loop=True),
            pool=steps("core_pool", ["kmask", "s0g0", "spread0", "s0g1", "spread1"], loop=True))
        state_in, state_out, pads = sem("states_in"), sem("states_out"), sem("core_pads")
        PB = [(2, 3, 4), (5, 6, 7)]

        STATES = 64

        def pe_core(pe):
            pe_steps, dve_steps, act_steps, pool_steps = S5["pe"], S5["dve"], S5["act"], S5["pool"]
            chunk = [(0, P), (P, P), (TP, TS)]
            pe.sem_inc(pe_steps.sem, 1)
            pe.wait_ge(pads, 9)
            with pe.Fori(0, QKH) as i:
                pe.wait_ge(act_steps.sem, act_steps.count("v1", i))
                pe.wait_ge(dve_steps.sem, dve_steps.all_before(i))
                for rhs, b in ((kS, 0), (qS, 1)):
                    for c0, n in chunk:
                        last = pe.matmul(psum[:, b, c0:c0 + n], kS[:, c0:c0 + P], rhs[:, c0:c0 + n], start=True, stop=True)
                last.then_inc(pe_steps.sem, pe_steps.step("gram"))
                for u in range(3):
                    last = pe.transpose(psum[:, 4, u * P:(u + 1) * P], kS[:, u * P:(u + 1) * P], ident)
                last.then_inc(pe_steps.sem, pe_steps.step("ktok"))
                for h in range(2):
                    if h == 0:
                        pe.wait_ge(act_steps.sem, act_steps.all_before(i))
                    pe.wait_ge(dve_steps.sem, dve_steps.count(f"row{h}", i))
                    for q in range(2):
                        last = pe.matmul(psum[:, PB[h][q], 0:T], ones[0:VH, :], row_src[h][:, q, :], start=True, stop=True)
                    last.then_inc(pe_steps.sem, pe_steps.step(f"rows{h}"))
                for h in range(2):
                    pe.wait_ge(dve_steps.sem, dve_steps.count(f"at2{h}", i))
                    if h == 0:
                        pe.wait_ge(act_steps.sem, act_steps.count("ktok", i))
                    for u in range(3):
                        last = pe.transpose(psum[:, PB[h][2], u * P:(u + 1) * P], hd[h]["at"][:, u * P:(u + 1) * P], ident)
                    last.then_inc(pe_steps.sem, pe_steps.step(f"at{h}"))
                for k in range(1, LEVELS):
                    cs = chunk if k < 3 else chunk[:2]
                    for h in range(2):
                        d = hd[h]
                        pe.wait_ge(dve_steps.sem, dve_steps.count(f"xb{h}" if k == 1 else f"x{k - 1}{h}", i))
                        for c0, n in cs:
                            last = pe.matmul(psum[:, PB[h][0], c0:c0 + n], d["at"][:, c0:c0 + P], d["X"][:, c0:c0 + n], start=True, stop=True)
                        last.then_inc(pe_steps.sem, pe_steps.step(f"p{k}{h}"))
                    if k < LEVELS - 1:
                        for h in range(2):
                            d = hd[h]
                            pe.wait_ge(dve_steps.sem, dve_steps.count(f"p{k}{h}", i))
                            if k > 1:
                                pe.wait_ge(dve_steps.sem, dve_steps.count(f"y{k - 1}{h}", i))
                            for c0, n in cs:
                                last = pe.matmul(psum[:, PB[h][1], c0:c0 + n], d["Y"][:, c0:c0 + P], d["P"][:, c0:c0 + n], start=True, stop=True)
                            last.then_inc(pe_steps.sem, pe_steps.step(f"x{k}{h}"))
                    for h in range(2):
                        d = hd[h]
                        pe.wait_ge(dve_steps.sem, dve_steps.count(f"p{k}{h}", i))
                        if k == LEVELS - 1:
                            pe.wait_ge(dve_steps.sem, dve_steps.count(f"y{k - 1}{h}", i))
                        for c0, n in cs:
                            last = pe.matmul(psum[:, PB[h][2], c0:c0 + n], d["P"][:, c0:c0 + P], d["Y"][:, c0:c0 + n], start=True, stop=True)
                        last.then_inc(pe_steps.sem, pe_steps.step(f"y{k}{h}"))
                for h in range(2):
                    pe.wait_ge(dve_steps.sem, dve_steps.count(f"p{LEVELS - 1}{h}", i))
                    for u in range(3):
                        last = pe.transpose(psum[:, PB[h][0], u * P:(u + 1) * P], hd[h]["v"][:, u * P:(u + 1) * P], ident)
                    last.then_inc(pe_steps.sem, pe_steps.step(f"vtok{h}"))
                for h in range(2):
                    pe.wait_ge(pool_steps.sem, pool_steps.count("kmask", i))
                    pe.wait_ge(state_in, 32 * (i + 1))
                    for b in range(NB):
                        last = pe.matmul(psum[0:TS, PB[h][1], 0:P], kmask[:, b, :], hd[h]["S0"][:, b, :], start=(b == 0), stop=(b == NB - 1))
                    last.then_inc(pe_steps.sem, pe_steps.step(f"ks{h}"))
                for h in range(2):
                    d = hd[h]
                    pe.wait_ge(dve_steps.sem, dve_steps.count(f"rs{h}", i))
                    pe.wait_ge(dve_steps.sem, dve_steps.count(f"y{LEVELS - 1}{h}", i))
                    pe.wait_ge(act_steps.sem, act_steps.count(f"r{h}", i))
                    pe.matmul(psum[:, PB[h][1], P:2 * P], d["Y"][:, 0:P], d["R"][:, 0, :], start=True, stop=True)
                    last = pe.matmul(psum[0:TS, PB[h][1], 2 * P:3 * P], d["Y"][0:TS, TP:T], d["R"][0:TS, 2, :], start=True, stop=True)
                    last.then_inc(pe_steps.sem, pe_steps.step(f"v0{h}"))
                for h in range(2):
                    d = hd[h]
                    pe.wait_ge(dve_steps.sem, dve_steps.count(f"vn0{h}", i))
                    pe.matmul(psum[:, PB[h][2], 0:P], d["kdec"][:, 0, :], d["vn"][:, 0, :], start=True, stop=True).then_inc(pe_steps.sem, pe_steps.step(f"s1{h}"))
                for h in range(2):
                    d = hd[h]
                    pe.wait_ge(dve_steps.sem, dve_steps.count(f"s1{h}", i))
                    pe.matmul(psum[:, PB[h][2], P:2 * P], kS[:, P:2 * P], d["S"][:, 0, :], start=True, stop=True).then_inc(pe_steps.sem, pe_steps.step(f"ks1{h}"))
                for h in range(2):
                    d = hd[h]
                    pe.wait_ge(dve_steps.sem, dve_steps.count(f"r1{h}", i))
                    pe.matmul(psum[:, PB[h][2], 2 * P:3 * P], d["Y"][:, P:2 * P], d["R"][:, 1, :], start=True, stop=True).then_inc(pe_steps.sem, pe_steps.step(f"v1{h}"))
                for h in range(2):
                    d = hd[h]
                    pe.wait_ge(dve_steps.sem, dve_steps.count(f"vn1{h}", i))
                    pe.matmul(psum[:, PB[h][2], 3 * P:4 * P], d["kdec"][:, 1, :], d["vn"][:, 1, :], start=True, stop=True).then_inc(pe_steps.sem, pe_steps.step(f"s2{h}"))
                for h in range(2):
                    d, o = hd[h], psum[:, PB[h][0], :]
                    pe.matmul(o[:, 0:P], d["vn"][:, 0, :], d["qkd"][:, 0:P], start=True, stop=True)
                    pe.matmul(o[:, P:TP], d["vn"][:, 1, :], d["qkd"][:, P:TP], start=True, stop=False)
                    pe.matmul(o[:, P:TP], d["S"][:, 0, :], d["qd"][:, P:TP], start=False, stop=True)
                    pe.matmul(o[:, TP:T], d["vn"][0:TS, 2, :], d["qkd"][0:TS, TP:T], start=True, stop=True, skip_group_check=True)
                    for b in range(NB):
                        c = TP + b * TQ
                        last = pe.matmul(o[:, c:c + TQ], d["S0"][:, b, :], d["qd"][:, c:c + TQ], start=False, stop=True,
                                         skip_group_check=True)
                    last.then_inc(pe_steps.sem, pe_steps.step(f"o{h}"))
                for h in range(2):
                    d = hd[h]
                    pe.wait_ge(pool_steps.sem, pool_steps.count(f"spread{h}", i))
                    if h:
                        pe.wait_ge(dve_steps.sem, dve_steps.count("snew0", i))
                    for x in range(2):
                        last = pe.matmul(psum[:, x, :], d["kdec"][0:TS, 2, :],
                                         d["spread"][0:TS, 4 * x:4 * x + 4, :].rearrange("p a b -> p (a b)"), start=True, stop=True)
                    last.then_inc(pe_steps.sem, pe_steps.step(f"snew{h}"))

        def act_core(act):
            act_steps, dve_steps, pe_steps = S5["act"], S5["dve"], S5["pe"]
            new = outs["gdn_s_sample"].rearrange("l b h k v -> (l h) k b v")
            first = outs["gdn_s_prompt"].rearrange("l b h k v -> (l b h) k v")
            act.sem_inc(act_steps.sem, 1)
            act.sem_inc(state_out, 16)
            with act.Fori(0, QKH) as i:
                act.wait_ge(pe_steps.sem, pe_steps.all_before(i))
                act.copy(kS[:, 0:T], one(qkv[:, bass.ds(QKH + i, 1), :])).then_inc(act_steps.sem, act_steps.step("k"))
                act.copy(qS, one(qkv[:, bass.ds(i, 1), :])).then_inc(act_steps.sem, act_steps.step("q"))
                for h in range(2):
                    act.copy(hd[h]["v"][:, 0:T], one(qkv[:, bass.ds(2 * QKH + 2 * i + h, 1), :])).then_inc(act_steps.sem, act_steps.step(f"v{h}"))
                act.wait_ge(pe_steps.sem, pe_steps.count("ktok", i))
                act.copy(ktok, psum[:, 4, 0:W3].rearrange("p (u c) -> p u c", u=3)).then_inc(act_steps.sem, act_steps.step("ktok"))
                for h in range(2):
                    act.wait_ge(pe_steps.sem, pe_steps.count(f"rows{h}", i))
                    act.wait_ge(S5["pool"].sem, S5["pool"].all_before(i))
                    act.activation(hd[h]["egc"], psum[:, PB[h][0], 0:T], ACT.Exp).then_inc(act_steps.sem, act_steps.step(f"egc{h}"))
                for h in range(2):
                    act.wait_ge(dve_steps.sem, dve_steps.count(f"d{h}", i))
                    act.activation(hd[h]["dec"], hd[h]["dec"], ACT.Exp).then_inc(act_steps.sem, act_steps.step(f"dec{h}"))
                act.wait_ge(act_steps.sem, act_steps.count("ktok", i))
                for h in range(2):
                    for u in range(3):
                        last = act.activation(hd[h]["kdec"][:, u, :], ktok[:, u, :], ACT.Copy, scale=gtok[:, u, C_E, bass.ds(2 * i + h, 1)])
                    last.then_inc(act_steps.sem, act_steps.step(f"kdec{h}"))
                for h in range(2):
                    act.wait_ge(pe_steps.sem, pe_steps.count(f"vtok{h}", i))
                    for u in range(3):
                        r = P if u < 2 else TS
                        last = act.activation(hd[h]["R"][0:r, u, :], psum[0:r, PB[h][0], u * P:(u + 1) * P], ACT.Copy,
                                              scale=gtok[0:r, u, C_B, bass.ds(2 * i + h, 1)])
                    last.then_inc(act_steps.sem, act_steps.step(f"r{h}"))
                for h in range(2):
                    act.wait_ge(pe_steps.sem, pe_steps.count(f"o{h}", i))
                    act.copy(one(o_heads[:, bass.ds(2 * i + h, 1), :]), psum[:, PB[h][0], 0:T]).then_inc(act_steps.sem, act_steps.step(f"o{h}"))
                for h in range(2):
                    act.wait_ge(dve_steps.sem, dve_steps.count(f"snew{h}", i))
                    act.dma_start(new[bass.ds(2 * i + h, 1)].rearrange("o k b v -> (o k) b v"), hd[h]["S0"]).then_inc(state_out, 16)
                    act.dma_start(first[bass.ds(2 * i + h, 1)].rearrange("o k v -> (o k) v"), hd[h]["S"][:, 1, :]).then_inc(state_out, 16)

        def dve_core(dve):
            dve_steps, pe_steps, act_steps, pool_steps = S5["dve"], S5["pe"], S5["act"], S5["pool"]
            dve.sem_inc(dve_steps.sem, 1)
            dve.memset(kS[:, T:W3], 0.0).then_inc(pads, 1)
            for h in hd:
                for name in ("v", "at", "bts", "Y"):
                    dve.memset(h[name][:, T:W3], 0.0).then_inc(pads, 1)
            dve.wait_ge(pads, 9)
            w3 = lambda ap, w: ap[:, 0:w]
            col = lambda parts, u, c, i, h: gtok[0:parts, u, c, bass.ds(2 * i + h, 1)]
            with dve.Fori(0, QKH) as i:
                for h in range(2):
                    dve.wait_ge(pe_steps.sem, pe_steps.all_before(i))
                    dve.tensor_scalar(row_src[h], rows4[:, 0:2, :], ident[0:VH, bass.ds(2 * i + h, 1)], None, ALU.mult).then_inc(dve_steps.sem, dve_steps.step(f"row{h}"))
                for h in range(2):
                    dve.wait_ge(pe_steps.sem, pe_steps.count(f"rows{h}", i))
                    dve.tensor_tensor(hd[h]["bts"][:, 0:T], psum[:, PB[h][1], 0:T], const("strict3"), ALU.mult).then_inc(dve_steps.sem, dve_steps.step(f"bts{h}"))
                for h in range(2):
                    dve.wait_ge(act_steps.sem, act_steps.count(f"egc{h}", i))
                    for u, (c0, n) in enumerate(((0, P), (P, P), (TP, TS))):
                        last = dve.tensor_scalar(hd[h]["dec"][:, c0:c0 + n], psum[:, PB[h][0], c0:c0 + n], col(P, u, C_G, i, h), 0.0,
                                                 ALU.subtract, ALU.min)
                    last.then_inc(dve_steps.sem, dve_steps.step(f"d{h}"))
                for h in range(2):
                    dve.wait_ge(act_steps.sem, act_steps.count(f"dec{h}", i))
                    dve.tensor_tensor(hd[h]["dec"], hd[h]["dec"], const("causal3"), ALU.mult).then_inc(dve_steps.sem, dve_steps.step(f"cd{h}"))
                for h in range(2):
                    dve.wait_ge(dve_steps.sem, dve_steps.count(f"cd{h}", i))
                    dve.tensor_tensor(hd[h]["at"][:, 0:T], psum[:, 0, 0:T], hd[h]["dec"], ALU.mult).then_inc(dve_steps.sem, dve_steps.step(f"at1{h}"))
                for h in range(2):
                    dve.wait_ge(dve_steps.sem, dve_steps.count(f"at1{h}", i))
                    dve.tensor_tensor(hd[h]["at"][:, 0:T], hd[h]["at"][:, 0:T], hd[h]["bts"][:, 0:T], ALU.mult).then_inc(dve_steps.sem, dve_steps.step(f"at2{h}"))
                for h in range(2):
                    dve.tensor_tensor(hd[h]["qkd"], psum[:, 1, 0:T], hd[h]["dec"], ALU.mult).then_inc(dve_steps.sem, dve_steps.step(f"qkd{h}"))
                for h in range(2):
                    dve.wait_ge(act_steps.sem, act_steps.count(f"egc{h}", i))
                    dve.tensor_tensor(hd[h]["qd"], qS, hd[h]["egc"], ALU.mult).then_inc(dve_steps.sem, dve_steps.step(f"qd{h}"))
                for h in range(2):
                    dve.wait_ge(dve_steps.sem, dve_steps.count(f"qkd{h}", i))
                    dve.tensor_tensor(hd[h]["Y"][:, 0:T], hd[h]["at"][:, 0:T], const("level0T"), ALU.mult).then_inc(dve_steps.sem, dve_steps.step(f"ya{h}"))
                for h in range(2):
                    dve.wait_ge(dve_steps.sem, dve_steps.count(f"ya{h}", i))
                    dve.tensor_tensor(hd[h]["Y"][:, 0:T], const("eye3"), hd[h]["Y"][:, 0:T], ALU.subtract).then_inc(dve_steps.sem, dve_steps.step(f"yb{h}"))
                for h in range(2):
                    dve.wait_ge(pe_steps.sem, pe_steps.count(f"at{h}", i))
                    dve.tensor_tensor(hd[h]["X"], psum[:, PB[h][2], 0:T], const("level0"), ALU.mult).then_inc(dve_steps.sem, dve_steps.step(f"xa{h}"))
                for h in range(2):
                    dve.wait_ge(dve_steps.sem, dve_steps.count(f"xa{h}", i))
                    dve.tensor_tensor(hd[h]["X"], const("eye3"), hd[h]["X"], ALU.subtract).then_inc(dve_steps.sem, dve_steps.step(f"xb{h}"))
                for k in range(1, LEVELS):
                    n = width(k)
                    for h in range(2):
                        dve.wait_ge(pe_steps.sem, pe_steps.count(f"p{k}{h}", i))
                        if k < 3:
                            dve.tensor_tensor(hd[h]["P"][:, 0:n], psum[:, PB[h][0], 0:n], const(f"level{k}"), ALU.mult).then_inc(dve_steps.sem, dve_steps.step(f"p{k}{h}"))
                        else:
                            pair = lambda ap: ap.rearrange("p (a b) -> p a b", a=2)
                            dve.tensor_tensor(pair(hd[h]["P"][:, 0:n]), pair(psum[:, PB[h][0], 0:n]),
                                                     const(f"level{k}").unsqueeze(1).to_broadcast([P, 2, P]), ALU.mult).then_inc(dve_steps.sem, dve_steps.step(f"p{k}{h}"))
                    for x, nm, b in (("x", "X", 1), ("y", "Y", 2)):
                        if x == "x" and k == LEVELS - 1:
                            continue
                        for h in range(2):
                            dve.wait_ge(pe_steps.sem, pe_steps.count(f"{x}{k}{h}", i))
                            dve.tensor_tensor(hd[h][nm][:, 0:n], hd[h][nm][:, 0:n], psum[:, PB[h][b], 0:n], ALU.subtract).then_inc(dve_steps.sem, dve_steps.step(f"{x}{k}{h}"))
                for h in range(2):
                    dve.wait_ge(pe_steps.sem, pe_steps.count(f"ks{h}", i))
                    dve.wait_ge(act_steps.sem, act_steps.count(f"r{h}", i))
                    dve.scalar_tensor_tensor(out=hd[h]["R"][0:TS, 2, :], in0=psum[0:TS, PB[h][1], 0:P], scalar=col(TS, 2, C_N, i, h),
                                                    in1=hd[h]["R"][0:TS, 2, :], op0=ALU.mult, op1=ALU.add).then_inc(dve_steps.sem, dve_steps.step(f"rs{h}"))
                for h in range(2):
                    dve.wait_ge(pe_steps.sem, pe_steps.count(f"v0{h}", i))
                    dve.tensor_copy(hd[h]["vn"][:, 0, :], psum[:, PB[h][1], P:2 * P]).then_inc(dve_steps.sem, dve_steps.step(f"vn0{h}"))
                for h in range(2):
                    dve.tensor_copy(hd[h]["vn"][0:TS, 2, :], psum[0:TS, PB[h][1], 2 * P:3 * P]).then_inc(dve_steps.sem, dve_steps.step(f"vns{h}"))
                for h in range(2):
                    dve.wait_ge(pe_steps.sem, pe_steps.count(f"s1{h}", i))
                    dve.tensor_copy(hd[h]["S"][:, 0, :], psum[:, PB[h][2], 0:P]).then_inc(dve_steps.sem, dve_steps.step(f"s1{h}"))
                for h in range(2):
                    dve.wait_ge(pe_steps.sem, pe_steps.count(f"ks1{h}", i))
                    dve.scalar_tensor_tensor(out=hd[h]["R"][:, 1, :], in0=psum[:, PB[h][2], P:2 * P], scalar=col(P, 1, C_N, i, h),
                                                    in1=hd[h]["R"][:, 1, :], op0=ALU.mult, op1=ALU.add).then_inc(dve_steps.sem, dve_steps.step(f"r1{h}"))
                for h in range(2):
                    dve.wait_ge(pe_steps.sem, pe_steps.count(f"v1{h}", i))
                    dve.tensor_copy(hd[h]["vn"][:, 1, :], psum[:, PB[h][2], 2 * P:3 * P]).then_inc(dve_steps.sem, dve_steps.step(f"vn1{h}"))
                for h in range(2):
                    dve.wait_ge(pe_steps.sem, pe_steps.count(f"s2{h}", i))
                    dve.wait_ge(dve_steps.sem, dve_steps.count(f"s1{h}", i))
                    dve.wait_ge(state_out, STATES * i + 16)
                    dve.scalar_tensor_tensor(out=hd[h]["S"][:, 1, :], in0=hd[h]["S"][:, 0, :], scalar=hd[h]["egc"][:, TP - 1:TP],
                                                    in1=psum[:, PB[h][2], 3 * P:4 * P], op0=ALU.mult, op1=ALU.add).then_inc(dve_steps.sem, dve_steps.step(f"s2{h}"))
                for h in range(2):
                    dve.wait_ge(pe_steps.sem, pe_steps.count(f"snew{h}", i))
                    dve.wait_ge(pool_steps.sem, pool_steps.count(f"s0g{h}", i))
                    x = hd[h]["S0"].rearrange("p (x a) b -> p x (a b)", x=2)
                    dve.tensor_tensor(x, x, psum[:, 0:2, :], ALU.add).then_inc(dve_steps.sem, dve_steps.step(f"snew{h}"))

        def pool_core(pool):
            pool_steps, dve_steps, pe_steps, act_steps = S5["pool"], S5["dve"], S5["pe"], S5["act"]
            st = ins["state_gdn_s"].rearrange("l b h k v -> (l h) k b v")
            pool.sem_inc(pool_steps.sem, 1)
            with pool.Fori(0, QKH) as i:
                pool.wait_ge(state_out, STATES * i + 16)
                for h in range(2):
                    pool.dma_start(hd[h]["S0"], st[bass.ds(2 * i + h, 1)].rearrange("o k b v -> (o k) b v")).then_inc(state_in, 16)
                pool.wait_ge(act_steps.sem, act_steps.count("k", i))
                pool.tensor_tensor(kmask, const("col_seq").rearrange("p (b c) -> p b c", b=NB),
                                          kS[:, TP:T].unsqueeze(1).to_broadcast([P, NB, TS]), ALU.mult).then_inc(pool_steps.sem, pool_steps.step("kmask"))
                for h in range(2):
                    pool.wait_ge(pe_steps.sem, pe_steps.count(f"o{h}", i))
                    pool.tensor_tensor(hd[h]["S0"], hd[h]["S0"],
                                              hd[h]["egc"][:, TP + TQ - 1:T:TQ].unsqueeze(2).to_broadcast([P, NB, P]), ALU.mult).then_inc(pool_steps.sem, pool_steps.step(f"s0g{h}"))
                    pool.wait_ge(dve_steps.sem, dve_steps.count(f"vns{h}", i))
                    pool.tensor_tensor(hd[h]["spread"][0:TS], hd[h]["vn"][0:TS, 2, :].unsqueeze(1).to_broadcast([TS, NB, P]),
                                              const("tok_seq", TS).unsqueeze(2).to_broadcast([TS, NB, P]), ALU.mult).then_inc(pool_steps.sem, pool_steps.step(f"spread{h}"))
            pool.wait_ge(state_out, STATES * QKH + 16)

        space.at = scratch
        sq6 = space.take(4, T)
        inv6 = space.take(4, T)
        S6 = dict(pe=steps("gate_norm_pe", [f"sum{g}" for g in range(4)]),
                  act=steps("gate_norm_act", [f"{x}{g}" for g in range(4) for x in ("sq", "root")]),
                  dve=steps("gate_norm_dve", [f"{x}{g}" for g in range(4) for x in ("inv", "w", "out")]))

        o_hi = [rounded(f"gated_high{g}", o_heads[:, 4 * g:4 * g + 4, :]) for g in range(4)]
        o_lo = [rounded(f"gated_low{g}", z[:, 4 * g:4 * g + 4, :]) for g in range(4)]

        def act_gate_norm(act):
            for j in range(2):
                high_part(act, "gdn_out", 0, j, VH, free=True)
            for g in range(4):
                if g:
                    act.wait_ge(S6["pe"].sem, S6["pe"].count(f"sum{g - 1}"))
                act.activation(sq6, o_heads[:, 4 * g:4 * g + 4, :], ACT.Square).then_inc(S6["act"].sem, S6["act"].step(f"sq{g}"))
                if g:
                    act.wait_ge(S6["dve"].sem, S6["dve"].count(f"out{g - 1}"))
                    act.copy(o_hi[g - 1], z[:, 4 * g - 4:4 * g, :]).then_inc(x_hi, 1)
                act.wait_ge(S6["pe"].sem, S6["pe"].count(f"sum{g}"))
                act.activation(inv6, psum[:, 0:4, 0:T], ACT.Sqrt, bias=eps_col, scale=1.0 / DK).then_inc(
                    S6["act"].sem, S6["act"].step(f"root{g}"))
            act.wait_ge(S6["dve"].sem, S6["dve"].count("out3"))
            act.copy(o_hi[3], z[:, 12:16, :]).then_inc(x_hi, 1)
            for j in range(2, 8):
                high_part(act, "gdn_out", 0, j, VH)

        def pe_gate_norm(pe):
            for g in range(4):
                pe.wait_ge(S6["act"].sem, S6["act"].count(f"sq{g}"))
                if g:
                    pe.wait_ge(S6["act"].sem, S6["act"].count(f"root{g - 1}"))
                for j in range(4):
                    last = pe.matmul(psum[:, j, 0:T], ones, sq6[:, j, :], start=True, stop=True)
                last.then_inc(S6["pe"].sem, S6["pe"].step(f"sum{g}"))

        def dve_gate_norm(dve):
            dve_steps = S6["dve"]
            for g in range(4):
                dve.wait_ge(S6["act"].sem, S6["act"].count(f"root{g}"))
                dve.reciprocal(inv6, inv6).then_inc(dve_steps.sem, dve_steps.step(f"inv{g}"))
                dve.wait_ge(dve_steps.sem, dve_steps.count(f"inv{g}"))
                t = o_heads[:, 4 * g:4 * g + 4, :]
                dve.scalar_tensor_tensor(out=t, in0=t, scalar=out_norm, in1=inv6, op0=ALU.mult, op1=ALU.mult).then_inc(
                    dve_steps.sem, dve_steps.step(f"w{g}"))
                dve.wait_ge(dve_steps.sem, dve_steps.count(f"w{g}"))
                gate = z[:, 4 * g:4 * g + 4, :]
                dve.tensor_tensor(gate, t, gate, ALU.mult).then_inc(dve_steps.sem, dve_steps.step(f"out{g}"))

        def pool_gate_norm(pool):
            for j in range(2):
                low_part(pool, "gdn_out", 0, j, VH)
            for g in range(4):
                pool.wait_ge(x_hi, SPLITS["gdn_out"][0] + g + 1)
                pool.tensor_tensor(o_lo[g], z[:, 4 * g:4 * g + 4, :], o_hi[g], ALU.subtract).then_inc(x_lo, 1)
            for j in range(2, 8):
                low_part(pool, "gdn_out", 0, j, VH)

        def pe_add(pe, name, high, low, kn):
            w0, n = UNITS[name]
            pe.wait_ge(x_lo, split_count(name))
            with pe.Fori(0, n // 4) as i:
                for j in range(4):
                    multiply_unit(pe, name, i, j, single_tile(kn), high, low, kn, lanes=(1,))

        def dve_add(dve, name):
            w0, n = UNITS[name]
            with dve.Fori(0, n // 4) as i:
                for j in range(4):
                    dve.wait_ge(unit_done, product_count(name, i, j, 1))
                    x = one(xT[:, bass.ds(4 * i + j, 1), :])
                    dve.tensor_tensor(x, x, bank(name, j, 1)[:, 0:T], ALU.add).then_inc(lane_free[1], 1)

        def ffn_up(l):
            name = f"ffn_up{l}"
            space.at = phase
            hid = space.take(NFT, T)
            rows = space.take(FF, parts=18)
            sil = [space.take(T) for _ in range(2)]
            x_low = space.take(KD, T)
            hid_hi = space.take(NFT, T, off=phase + NFT * T + FF)
            assert phase + 2 * NFT * T + FF <= wide_at
            parts = [(0, 6), (6, 12), (12, 17), (17, NFT)]
            low_rounded = rounded(f"h_low_ffn{l}", x_low)
            hidden_lo = [rounded(f"hidden{l}_low{a}", hid[:, a:b, :]) for a, b in parts]
            hidden_hi = [rounded(f"hidden{l}_high{a}", hid_hi[:, a:b, :]) for a, b in parts]
            part_of = [(n, k - a) for n, (a, b) in enumerate(parts) for k in range(a, b)]
            in_parts = lambda tensors: lambda k: tensors[part_of[k][0]][:, part_of[k][1], :]
            nt = NB * FP + FP
            s = dict(pe=steps(f"ffn{l}_tails_turned", ["tails"]),
                     act=steps(f"ffn{l}_silu", [f"silu{j}" for j in range(4)] + ["rows"], loop=True),
                     dve=steps(f"ffn{l}_conv", [x for j in range(4) for x in conv_steps(f"{j}", FP)]))
            full, rest = NFT // 4, NFT % 4

            def tile(sl, k, lane):
                return sl[:, 0:KD * 256].rearrange("p (k g n) -> p k g n", k=KD, g=2)[:, k, lane, :]

            def source(n, sl):
                v = ins["ffn_w_up"][l].rearrange("(k p) (g n) -> p k g n", p=P, g=2)
                dst = sl[:, 0:KD * 256].rearrange("p (k g n) -> p k g n", k=KD, g=2)
                return [(dst[:, :, g, :], v[:, :, g, bass.ds(n * P, P)]) for g in range(2)]

            def pe(eng):
                eng.wait_ge(x_lo, split_count(name))

                def body(i, n):
                    for j in range(n):
                        multiply_unit(eng, name, i, j, tile, h_high, lambda k: low_rounded[:, k, :], KD)
                    eng.wait_ge(lane_free[0], read_count(name, i, n - 1, 0))
                    eng.wait_ge(s["act"].sem, s["act"].all_before(i))
                    for j in range(n):
                        last = eng.transpose(psum[0:nt, 4, j * P:(j + 1) * P], tails[:, j, 0:nt], ident)
                    last.then_inc(s["pe"].sem, 1)
                with eng.Fori(0, full) as i:
                    body(i, 4)
                body(full, rest)

            def act(eng):
                eng.sem_inc(s["act"].sem, 1)

                def body(i, n):
                    def silu(j):
                        eng.wait_ge(s["dve"].sem, s["dve"].count(f"{j}t{FP}s", i))
                        if j >= 2:
                            eng.wait_ge(lane_free[1], read_count(name, i, j - 2, 1))
                        else:
                            eng.wait_ge(lane_free[1], lane_before[1][name] + 4 * i + j + 1)
                        eng.activation(sil[j % 2], conv_y[j % 2], ACT.Silu).then_inc(s["act"].sem, 1)
                    for j in range(n):
                        eng.wait_ge(half_done, product_count(name, i, j, 0))
                        if n == 4:
                            high_part(eng, name, i, j + 2, KD * 2, free=True)
                        state = fconv[l][:, bass.ds(4 * i + j, 1), 0:NB * FP].rearrange("p o (b c) -> p (o b) c", b=NB)
                        last = take_in(eng, bank(name, j, 0), xpf[j % 2], tails[:, j, :], state, FP)
                        last.then_inc(lane_free[0], 1)
                        if j:
                            silu(j - 1)
                    silu(n - 1)
                    eng.wait_ge(s["pe"].sem, i + 1)
                    eng.copy(rows[:, bass.ds(512 * i, n * P)], psum[0:nt, 4, 0:n * P]).then_inc(s["act"].sem, 1)
                with eng.Fori(0, full) as i:
                    body(i, 4)
                body(full, rest)

            def dve(eng):
                def body(i, n):
                    def product(j):
                        eng.wait_ge(s["act"].sem, s["act"].all_before(i, j + 1))
                        eng.wait_ge(unit_done, product_count(name, i, j, 1))
                        eng.tensor_tensor(one(hid[:, bass.ds(4 * i + j, 1), :]), sil[j % 2], bank(name, j, 1)[:, 0:T],
                                          ALU.mult).then_inc(lane_free[1], 1)
                    for j in range(n):
                        eng.wait_ge(lane_free[0], read_count(name, i, j, 0))
                        if j >= 2:
                            eng.wait_ge(s["act"].sem, s["act"].all_before(i, j - 1))
                        else:
                            eng.wait_ge(s["act"].sem, s["act"].all_before(i))
                        conv(eng, s["dve"], i, f"{j}", xpf[j % 2], conv_y[j % 2],
                             lambda t: one(fconv[l][:, bass.ds(4 * i + j, 1), NB * FP + t:NB * FP + t + 1]), FP)
                        if j:
                            product(j - 1)
                    product(n - 1)
                with eng.Fori(0, full) as i:
                    body(i, 4)
                body(full, rest)

            def pool(eng):
                low_parts(eng, name, KD * 2)
                eng.wait_ge(s["act"].sem, s["act"].all_before(full, rest + 1))
                eng.dma_start(outs["ffn_conv_prompt"][l].rearrange("b w c -> (b w) c"), rows[0:FP, :]).then_inc(stored, 16)
                eng.dma_start(outs["ffn_conv_sample"][l].rearrange("b w c -> (b w) c"), rows[FP:nt, :]).then_inc(stored, 16)
                n_stored[0] += 2

            down = f"ffn_down{l}"

            def act_down(act):
                high_part(act, down, 0, 0, NFT, free=True)
                for n, (a, b) in enumerate(parts):
                    act.copy(hidden_hi[n], hid[:, a:b, :]).then_inc(x_hi, 1)
                for j in range(1, 8):
                    high_part(act, down, 0, j, NFT)

            def dve_down(dve):
                for n, (a, b) in enumerate(parts):
                    dve.wait_ge(x_hi, SPLITS[down][0] + n + 1)
                    dve.tensor_tensor(hidden_lo[n], hid[:, a:b, :], hidden_hi[n], ALU.subtract).then_inc(x_lo, 1)
                dve_add(dve, down)

            def pool_down(pool):
                low_parts(pool, down, NFT)
                pool.wait_ge(stored, 16 * n_stored[0])

            def pe_down(pe):
                pe_add(pe, down, in_parts(hidden_hi), in_parts(hidden_lo), NFT)
            return dict(pe=pe, act=act, dve=dve, pool=pool, source=source, low=lambda k: x_low[:, k, :],
                        low_rounded=lambda k: low_rounded[:, k, :],
                        act_down=act_down, dve_down=dve_down, pool_down=pool_down, pe_down=pe_down)

        def nsa_stages():
            space.at = phase
            n_tab = sum(n for at, n in where.values() if at >= base_cols)
            att = space.take(n_tab)

            def table(name, *dims):
                at, n = where[name]
                ap = att[:, at - base_cols:at - base_cols + n]
                if dims:
                    ap = ap.rearrange("p (a b) -> p a b", a=dims[0])
                return ap

            w2 = space.take(4, DH)
            pe_bias = space.take(4)
            ckT = space.take(2, NB * NCMP)
            cv = space.take(NB, KV_DIM, parts=NCMP)
            ckT_p = space.take(2, PCMP)
            cv_p = space.take(KV_DIM, parts=PCMP)
            past_projection = space.at
            att_in, w1_in = sem("attention_tables_in"), sem("w1_in")
            raw_in = [sem("raw_keys_in"), sem("raw_values_in")]

            w1 = space.take(2, 16, CHID)
            raw = [space.take(STRIDE, KV_DIM) for _ in range(2)]
            turned = space.take(8, 4 * P)
            NC2 = 2 * NCMP
            hid = space.take(2, 4 * NC2, off=xpg_at)
            C = dict(
                pe=steps("cmp_pe", [x for v in range(2) for x in [f"t{v}{m}" for m in range(8)] + [f"h{v}0", f"h{v}1", f"o{v}"]], lag=True),
                dve=steps("cmp_dve", [x for v in range(2) for x in [f"t{v}{m}" for m in range(0, 8, 2)]] + ["k", "v"], loop=True),
                act=steps("cmp_act", [x for v in range(2) for x in [f"t{v}{m}" for m in range(1, 8, 2)] + [f"h{v}0", f"h{v}1"]], loop=True))
            bias_pe, bias_dve = sem("pe_bias_product"), sem("pe_bias_copied")
            kv_pages = ins["cache_nsa_kv"].rearrange("l g (n s) c j d -> (l g) n s (c j d)", s=STRIDE)

            def load_w1(pool):
                for v in range(2):
                    pool.dma_start(w1[:, v], ins["nsa_cmp_w1"][0, v].rearrange("s d h -> (s d) h").rearrange("(c p) h -> p c h", p=P)).then_inc(w1_in, 16)

            def pool_cmp(pool):
                pool.dma_start(att, ins["tables"][:, base_cols:base_cols + n_tab]).then_inc(att_in, 16)
                pool.dma_start(w2, ins["nsa_cmp_w2"][0].rearrange("v (t p) d -> p (v t) d", p=P)).then_inc(att_in, 16)
                load_w1(pool)
                with pool.Fori(0, NB // 2) as i:
                    for v in range(2):
                        pool.wait_ge(C["pe"].sem, C["pe"].count(f"t{v}7", i - 1))
                        for n in range(2 * NPG):
                            page = pool.value_load(pages_sb[0:1, bass.ds(2 * NPG * i + NB * NPG * v + n, 1)], min_val=0, max_val=NPOOL - 1)
                            src = kv_pages[bass.ds(page, 1)].rearrange("o n s c -> (o n) s c")[:, :, v * KV_DIM:(v + 1) * KV_DIM]
                            pool.dma_start(raw[v][8 * n:8 * n + 8], src).then_inc(raw_in[v], 16)

            def hidden_products(pe, v, t, out, rhs):
                for half in range(2):
                    for m in range(8):
                        last = pe.matmul(out, w1[:, v, 8 * half + m, t * P:(t + 1) * P], rhs(m, half),
                                         start=(half == 0 and m == 0), stop=(half == 1 and m == 7))
                return last

            def pe_cmp(pe):
                pe_steps, dve_steps, act_steps = C["pe"], C["dve"], C["act"]
                pe.sem_inc(pe_steps.sem, pe_steps.first)
                pe.wait_ge(w1_in, 32)
                for v in range(2):
                    for t in range(2):
                        for c in range(16):
                            last = pe.matmul(psum[:, 7, 2 * v + t:2 * v + t + 1], w1[:, v, c, t * P:(t + 1) * P], embed[:, 16 * v + c:16 * v + c + 1],
                                             start=(c == 0), stop=(c == 15))
                last.then_inc(bias_pe, 1)
                pe.wait_ge(bias_dve, 1)
                pe.wait_ge(att_in, 32)
                with pe.Fori(0, NB // 2) as i:
                    for v in range(2):
                        pe.wait_ge(raw_in[v], 256 * (i + 1))
                        for m in range(8):
                            if m >= 4:
                                pe.wait_ge((dve_steps if m % 2 == 0 else act_steps).sem, (dve_steps if m % 2 == 0 else act_steps).count(f"t{v}{m - 4}", i))
                            elif v:
                                pe.wait_ge((dve_steps if m % 2 == 0 else act_steps).sem, (dve_steps if m % 2 == 0 else act_steps).count(f"t{v - 1}{m + 4}", i))
                            else:
                                pe.wait_ge((dve_steps if m % 2 == 0 else act_steps).sem, (dve_steps if m % 2 == 0 else act_steps).all_before(i))
                            for j in range(4):
                                c0 = (j % 2) * P
                                last = pe.transpose(psum[:, m % 4, j * P:(j + 1) * P], raw[v][:, 2 * m + j // 2, c0:c0 + P], ident)
                            last.then_inc(pe_steps.sem, pe_steps.step(f"t{v}{m}"))
                        pe.wait_ge(dve_steps.sem, dve_steps.count(f"t{v}6", i))
                        pe.wait_ge(act_steps.sem, act_steps.count(f"t{v}7", i))
                        blocks = lambda m, half: turned[:, m, :].rearrange("p (x n) -> p x n", x=8)[:, :, half:half + NCMP]
                        for t in range(2):
                            if v:
                                pe.wait_ge(act_steps.sem, act_steps.count(f"h{v - 1}{t}", i))
                            hidden_products(pe, v, t, psum[:, 4 + t, 0:4 * NC2], blocks).then_inc(pe_steps.sem, pe_steps.step(f"h{v}{t}"))
                        pe.wait_ge(act_steps.sem, act_steps.count(f"h{v}1", i))
                        pe.wait_ge(dve_steps.sem, dve_steps.all_before(i))
                        for g in range(4):
                            for t in range(2):
                                if v == 0:
                                    h0 = 64 * (g % 2)
                                    last = pe.matmul(psum[h0:h0 + DH, 6, (g // 2) * NC2:(g // 2 + 1) * NC2], w2[:, t, :],
                                                     hid[:, t, g * NC2:(g + 1) * NC2], start=(t == 0), stop=(t == 1))
                        if v == 1:
                            for b in range(2):
                                for g in range(4):
                                    for t in range(2):
                                        c0 = g * NC2 + b * NCMP
                                        last = pe.matmul(psum[0:NCMP, 7, b * KV_DIM + g * DH:b * KV_DIM + (g + 1) * DH], hid[:, t, c0:c0 + NCMP],
                                                         w2[:, 2 + t, :], start=(t == 0), stop=(t == 1))
                        last.then_inc(pe_steps.sem, pe_steps.step(f"o{v}"))

            def copy_batches(eng, kind, v, i):
                own, pe_steps = C[kind], C["pe"]
                for m in range(8):
                    if m % 2 == (kind == "act"):
                        eng.wait_ge(pe_steps.sem, pe_steps.count(f"t{v}{m}", i))
                        if v:
                            eng.wait_ge(pe_steps.sem, pe_steps.count("h01", i))
                        for s2 in range(2):
                            for g2 in range(2):
                                src = psum[64 * g2:64 * g2 + DH, m % 4, 256 * s2:256 * (s2 + 1)].rearrange("p (a b) -> p a b", a=2)
                                dst = turned[64 * s2:64 * s2 + DH, m, :].rearrange("p (a g b) -> p a g b", a=2, g=2)[:, :, g2, :]
                                last = (eng.tensor_copy if kind == "dve" else eng.copy)(dst, src)
                        last.then_inc(own.sem, own.step(f"t{v}{m}"))

            def dve_cmp(dve):
                dve_steps, pe_steps = C["dve"], C["pe"]
                dve.sem_inc(dve_steps.sem, 1)
                dve.wait_ge(bias_pe, 1)
                dve.tensor_copy(pe_bias, psum[:, 7, 0:4]).then_inc(bias_dve, 1)
                with dve.Fori(0, NB // 2) as i:
                    for v in range(2):
                        copy_batches(dve, "dve", v, i)
                    dve.wait_ge(pe_steps.sem, pe_steps.count("o0", i))
                    dve.tensor_copy(ckT[:, :, bass.ds(NC2 * i, NC2)], psum[:, 6, 0:2 * NC2].rearrange("p (a b) -> p a b", a=2)).then_inc(dve_steps.sem, dve_steps.step("k"))
                    dve.wait_ge(pe_steps.sem, pe_steps.count("o1", i))
                    dve.tensor_copy(cv[:, bass.ds(2 * i, 2), :], psum[0:NCMP, 7, :].rearrange("p (a b) -> p a b", a=2)).then_inc(dve_steps.sem, dve_steps.step("v"))

            def act_cmp(act):
                act_steps, pe_steps = C["act"], C["pe"]
                act.sem_inc(act_steps.sem, 1)
                act.wait_ge(bias_dve, 1)
                with act.Fori(0, NB // 2) as i:
                    for v in range(2):
                        copy_batches(act, "act", v, i)
                        for t in range(2):
                            act.wait_ge(pe_steps.sem, pe_steps.count(f"h{v}{t}", i))
                            if v:
                                act.wait_ge(pe_steps.sem, pe_steps.count("o0", i))
                            act.activation(hid[:, t, :], psum[:, 4 + t, 0:4 * NC2], ACT.Silu, bias=pe_bias[:, 2 * v + t:2 * v + t + 1]).then_inc(act_steps.sem, act_steps.step(f"h{v}{t}"))

            space.at = past_projection
            gates48 = space.take(T, parts=3 * HEADS)
            w_gate = space.take(KD, 3 * HEADS)
            gate_p = space.take(3, 3 * HEADS)
            gate_wide = space.take(NB, 3 * HEADS, parts=TS)
            gate_pick = space.take(NB, 3 * HEADS)
            gate_s = space.take(NB, 3)
            qT = space.take(8, T)
            kvT = space.take(12, T)
            rows_s = space.take(NKV * KV_DIM, parts=TS)
            after_rows_s = space.at
            rows_p = space.take(2, NKV * KV_DIM)
            work = space.at
            x_low = space.take(KD, T, off=after_rows_s)
            w_gate_hi = space.take(KD, 3 * HEADS, off=after_rows_s + KD * T)
            assert after_rows_s + KD * (T + 3 * HEADS) <= hi_at
            low_rounded = rounded("h_low_nsa", x_low)
            w_gate_lo, w_gate_hi = rounded("w_gate_low", w_gate), rounded("w_gate_high", w_gate_hi)
            out_hi = rounded("o_high", space.take(KD, T, off=after_rows_s))
            gate_done, wg_in, gate_split = sem("gates_product"), sem("gate_columns_in"), sem("gate_columns_split")
            K_SEL, V_SEL, K_WIN, V_WIN = (slice(x * KV_DIM, (x + 1) * KV_DIM) for x in (2, 3, 4, 5))

            def stream_in(sp):
                w0 = UNITS["nsa_in"][0]
                w = ins["nsa_w_in"][0].rearrange("(k p) n -> p k n", p=P)
                for n in range(10):
                    sp.wait_ge(unit_done, w0 + n - RING + 1)
                    sl = slot(w0 + n)[:, 0:KD * 256]
                    if n < 4:
                        c0 = (n // 2) * 512 + (n % 2) * P
                        views = [(sl.rearrange("p (k r h d) -> p k r h d", k=KD, r=2, h=2)[:, :, r, h, :],
                                  w[:, :, c0 + 256 * h + DH * r:c0 + 256 * h + DH * (r + 1)]) for h in range(2) for r in range(2)]
                    else:
                        c0 = Q_DIM + (n - 4) * 256
                        views = [(sl.rearrange("p (k n) -> p k n", k=KD)[:, h:h + 4, :], w[:, h:h + 4, c0:c0 + 256]) for h in (0, 4)]
                    for dst, src in views:
                        sp.dma_start(dst, src).then_inc(w_in[(w0 + n) % RING], 16)

            def pe_in(pe):
                pe.wait_ge(x_lo, split_count("nsa_in"))
                for n in range(10):
                    multiply_unit(pe, "nsa_in", n // 4, n % 4, pair_tile, h_high, lambda k: low_rounded[:, k, :], KD)
                pe.wait_ge(gate_split, 2)
                for k in range(KD):
                    last = three_products(pe, psum[0:3 * HEADS, 6, 0:T], w_gate_hi[:, k, :], w_gate_lo[:, k, :], h_high(k), low_rounded[:, k, :],
                                          k == 0, k == KD - 1)
                last.then_inc(gate_done, 1)

            def act_in(act):
                act.wait_ge(wg_in, 16)
                act.copy(w_gate_hi, w_gate).then_inc(gate_split, 1)
                for n in range(10):
                    for l in range(2):
                        act.wait_ge(tile_done[l], product_count("nsa_in", n // 4, n % 4, l))
                        if l == 0 and n + 2 < 10:
                            high_part(act, "nsa_in", 0, n + 2, KD * 2, free=True)
                        src = bank("nsa_in", n % 4, l)[:, 0:T]
                        if n < 4:
                            ins_ = act.activation(qT[:, 2 * n + l, :], src, ACT.Copy, scale=float(DH) ** -0.5)
                        else:
                            ins_ = act.copy(kvT[:, 2 * (n - 4) + l, :], src)
                        ins_.then_inc(lane_free[l], 1)

            def pool_in(pool):
                pool.dma_start(w_gate, ins["nsa_w_in"][0].rearrange("(k p) n -> p k n", p=P)[:, :, Q_DIM + NKV * KV_DIM:]).then_inc(wg_in, 16)
                low_parts(pool, "nsa_in", KD * 2)
                pool.wait_ge(gate_split, 1)
                pool.tensor_tensor(w_gate_lo, w_gate, w_gate_hi, ALU.subtract).then_inc(gate_split, 1)


            space.at = work
            w1_again = space.take(2, 16, CHID)
            sub = space.take(2, 8, 4 * PSUB)
            hid_p = space.take(2, 2 * 4 * PCMP, off=xpg_at)
            groups = [(tb, rows, q) for tb, rows in ((0, P), (1, P), (2, TS)) for q in range(3)]
            R = dict(pe=steps("rows_pe", [f"g{n}" for n in range(9)] + ["gt", "gw", "hk", "hv", "ok", "ov"]),
                     dve=steps("rows_dve", ["g0", "g2", "g4", "g6", "g8", "den", "gate", "gtok", "gwide", "gpick", "gsum"]
                               + [f"sub{n}" for n in range(8)] + ["k", "v"]),
                     act=steps("rows_act", ["g1", "g3", "g5", "g7", "gexp"] + [f"sub{n}" for n in range(8)] + ["hk", "hv"]))
            same_q = table("same_q")

            def rows_dst(tb, rows, q):
                return (rows_p[:, tb, 512 * q:512 * (q + 1)] if tb < 2 else rows_s[:, 512 * q:512 * (q + 1)])

            def pe_rows(pe):
                pe_steps, dve_steps, act_steps = R["pe"], R["dve"], R["act"]
                for n, (tb, rows, q) in enumerate(groups):
                    if n >= 4:
                        pe.wait_ge((dve_steps if n % 2 == 0 else act_steps).sem, (dve_steps if n % 2 == 0 else act_steps).count(f"g{n - 4}"))
                    for j in range(4):
                        last = pe.transpose(psum[0:rows, n % 4, j * P:(j + 1) * P], kvT[:, 4 * q + j, tb * P:tb * P + rows], ident)
                    last.then_inc(pe_steps.sem, pe_steps.step(f"g{n}"))
                pe.wait_ge(dve_steps.sem, dve_steps.count("gate"))
                for tb, rows in ((0, P), (1, P), (2, TS)):
                    last = pe.transpose(psum[0:rows, 4, tb * 48:(tb + 1) * 48], gates48[:, tb * P:tb * P + rows], ident[0:48, 0:48])
                last.then_inc(pe_steps.sem, pe_steps.step("gt"))
                pe.wait_ge(dve_steps.sem, dve_steps.count("gwide"))
                pe.matmul(psum[:, 5, 0:NB * 48], same_q[0:TS, :], gate_wide.rearrange("p b c -> p (b c)"), start=True, stop=True).then_inc(pe_steps.sem, pe_steps.step("gw"))
                pe.wait_ge(w1_in, 64)
                pe.wait_ge(dve_steps.sem, dve_steps.count("sub7"))
                pe.wait_ge(act_steps.sem, act_steps.count("sub7"))
                for kv, name in enumerate(("hk", "hv")):
                    for t in range(2):
                        blocks = lambda m, half: sub[:, kv, m, :].rearrange("p (x n) -> p x n", x=4)[:, :, half:half + PCMP]
                        last = hidden_products_again(pe, kv, t, psum[:, 6 + kv, t * 60:(t + 1) * 60], blocks)
                    last.then_inc(pe_steps.sem, pe_steps.step(name))
                pe.wait_ge(act_steps.sem, act_steps.count("hk"))
                for g in range(4):
                    for t in range(2):
                        h0 = 64 * (g % 2)
                        last = pe.matmul(psum[h0:h0 + DH, 0, (g // 2) * PCMP:(g // 2 + 1) * PCMP], w2[:, t, :],
                                         hid_p[:, 0, t * 60 + g * PCMP:t * 60 + (g + 1) * PCMP], start=(t == 0), stop=(t == 1))
                last.then_inc(pe_steps.sem, pe_steps.step("ok"))
                pe.wait_ge(act_steps.sem, act_steps.count("hv"))
                for g in range(4):
                    for t in range(2):
                        last = pe.matmul(psum[0:PCMP, 1, g * DH:(g + 1) * DH], hid_p[:, 1, t * 60 + g * PCMP:t * 60 + (g + 1) * PCMP],
                                         w2[:, 2 + t, :], start=(t == 0), stop=(t == 1))
                last.then_inc(pe_steps.sem, pe_steps.step("ov"))

            def hidden_products_again(pe, v, t, out, rhs):
                for half in range(2):
                    for m in range(8):
                        last = pe.matmul(out, w1_again[:, v, 8 * half + m, t * P:(t + 1) * P], rhs(m, half),
                                         start=(half == 0 and m == 0), stop=(half == 1 and m == 7))
                return last

            def sub_copies(eng, kind):
                n = 0
                for kv in range(2):
                    for g in range(4):
                        for s2 in range(2):
                            if s2 == (kind == "act"):
                                src = kvT[64 * (g % 2):64 * (g % 2) + DH, 2 * kv + g // 2, 0:TP].rearrange("p (n m s) -> p m n s", m=8, s=2)[:, :, :, s2]
                                dst = sub[64 * s2:64 * s2 + DH, kv, :, g * PSUB:(g + 1) * PSUB]
                                (eng.tensor_copy if kind == "dve" else eng.copy)(dst, src).then_inc(R[kind].sem, R[kind].step(f"sub{n}"))
                                n += 1

            def act_rows(act):
                act_steps, pe_steps = R["act"], R["pe"]
                for n, (tb, rows, q) in enumerate(groups):
                    if n % 2:
                        act.wait_ge(pe_steps.sem, pe_steps.count(f"g{n}"))
                        act.copy(rows_dst(tb, rows, q), psum[0:rows, n % 4, :]).then_inc(act_steps.sem, act_steps.step(f"g{n}"))
                act.wait_ge(gate_done, 1)
                act.activation(gates48, psum[0:48, 6, 0:T], ACT.Exp, scale=-1.0).then_inc(act_steps.sem, act_steps.step("gexp"))
                sub_copies(act, "act")
                for kv, name in enumerate(("hk", "hv")):
                    act.wait_ge(pe_steps.sem, pe_steps.count(name))
                    for t in range(2):
                        last = act.activation(hid_p[:, kv, t * 60:(t + 1) * 60], psum[:, 6 + kv, t * 60:(t + 1) * 60], ACT.Silu,
                                              bias=pe_bias[:, 2 * kv + t:2 * kv + t + 1])
                    last.then_inc(act_steps.sem, act_steps.step(name))

            def dve_rows(dve):
                dve_steps, pe_steps, act_steps = R["dve"], R["pe"], R["act"]
                for n, (tb, rows, q) in enumerate(groups):
                    if n % 2 == 0:
                        dve.wait_ge(pe_steps.sem, pe_steps.count(f"g{n}"))
                        dve.tensor_copy(rows_dst(tb, rows, q), psum[0:rows, n % 4, :]).then_inc(dve_steps.sem, dve_steps.step(f"g{n}"))
                dve.wait_ge(act_steps.sem, act_steps.count("gexp"))
                dve.tensor_scalar(gates48, gates48, 1.0, None, ALU.add).then_inc(dve_steps.sem, dve_steps.step("den"))
                dve.wait_ge(dve_steps.sem, dve_steps.count("den"))
                dve.reciprocal(gates48, gates48).then_inc(dve_steps.sem, dve_steps.step("gate"))
                dve.wait_ge(pe_steps.sem, pe_steps.count("gt"))
                gt = psum[:, 4, 0:3 * 48].rearrange("p (a b) -> p a b", a=3)
                dve.tensor_copy(gate_p[:, 0:2, :], gt[:, 0:2, :])
                dve.tensor_copy(gate_p[0:TS, 2, :], gt[0:TS, 2, :]).then_inc(dve_steps.sem, dve_steps.step("gtok"))
                dve.wait_ge(dve_steps.sem, dve_steps.count("gtok"))
                dve.tensor_tensor(gate_wide, gate_p[0:TS, 2, :].unsqueeze(1).to_broadcast([TS, NB, 48]),
                                         const("tok_seq", TS).unsqueeze(2).to_broadcast([TS, NB, 48]), ALU.mult).then_inc(dve_steps.sem, dve_steps.step("gwide"))
                dve.wait_ge(pe_steps.sem, pe_steps.count("gw"))
                dve.tensor_tensor(gate_pick, psum[:, 5, 0:NB * 48].rearrange("p (b c) -> p b c", b=NB),
                                         table("own_head").unsqueeze(1).to_broadcast([P, NB, 48]), ALU.mult).then_inc(dve_steps.sem, dve_steps.step("gpick"))
                dve.wait_ge(dve_steps.sem, dve_steps.count("gpick"))
                dve.tensor_reduce(gate_s, gate_pick.rearrange("p b (h c) -> p b c h", c=3), AX.X, ALU.add).then_inc(dve_steps.sem, dve_steps.step("gsum"))
                sub_copies(dve, "dve")
                dve.wait_ge(pe_steps.sem, pe_steps.count("ok"))
                dve.tensor_copy(ckT_p, psum[:, 0, 0:2 * PCMP].rearrange("p (a b) -> p a b", a=2)).then_inc(dve_steps.sem, dve_steps.step("k"))
                dve.wait_ge(pe_steps.sem, pe_steps.count("ov"))
                dve.tensor_copy(cv_p, psum[0:PCMP, 1, 0:KV_DIM]).then_inc(dve_steps.sem, dve_steps.step("v"))

            def pool_rows(pool):
                for v in range(2):
                    pool.dma_start(w1_again[:, v], ins["nsa_cmp_w1"][0, v].rearrange("s d h -> (s d) h").rearrange("(c p) h -> p c h", p=P)).then_inc(w1_in, 16)
                pool.wait_ge(R["dve"].sem, R["dve"].count("g8"))
                pool.wait_ge(R["act"].sem, R["act"].count("g7"))
                kvp = outs["kv_rows_prompt"].rearrange("l b (t p) c g d -> p (l b t) (c g d)", p=P)
                wp = outs["win_prompt"].rearrange("l b (t p) c g d -> p (l b t) (c g d)", p=P)
                pool.dma_start(kvp, rows_p[:, :, 0:4 * KV_DIM]).then_inc(stored, 16)
                pool.dma_start(wp, rows_p[:, :, 4 * KV_DIM:]).then_inc(stored, 16)
                pool.dma_start(outs["kv_rows_sample"].rearrange("l b q c g d -> (l b q) (c g d)"), rows_s[:, 0:4 * KV_DIM]).then_inc(stored, 16)
                for b in range(NB):
                    pool.dma_start(outs["win_sample"][0, b].rearrange("w c g d -> w (c g d)")[WIN - TQ:, :],
                                   rows_s[b * TQ:(b + 1) * TQ, 4 * KV_DIM:]).then_inc(stored, 16)
                n_stored[0] += 11

            space.at = work
            o_tok = space.take(2, Q_DIM)
            qs = space.take(TP)
            hs = [dict(s0=space.take(2, P), s1=space.take(2, TP), sc=space.take(2, PCMP), mx=space.take(2, 3), sm=space.take(2, 3),
                       c=space.take(2, 3), p0=space.take(2 * P), pc=space.take(2 * P, parts=PCMP), p1=space.take(4 * P)) for _ in range(2)]
            B2 = lambda names: [f"{x}{h}" for x in names for h in range(2)]
            A = dict(pe=steps("prompt_pe", B2(["s"]) + B2(["t"]) + B2(["o"]), loop=True),
                     dve=steps("prompt_dve", B2(["s0", "sc", "s1", "m0", "mc", "m1", "pc", "inv", "c", "p0", "o0", "o1", "o2"])),
                     act=steps("prompt_act", ["q"] + B2(["e", "p1"])))
            AO = dict(pe=steps("prompt_out_pe", [f"g{n}" for n in range(4)]),
                      dve=steps("prompt_out_dve", ["g0", "g2"]), act=steps("prompt_out_act", ["g1", "g3"]))

            def pe_prompt(pe):
                pe_steps, dve_steps, act_steps = A["pe"], A["dve"], A["act"]
                pe.sem_inc(pe_steps.sem, 1)
                for gp in range(2):
                    with pe.Fori(4 * gp, 4 * gp + 4) as i:
                        pe.wait_ge(act_steps.sem, act_steps.count("q", i))
                        for h in range(2):
                            lo = slice(64 * h, 64 * h + DH)
                            b0, b1 = psum[:, 3 * h, :], psum[:, 3 * h + 1, :]
                            q0, q1 = qs[lo, 0:P], qs[lo, P:TP]
                            ks, kw, kc = kvT[lo, 4 + gp, :], kvT[lo, 8 + gp, :], ckT_p[lo, gp, :]
                            pe.matmul(b0[:, 0:P], q0, ks[:, 0:P], start=True, stop=True)
                            pe.matmul(b0[:, P:2 * P], q0, kw[:, 0:P], start=True, stop=True)
                            pe.matmul(b0[:, 256:256 + PCMP], q0, kc, start=True, stop=True)
                            pe.matmul(b0[:, 272:272 + PCMP], q1, kc, start=True, stop=True)
                            pe.matmul(b1[:, 0:TP], q1, ks[:, 0:TP], start=True, stop=True)
                            pe.matmul(b1[:, TP:2 * TP], q1, kw[:, 0:TP], start=True, stop=True).then_inc(pe_steps.sem, pe_steps.step(f"s{h}"))
                        for h in range(2):
                            d = hs[h]
                            b0, b1 = psum[:, 3 * h, :], psum[:, 3 * h + 1, :]
                            pe.wait_ge(act_steps.sem, act_steps.count(f"e{h}", i))
                            pe.wait_ge(dve_steps.sem, dve_steps.count(f"pc{h}", i))
                            for x in range(2):
                                pe.transpose(b0[:, x * P:(x + 1) * P], d["s0"][:, x, :], ident)
                                pe.transpose(b0[0:PCMP, (2 + x) * P:(3 + x) * P], d["sc"][:, x, :], ident)
                                for y in range(2):
                                    last = pe.transpose(b1[:, (2 * x + y) * P:(2 * x + y + 1) * P], d["s1"][:, x, y * P:(y + 1) * P], ident)
                            last.then_inc(pe_steps.sem, pe_steps.step(f"t{h}"))
                        for h in range(2):
                            d, g = hs[h], 2 * gp + h
                            pe.wait_ge(dve_steps.sem, dve_steps.count(f"p0{h}", i))
                            pe.wait_ge(act_steps.sem, act_steps.count(f"p1{h}", i))
                            o = psum[:, 3 * h + 2, 0:384].rearrange("p (t b d) -> p t b d", t=2, b=3)
                            cols = lambda x: slice(x.start + g * DH, x.start + (g + 1) * DH)
                            for t in range(2):
                                pe.matmul(o[:, t, 0, :], d["pc"][:, t * P:(t + 1) * P], cv_p[:, g * DH:(g + 1) * DH], start=True, stop=True)
                            for x, vc in ((0, V_SEL), (1, V_WIN)):
                                pe.matmul(o[:, 0, 1 + x, :], d["p0"][:, x * P:(x + 1) * P], rows_p[:, 0, cols(vc)], start=True, stop=True)
                                for y in range(2):
                                    last = pe.matmul(o[:, 1, 1 + x, :], d["p1"][:, (2 * x + y) * P:(2 * x + y + 1) * P], rows_p[:, y, cols(vc)],
                                                     start=(y == 0), stop=(y == 1))
                            last.then_inc(pe_steps.sem, pe_steps.step(f"o{h}"))

            def act_prompt(act):
                act_steps, dve_steps, pe_steps = A["act"], A["dve"], A["pe"]
                for gp in range(2):
                    with act.Fori(4 * gp, 4 * gp + 4) as i:
                        act.wait_ge(pe_steps.sem, pe_steps.all_before(i))
                        act.copy(qs, one(qT[:, bass.ds(i, 1), 0:TP])).then_inc(act_steps.sem, act_steps.step("q"))
                        for h in range(2):
                            d = hs[h]
                            act.wait_ge(dve_steps.sem, dve_steps.count(f"m1{h}", i))
                            for x in range(2):
                                act.activation(d["s0"][:, x, :], d["s0"][:, x, :], ACT.Exp, bias=d["mx"][:, 0, 1 + x:2 + x], accum_out=d["sm"][:, 0, 1 + x:2 + x])
                                act.activation(d["sc"][:, x, :], d["sc"][:, x, :], ACT.Exp, bias=d["mx"][:, x, 0:1], accum_out=d["sm"][:, x, 0:1])
                                last = act.activation(d["s1"][:, x, :], d["s1"][:, x, :], ACT.Exp, bias=d["mx"][:, 1, 1 + x:2 + x], accum_out=d["sm"][:, 1, 1 + x:2 + x])
                            last.then_inc(act_steps.sem, act_steps.step(f"e{h}"))
                        for h in range(2):
                            act.wait_ge(pe_steps.sem, pe_steps.count(f"t{h}", i))
                            act.copy(hs[h]["p1"], psum[:, 3 * h + 1, :]).then_inc(act_steps.sem, act_steps.step(f"p1{h}"))

            def dve_prompt(dve):
                dve_steps, pe_steps, act_steps = A["dve"], A["pe"], A["act"]
                dve.wait_ge(att_in, 32)
                for gp in range(2):
                    with dve.Fori(4 * gp, 4 * gp + 4) as i:
                        for h in range(2):
                            d = hs[h]
                            slope = table("slopes")[:, bass.ds(i + 4 * gp + 4 * h, 1)]
                            b0 = psum[:, 3 * h, :]
                            dve.wait_ge(pe_steps.sem, pe_steps.count(f"s{h}", i))
                            dve.scalar_tensor_tensor(out=d["s0"], in0=table("dist0").unsqueeze(1).to_broadcast([P, 2, P]), scalar=slope,
                                                            in1=b0[:, 0:256].rearrange("p (a b) -> p a b", a=2), op0=ALU.mult, op1=ALU.add).then_inc(dve_steps.sem, dve_steps.step(f"s0{h}"))
                        for h in range(2):
                            d = hs[h]
                            slope = table("slopes")[:, bass.ds(i + 4 * gp + 4 * h, 1)]
                            dve.scalar_tensor_tensor(out=d["sc"], in0=table("cdist", 2), scalar=slope,
                                                            in1=psum[:, 3 * h, 256:288].rearrange("p (a b) -> p a b", a=2)[:, :, 0:PCMP], op0=ALU.mult, op1=ALU.add).then_inc(dve_steps.sem, dve_steps.step(f"sc{h}"))
                        for h in range(2):
                            d = hs[h]
                            slope = table("slopes")[:, bass.ds(i + 4 * gp + 4 * h, 1)]
                            dve.scalar_tensor_tensor(out=d["s1"], in0=table("dist1").unsqueeze(1).to_broadcast([P, 2, TP]), scalar=slope,
                                                            in1=psum[:, 3 * h + 1, :].rearrange("p (a b) -> p a b", a=2), op0=ALU.mult, op1=ALU.add).then_inc(dve_steps.sem, dve_steps.step(f"s1{h}"))
                        for h in range(2):
                            dve.wait_ge(dve_steps.sem, dve_steps.count(f"s0{h}", i))
                            dve.tensor_reduce(hs[h]["mx"][:, 0, 1:3], hs[h]["s0"], AX.X, ALU.max, negate=True).then_inc(dve_steps.sem, dve_steps.step(f"m0{h}"))
                        for h in range(2):
                            dve.wait_ge(dve_steps.sem, dve_steps.count(f"sc{h}", i))
                            dve.tensor_reduce(hs[h]["mx"][:, :, 0], hs[h]["sc"], AX.X, ALU.max, negate=True).then_inc(dve_steps.sem, dve_steps.step(f"mc{h}"))
                        for h in range(2):
                            dve.wait_ge(dve_steps.sem, dve_steps.count(f"s1{h}", i))
                            dve.tensor_reduce(hs[h]["mx"][:, 1, 1:3], hs[h]["s1"], AX.X, ALU.max, negate=True).then_inc(dve_steps.sem, dve_steps.step(f"m1{h}"))
                        for h in range(2):
                            dve.wait_ge(act_steps.sem, act_steps.count(f"e{h}", i))
                            dve.tensor_tensor(hs[h]["sc"], hs[h]["sc"], table("cvalid", 2), ALU.mult).then_inc(dve_steps.sem, dve_steps.step(f"pc{h}"))
                        for h in range(2):
                            dve.reciprocal(hs[h]["sm"], hs[h]["sm"]).then_inc(dve_steps.sem, dve_steps.step(f"inv{h}"))
                        for h in range(2):
                            dve.wait_ge(dve_steps.sem, dve_steps.count(f"inv{h}", i))
                            dve.tensor_tensor(hs[h]["c"], hs[h]["sm"], gate_p[:, 0:2, bass.ds(3 * i + 12 * gp + 12 * h, 3)], ALU.mult).then_inc(dve_steps.sem, dve_steps.step(f"c{h}"))
                        for h in range(2):
                            dve.wait_ge(pe_steps.sem, pe_steps.count(f"t{h}", i))
                            dve.tensor_copy(hs[h]["p0"], psum[:, 3 * h, 0:256])
                            dve.tensor_copy(hs[h]["pc"], psum[0:PCMP, 3 * h, 256:512]).then_inc(dve_steps.sem, dve_steps.step(f"p0{h}"))
                        for br in range(3):
                            for h in range(2):
                                if br == 0:
                                    dve.wait_ge(pe_steps.sem, pe_steps.count(f"o{h}", i))
                                    dve.wait_ge(dve_steps.sem, dve_steps.count(f"c{h}", i))
                                else:
                                    dve.wait_ge(dve_steps.sem, dve_steps.count(f"o{br - 1}{h}", i))
                                for t in range(2):
                                    src = psum[:, 3 * h + 2, 0:384].rearrange("p (t b d) -> p t b d", t=2, b=3)[:, t, br, :]
                                    dst = o_tok[:, t, bass.ds(DH * i + 256 * gp + 256 * h, DH)]
                                    c = hs[h]["c"][:, t, br:br + 1]
                                    if br == 0:
                                        last = dve.tensor_scalar(dst, src, c, None, ALU.mult)
                                    else:
                                        last = dve.scalar_tensor_tensor(out=dst, in0=src, scalar=c, in1=dst, op0=ALU.mult, op1=ALU.add)
                                last.then_inc(dve_steps.sem, dve_steps.step(f"o{br}{h}"))

            out_blocks = [(tb, half) for tb in range(2) for half in range(2)]

            def pe_prompt_out(pe):
                for n, (tb, half) in enumerate(out_blocks):
                    for j in range(4):
                        c0 = (4 * half + j) * P
                        last = pe.transpose(psum[:, n, j * P:(j + 1) * P], o_tok[:, tb, c0:c0 + P], ident)
                    last.then_inc(AO["pe"].sem, AO["pe"].step(f"g{n}"))

            def prompt_out(eng, kind):
                for n, (tb, half) in enumerate(out_blocks):
                    if n % 2 == (kind == "act"):
                        eng.wait_ge(AO["pe"].sem, AO["pe"].count(f"g{n}"))
                        (eng.tensor_copy if kind == "dve" else eng.copy)(
                            hT[:, 4 * half:4 * half + 4, tb * P:(tb + 1) * P], psum[:, n, :].rearrange("p (a b) -> p a b", a=4)).then_inc(AO[kind].sem, AO[kind].step(f"g{n}"))

            space.at = after_rows_s
            k_sel = space.take(NPG, KV_DIM)
            v_sel = space.take(NPG, KV_DIM)
            k_win = space.take(WIN // P, KV_DIM)
            v_win = space.take(WIN // P, KV_DIM)
            kT = space.take(2, PAST)
            kTw = space.take(2, WIN, off=xpg_at)
            q2 = space.take(2, P)
            ss = space.take(PAST + TS)
            sw = space.take(WIN + TS)
            sc_wide = space.take(P)
            sc = sc_wide[:, 0:NCMP]
            mx, sm, cc = space.take(3), space.take(3), space.take(3)
            imp_r, imp, rank, pen = (space.take(FREE_BLKS) for _ in range(4))
            pcT = space.take(P, parts=NCMP)
            cmpg = space.take(FREE_BLKS, FREE_BLKS, off=space.at)
            cmpe = space.take(FREE_BLKS, FREE_BLKS, off=space.at + FREE_BLKS ** 2)
            pT = space.take(12, P)
            pTn = space.take(2 * P, parts=TS)
            o_wide = space.take(P)
            o_s = o_wide[:, 0:DH]
            assert space.at <= size
            F = dict(
                pe=steps("sample_pe", [f"t{n}" for n in range(6)] + ["cmp", "sel", "win", "pc", "ir", "is", "ptw", "pts", "ptn", "o", "ot"], lag=True),
                dve=steps("sample_dve", ["t0", "t2", "t4", "scmp", "mcmp", "icmp", "pcmp", "pc", "swin", "swn", "mwin", "ssel", "ssn",
                                         "ir", "is", "gt", "eq", "eqe", "gte", "rank", "pen", "spen", "msel", "pts1", "ptn", "inv", "c",
                                         "o0", "o1", "o2", "oT0", "oT1"], loop=True),
                act=steps("sample_act", ["q", "t1", "t3", "t5", "ecmp", "ewin", "ptw", "esel", "pts0"]))
            k_in, v_in, k_out, zeroed = sem("sample_k_in"), sem("sample_v_in"), sem("window_stored"), sem("q2_zeroed")
            kv_rows = ins["cache_nsa_kv"].rearrange("l g s c j d -> (l g) s (c j d)")
            win_rows = ins["cache_nsa_win"].rearrange("l b (t p) c j d -> (l b) p t (c j d)", p=P)
            win_out = outs["win_sample"].rearrange("l b w c j d -> (l b) w (c j d)")

            def store_window(eng, i, c0, src):
                dst = win_out[bass.ds(i, 1)].rearrange("o w c -> (o w) c")[:, c0:c0 + KV_DIM]
                eng.dma_start(dst[0:P - TQ, :], src[TQ:P, 0, :]).then_inc(k_out, 16)
                eng.dma_start(dst[P - TQ:WIN - TQ, :].rearrange("(t p) c -> p t c", p=P), src[:, 1:, :]).then_inc(k_out, 16)

            def pool_sample(pool):
                with pool.Fori(0, NB) as i:
                    pool.wait_ge(F["pe"].sem, F["pe"].count("t5", i - 1))
                    pool.wait_ge(k_out, 64 * i + 16)
                    pages = [pool.value_load(pages_sb[0:1, bass.ds(NPG * i + g, 1)], min_val=0, max_val=NPOOL - 1) for g in range(NPG)]
                    for g in range(NPG):
                        src = kv_rows[bass.ds(pages[g], 1)].rearrange("o s c -> (o s) c")
                        pool.dma_start(k_sel[:, g, :], src[:, K_SEL]).then_inc(k_in, 16)
                    w = win_rows[bass.ds(i, 1)].rearrange("o p t c -> (o p) t c")
                    pool.dma_start(k_win, w[:, :, 0:KV_DIM]).then_inc(k_in, 16)
                    pool.wait_ge(F["pe"].sem, F["pe"].count("o", i - 1))
                    for g in range(NPG):
                        page = pool.value_load(pages_sb[0:1, bass.ds(NPG * i + NB * NPG + g, 1)], min_val=0, max_val=NPOOL - 1)
                        src = kv_rows[bass.ds(page, 1)].rearrange("o s c -> (o s) c")
                        pool.dma_start(v_sel[:, g, :], src[:, V_SEL]).then_inc(v_in, 16)
                    pool.dma_start(v_win, w[:, :, KV_DIM:]).then_inc(v_in, 16)
                pool.wait_ge(k_out, 64 * NB + 16)

            def pe_sample(pe):
                pe_steps, dve_steps, act_steps = F["pe"], F["dve"], F["act"]
                pe.sem_inc(pe_steps.sem, pe_steps.first)
                pe.wait_ge(zeroed, 3)
                with pe.Fori(0, NB) as i:
                    pe.wait_ge(dve_steps.sem, dve_steps.all_before(i))
                    pe.wait_ge(k_in, 144 * (i + 1))
                    for n in range(6):
                        gp = n % 2
                        for j in range(4):
                            src = k_sel[:, 4 * (n // 2) + j, :] if n < 4 else k_win[:, j, :]
                            last = pe.transpose(psum[:, n, j * P:(j + 1) * P], src[:, gp * P:(gp + 1) * P], ident)
                        last.then_inc(pe_steps.sem, pe_steps.step(f"t{n}"))
                    pe.wait_ge(act_steps.sem, act_steps.count("q", i))
                    for c0, k in ((0, lambda gp: ckT[:, gp, bass.ds(NCMP * i, NCMP)]), (64, lambda gp: kvT[:, 4 + gp, TP:T]),
                                  (128, lambda gp: kvT[:, 8 + gp, TP:T])):
                        for gp in range(2):
                            last = pe.matmul(psum[:, 7, c0:c0 + (TS if c0 else NCMP)], q2[:, gp, :], k(gp), start=(gp == 0), stop=(gp == 1))
                    last.then_inc(pe_steps.sem, pe_steps.step("cmp"))
                    pe.wait_ge(dve_steps.sem, dve_steps.count("t4", i))
                    pe.wait_ge(act_steps.sem, act_steps.count("t5", i))
                    for x in range(2):
                        for gp in range(2):
                            last = pe.matmul(psum[:, x, :], q2[:, gp, :], kT[:, gp, x * 512:(x + 1) * 512], start=(gp == 0), stop=(gp == 1))
                    last.then_inc(pe_steps.sem, pe_steps.step("sel"))
                    for gp in range(2):
                        last = pe.matmul(psum[:, 2, :], q2[:, gp, :], kTw[:, gp, :], start=(gp == 0), stop=(gp == 1))
                    last.then_inc(pe_steps.sem, pe_steps.step("win"))
                    pe.wait_ge(dve_steps.sem, dve_steps.count("pcmp", i))
                    pe.transpose(psum[:, 3, 0:P], sc_wide, ident).then_inc(pe_steps.sem, pe_steps.step("pc"))
                    pe.wait_ge(dve_steps.sem, dve_steps.count("pc", i))
                    pe.matmul(psum[:, 4, 0:FREE_BLKS], pcT, table("overlap")[0:NCMP, :], start=True, stop=True).then_inc(pe_steps.sem, pe_steps.step("ir"))
                    pe.wait_ge(dve_steps.sem, dve_steps.count("ir", i))
                    pe.matmul(psum[:, 5, 0:FREE_BLKS], table("group_sum"), imp_r, start=True, stop=True).then_inc(pe_steps.sem, pe_steps.step("is"))
                    pe.wait_ge(act_steps.sem, act_steps.count("ewin", i))
                    for j in range(4):
                        last = pe.transpose(psum[:, 2, j * P:(j + 1) * P], sw[:, j * P:(j + 1) * P], ident)
                    last.then_inc(pe_steps.sem, pe_steps.step("ptw"))
                    pe.wait_ge(act_steps.sem, act_steps.count("esel", i))
                    for j in range(8):
                        last = pe.transpose(psum[:, j // 4, (j % 4) * P:(j % 4 + 1) * P], ss[:, j * P:(j + 1) * P], ident)
                    last.then_inc(pe_steps.sem, pe_steps.step("pts"))
                    pe.transpose(psum[0:TS, 3, 0:P], ss[:, PAST:], ident)
                    pe.transpose(psum[0:TS, 3, P:2 * P], sw[:, WIN:], ident).then_inc(pe_steps.sem, pe_steps.step("ptn"))
                    pe.wait_ge(v_in, 144 * (i + 1))
                    pe.matmul(psum[:, 5, 0:KV_DIM], pcT, cv[:, bass.ds(i, 1), :].rearrange("p o c -> p (o c)"), start=True, stop=True)
                    pe.wait_ge(act_steps.sem, act_steps.count("ptw", i))
                    pe.wait_ge(dve_steps.sem, dve_steps.count("ptn", i))
                    for j in range(4):
                        pe.matmul(psum[:, 6, KV_DIM:], pT[:, 8 + j, :], v_win[:, j, :], start=(j == 0), stop=False)
                    pe.matmul(psum[:, 6, KV_DIM:], pTn[:, P:], rows_s[:, V_WIN], start=False, stop=True)
                    pe.wait_ge(act_steps.sem, act_steps.count("pts0", i))
                    for j in range(8):
                        pe.matmul(psum[:, 6, 0:KV_DIM], pT[:, j, :], v_sel[:, j, :], start=(j == 0), stop=False)
                    pe.matmul(psum[:, 6, 0:KV_DIM], pTn[:, 0:P], rows_s[:, V_SEL], start=False, stop=True).then_inc(pe_steps.sem, pe_steps.step("o"))
                    pe.wait_ge(dve_steps.sem, dve_steps.count("o2", i))
                    pe.transpose(psum[:, 7, 0:P], o_wide, ident).then_inc(pe_steps.sem, pe_steps.step("ot"))

            def act_sample(act):
                act_steps, dve_steps, pe_steps = F["act"], F["dve"], F["pe"]
                act.sem_inc(k_out, 16)
                act.wait_ge(zeroed, 3)
                with act.Fori(0, NB) as i:
                    act.wait_ge(pe_steps.sem, pe_steps.all_before(i))
                    for h in range(2):
                        lo = slice(64 * h, 64 * h + 64)
                        for gp in range(2):
                            last = act.copy(q2[lo, gp, 64 * gp + 32 * h:64 * gp + 32 * h + 32].rearrange("p (r q) -> p r q", r=4), qT[lo, 4 * gp:4 * gp + 4, bass.ds(TP + TQ * i, TQ)])
                    last.then_inc(act_steps.sem, act_steps.step("q"))
                    for n in (1, 3, 5):
                        act.wait_ge(pe_steps.sem, pe_steps.count(f"t{n}", i))
                        dst = kT[:, 1, 512 * (n // 2):512 * (n // 2 + 1)] if n < 4 else kTw[:, 1, :]
                        act.copy(dst, psum[:, n, :]).then_inc(act_steps.sem, act_steps.step(f"t{n}"))
                    act.wait_ge(dve_steps.sem, dve_steps.count("mcmp", i))
                    act.activation(sc, sc, ACT.Exp, bias=mx[:, 0:1], accum_out=sm[:, 0:1]).then_inc(act_steps.sem, act_steps.step("ecmp"))
                    act.wait_ge(dve_steps.sem, dve_steps.count("mwin", i))
                    act.activation(sw, sw, ACT.Exp, bias=mx[:, 2:3], accum_out=sm[:, 2:3]).then_inc(act_steps.sem, act_steps.step("ewin"))
                    act.wait_ge(k_in, 144 * (i + 1))
                    act.wait_ge(v_in, 144 * (i + 1))
                    store_window(act, i, 0, k_win)
                    store_window(act, i, KV_DIM, v_win)
                    act.wait_ge(pe_steps.sem, pe_steps.count("ptw", i))
                    act.copy(pT[:, 8:12, :], psum[:, 2, :].rearrange("p (a b) -> p a b", a=4)).then_inc(act_steps.sem, act_steps.step("ptw"))
                    act.wait_ge(dve_steps.sem, dve_steps.count("msel", i))
                    act.activation(ss, ss, ACT.Exp, bias=mx[:, 1:2], accum_out=sm[:, 1:2]).then_inc(act_steps.sem, act_steps.step("esel"))
                    act.wait_ge(pe_steps.sem, pe_steps.count("pts", i))
                    act.copy(pT[:, 0:4, :], psum[:, 0, :].rearrange("p (a b) -> p a b", a=4)).then_inc(act_steps.sem, act_steps.step("pts0"))

            def dve_sample(dve):
                dve_steps, pe_steps, act_steps = F["dve"], F["pe"], F["act"]
                dve.sem_inc(dve_steps.sem, 1)
                for t in (q2, sc_wide, o_wide):
                    dve.memset(t, 0.0).then_inc(zeroed, 1)
                dve.wait_ge(zeroed, 3)
                n14 = FREE_BLKS
                with dve.Fori(0, NB) as i:
                    for n in (0, 2, 4):
                        dve.wait_ge(pe_steps.sem, pe_steps.count(f"t{n}", i))
                        dst = kT[:, 0, 512 * (n // 2):512 * (n // 2 + 1)] if n < 4 else kTw[:, 0, :]
                        dve.tensor_copy(dst, psum[:, n, :]).then_inc(dve_steps.sem, dve_steps.step(f"t{n}"))
                    dve.wait_ge(pe_steps.sem, pe_steps.count("cmp", i))
                    dve.tensor_tensor(sc, psum[:, 7, 0:NCMP], table("bias_cmp"), ALU.add).then_inc(dve_steps.sem, dve_steps.step("scmp"))
                    dve.wait_ge(dve_steps.sem, dve_steps.count("scmp", i))
                    dve.tensor_reduce(mx[:, 0:1], sc, AX.X, ALU.max, negate=True).then_inc(dve_steps.sem, dve_steps.step("mcmp"))
                    dve.wait_ge(act_steps.sem, act_steps.count("ecmp", i))
                    dve.reciprocal(sm[:, 0:1], sm[:, 0:1]).then_inc(dve_steps.sem, dve_steps.step("icmp"))
                    dve.wait_ge(dve_steps.sem, dve_steps.count("icmp", i))
                    dve.tensor_scalar(sc, sc, sm[:, 0:1], None, ALU.mult).then_inc(dve_steps.sem, dve_steps.step("pcmp"))
                    dve.wait_ge(pe_steps.sem, pe_steps.count("pc", i))
                    dve.tensor_copy(pcT, psum[0:NCMP, 3, 0:P]).then_inc(dve_steps.sem, dve_steps.step("pc"))
                    new = one(table("bias_new", NB)[:, bass.ds(i, 1), :])
                    dve.wait_ge(pe_steps.sem, pe_steps.count("win", i))
                    dve.tensor_tensor(sw[:, 0:WIN], psum[:, 2, :], table("bias_win"), ALU.add).then_inc(dve_steps.sem, dve_steps.step("swin"))
                    dve.tensor_tensor(sw[:, WIN:], psum[:, 7, 128:128 + TS], new, ALU.add).then_inc(dve_steps.sem, dve_steps.step("swn"))
                    dve.wait_ge(dve_steps.sem, dve_steps.count("swn", i))
                    dve.tensor_reduce(mx[:, 2:3], sw, AX.X, ALU.max, negate=True).then_inc(dve_steps.sem, dve_steps.step("mwin"))
                    dve.tensor_tensor(ss[:, 0:PAST].rearrange("p (a b) -> p a b", a=2), psum[:, 0:2, :], table("bias_sel", 2), ALU.add).then_inc(dve_steps.sem, dve_steps.step("ssel"))
                    dve.tensor_tensor(ss[:, PAST:], psum[:, 7, 64:64 + TS], new, ALU.add).then_inc(dve_steps.sem, dve_steps.step("ssn"))
                    dve.wait_ge(pe_steps.sem, pe_steps.count("ir", i))
                    dve.tensor_copy(imp_r, psum[:, 4, 0:n14]).then_inc(dve_steps.sem, dve_steps.step("ir"))
                    dve.wait_ge(pe_steps.sem, pe_steps.count("is", i))
                    dve.tensor_copy(imp, psum[:, 5, 0:n14]).then_inc(dve_steps.sem, dve_steps.step("is"))
                    dve.wait_ge(dve_steps.sem, dve_steps.count("is", i))
                    other = imp.unsqueeze(1).to_broadcast([P, n14, n14])
                    this = imp.unsqueeze(2).to_broadcast([P, n14, n14])
                    dve.tensor_tensor(cmpg, other, this, ALU.is_gt).then_inc(dve_steps.sem, dve_steps.step("gt"))
                    dve.tensor_tensor(cmpe, other, this, ALU.is_equal).then_inc(dve_steps.sem, dve_steps.step("eq"))
                    dve.wait_ge(dve_steps.sem, dve_steps.count("eq", i))
                    dve.tensor_tensor(cmpe, cmpe, table("earlier", n14), ALU.mult).then_inc(dve_steps.sem, dve_steps.step("eqe"))
                    dve.wait_ge(dve_steps.sem, dve_steps.count("eqe", i))
                    dve.tensor_tensor(cmpg, cmpg, cmpe, ALU.add).then_inc(dve_steps.sem, dve_steps.step("gte"))
                    dve.wait_ge(dve_steps.sem, dve_steps.count("gte", i))
                    dve.tensor_reduce(rank, cmpg, AX.X, ALU.add).then_inc(dve_steps.sem, dve_steps.step("rank"))
                    dve.wait_ge(dve_steps.sem, dve_steps.count("rank", i))
                    dve.tensor_scalar(pen, rank, FREE_TOP - 0.5, MASKED, ALU.is_ge, ALU.mult).then_inc(dve_steps.sem, dve_steps.step("pen"))
                    dve.wait_ge(dve_steps.sem, dve_steps.count("pen", i))
                    blocks = ss[:, SELB:SELB * (1 + n14)].rearrange("p (a b) -> p a b", a=n14)
                    dve.tensor_tensor(blocks, blocks, pen.unsqueeze(2).to_broadcast([P, n14, SELB]), ALU.add).then_inc(dve_steps.sem, dve_steps.step("spen"))
                    dve.wait_ge(dve_steps.sem, dve_steps.count("spen", i))
                    dve.tensor_reduce(mx[:, 1:2], ss, AX.X, ALU.max, negate=True).then_inc(dve_steps.sem, dve_steps.step("msel"))
                    dve.wait_ge(pe_steps.sem, pe_steps.count("pts", i))
                    dve.tensor_copy(pT[:, 4:8, :], psum[:, 1, :].rearrange("p (a b) -> p a b", a=4)).then_inc(dve_steps.sem, dve_steps.step("pts1"))
                    dve.wait_ge(pe_steps.sem, pe_steps.count("ptn", i))
                    dve.tensor_copy(pTn, psum[0:TS, 3, 0:2 * P]).then_inc(dve_steps.sem, dve_steps.step("ptn"))
                    dve.wait_ge(act_steps.sem, act_steps.count("esel", i))
                    dve.reciprocal(sm[:, 1:3], sm[:, 1:3]).then_inc(dve_steps.sem, dve_steps.step("inv"))
                    dve.wait_ge(dve_steps.sem, dve_steps.count("inv", i))
                    gate = one(gate_s[:, bass.ds(i, 1), :])
                    dve.tensor_copy(cc[:, 0:1], gate[:, 0:1])
                    dve.tensor_tensor(cc[:, 1:3], sm[:, 1:3], gate[:, 1:3], ALU.mult).then_inc(dve_steps.sem, dve_steps.step("c"))
                    dve.wait_ge(pe_steps.sem, pe_steps.count("o", i))
                    dve.wait_ge(dve_steps.sem, dve_steps.count("c", i))
                    for br, (b, c0) in enumerate(((5, 0), (6, 0), (6, KV_DIM))):
                        if br:
                            dve.wait_ge(dve_steps.sem, dve_steps.count(f"o{br - 1}", i))
                        for g in range(4):
                            r = slice(32 * g, 32 * g + 32)
                            src = psum[r, b, c0 + g * DH:c0 + (g + 1) * DH]
                            if br == 0:
                                last = dve.tensor_scalar(o_s[r, :], src, cc[r, 0:1], None, ALU.mult)
                            else:
                                last = dve.scalar_tensor_tensor(out=o_s[r, :], in0=src, scalar=cc[r, br:br + 1], in1=o_s[r, :], op0=ALU.mult, op1=ALU.add)
                        last.then_inc(dve_steps.sem, dve_steps.step(f"o{br}"))
                    dve.wait_ge(pe_steps.sem, pe_steps.count("ot", i))
                    ot = psum[0:DH, 7, 0:P].rearrange("p (t e q) -> p t e q", t=8, e=2)
                    for e in range(2):
                        dve.tensor_copy(hT[64 * e:64 * e + DH, :, bass.ds(TP + TQ * i, TQ)], ot[:, :, e, :]).then_inc(dve_steps.sem, dve_steps.step(f"oT{e}"))

            def act_out(act):
                act.copy(out_hi, hT).then_inc(x_hi, 1)
                for n in range(4):
                    high_part(act, "nsa_out", 0, n, KD * 2)

            def pool_out(pool):
                low_parts(pool, "nsa_out", KD * 2)

            def pe_out(pe):
                pe.wait_ge(x_lo, split_count("nsa_out"))
                for n in range(4):
                    multiply_unit(pe, "nsa_out", 0, n, pair_tile, lambda k: out_hi[:, k, :], h_high, KD)

            def dve_out(dve):
                for xp in xpg:
                    dve.memset(xp[:, 0:GP], 0.0)
                dve.wait_ge(x_hi, split_count("nsa_out"))
                dve.tensor_tensor(hT_rounded, hT, out_hi, ALU.subtract).then_inc(x_lo, 1)
                for n in range(4):
                    for l in range(2):
                        dve.wait_ge(tile_done[l], product_count("nsa_out", 0, n, l))
                        x = xT[:, 2 * n + l, :]
                        dve.tensor_tensor(x, x, bank("nsa_out", n, l)[:, 0:T], ALU.add).then_inc(lane_free[l], 1)

            return dict(stream_in=stream_in, low=lambda k: x_low[:, k, :], low_rounded=lambda k: low_rounded[:, k, :],
                        pe=(pe_cmp, pe_in, pe_rows, pe_prompt, pe_prompt_out, pe_sample, pe_out),
                        act=(act_cmp, act_in, act_rows, act_prompt, lambda e: prompt_out(e, "act"), act_sample, act_out),
                        dve=(dve_cmp, dve_rows, dve_prompt, lambda e: prompt_out(e, "dve"), dve_sample, dve_out),
                        pool=(pool_cmp, pool_in, pool_rows, pool_sample, pool_out))

        def final_stage():
            space.at = phase
            y = space.take(3, D)
            blocks = [(tb, rows, half) for tb, rows in ((0, P), (1, P), (2, TS)) for half in range(2)]
            s = dict(pe=steps("y_turned", [f"g{n}" for n in range(6)]),
                     dve=steps("y_copied_dve", ["g0", "g2", "g4"]), act=steps("y_copied_act", ["g1", "g3", "g5"]))

            def pe(eng):
                for n, (tb, rows, half) in enumerate(blocks):
                    for j in range(4):
                        last = eng.transpose(psum[0:rows, n, j * P:(j + 1) * P], hT[:, 4 * half + j, tb * P:tb * P + rows], ident)
                    last.then_inc(s["pe"].sem, s["pe"].step(f"g{n}"))

            def copy(eng, kind):
                for n, (tb, rows, half) in enumerate(blocks):
                    if n % 2 == (kind == "act"):
                        eng.wait_ge(s["pe"].sem, s["pe"].count(f"g{n}"))
                        dst = y[0:rows, tb, 512 * half:512 * half + 512]
                        (eng.tensor_copy if kind == "dve" else eng.copy)(dst, psum[0:rows, n, :]).then_inc(s[kind].sem, s[kind].step(f"g{n}"))

            def pool(eng):
                v = outs["y_prompt"].rearrange("b (t p) d -> p (b t) d", p=P)
                for tb in range(3):
                    eng.wait_ge(s["dve"].sem, s["dve"].count(f"g{2 * tb}"))
                    eng.wait_ge(s["act"].sem, s["act"].count(f"g{2 * tb + 1}"))
                    if tb < 2:
                        eng.dma_start(v[:, tb, :], y[:, tb, :]).then_inc(stored, 16)
                    else:
                        eng.dma_start(outs["y_sample"].rearrange("b q d -> (b q) d"), y[0:TS, 2, :]).then_inc(stored, 16)
                n_stored[0] += 3
                eng.wait_ge(stored, 16 * n_stored[0])
            return dict(pe=pe, copy=copy, pool=pool)

        ffns = [ffn_up(l) for l in range(2)]
        nsa = nsa_stages()
        norm_g = norm_stage("norm_gdn", 0, g_low, g_low_rounded, "gdn_in")
        norm_f0 = norm_stage("norm_ffn0", 2, ffns[0]["low"], ffns[0]["low_rounded"], "ffn_up0")
        norm_n = norm_stage("norm_nsa", 1, nsa["low"], nsa["low_rounded"], "nsa_in")
        norm_f1 = norm_stage("norm_ffn1", 3, ffns[1]["low"], ffns[1]["low_rounded"], "ffn_up1")
        norm_y = norm_stage("norm_final", 4)
        fin = final_stage()
        block = ctx.enter_context(nc.Block())

        @block.sync
        def _(sp):
            sp.dma_start(x_tok[:, 0:2, :], ins["x_prompt"].rearrange("b (t p) d -> p (b t) d", p=P)).then_inc(x_in, 16)
            sp.dma_start(x_tok[0:TS, 2, :], ins["x_sample"].rearrange("b q d -> (b q) d")).then_inc(x_in, 16)
            sp.dma_start(tables, ins["tables"][:, 0:base_cols]).then_inc(const_in, 16)
            flat = "l w c -> (l w) c"
            sp.dma_start(norm_rows[0:1, :], ins["gdn_norm"]).then_inc(rows_in, 16)
            sp.dma_start(norm_rows[1:2, :], ins["nsa_norm"]).then_inc(rows_in, 16)
            sp.dma_start(norm_rows[2:4, :], ins["ffn_norm"]).then_inc(rows_in, 16)
            sp.dma_start(norm_rows[4:5, :], ins["final_norm"].rearrange("(o d) -> o d", o=1)).then_inc(rows_in, 16)
            sp.dma_start(g_rows[0:NB * GP, :], ins["state_gdn_conv"].rearrange("l b w c -> (l b w) c")).then_inc(rows_in, 16)
            sp.dma_start(g_rows[NB * GP:, :], ins["gdn_conv_w"].rearrange(flat)).then_inc(rows_in, 16)
            for l in range(2):
                sp.dma_start(f_rows[l][0:NB * FP, :], ins["state_ffn_conv"][l].rearrange("b w c -> (b w) c")).then_inc(rows_in, 16)
                sp.dma_start(f_rows[l][NB * FP:, :], ins["ffn_conv_w"][l]).then_inc(rows_in, 16)
            sp.dma_start(e_rows, ins["nsa_cmp_pe"].rearrange("l v (c s) d -> (l v c) (s d)", s=2)).then_inc(rows_in, 16)
            for x in range(2):
                sp.dma_start(pages_sb[:, x * NB * NPG:(x + 1) * NB * NPG], ins["page_table"].rearrange("(o b) n -> o (b n)", o=1)).then_inc(rows_in, 16)
            sp.dma_start(out_norm, ins["gdn_out_norm"].rearrange("l d -> d l")).then_inc(small_in, 16)
            sp.dma_start(a_log, ins["gdn_a_log"].rearrange("l d -> d l")).then_inc(small_in, 16)
            sp.dma_start(dt_bias, ins["gdn_dt_bias"].rearrange("l d -> d l")).then_inc(small_in, 16)
            sp.dma_start(w_ab, ins["gdn_w_in"][0].rearrange("(k p) n -> p k n", p=P)[:, :, CONV_CH + V_DIM:]).then_inc(small_in, 16)
            stream(sp, "gdn_in", pair_source(ins["gdn_w_in"][0]))
            stream(sp, "gdn_out", single_source(ins["gdn_w_out"][0], VH))
            stream(sp, "ffn_up0", ffns[0]["source"])
            stream(sp, "ffn_down0", single_source(ins["ffn_w_down"][0], NFT))
            nsa["stream_in"](sp)
            stream(sp, "nsa_out", pair_source(ins["nsa_w_out"][0]))
            stream(sp, "ffn_up1", ffns[1]["source"])
            stream(sp, "ffn_down1", single_source(ins["ffn_w_down"][1], NFT))

        @block.tensor
        def _(pe):
            compress, project, rows, prompt, prompt_turn, sample, project_out = nsa["pe"]
            pe_turns(pe)
            pe.drain().then_inc(stage_closed, 1)
            pe.wait_ge(stage_closed, 4 * 1)
            norm_g["pe"](pe)
            pe_gdn_in(pe)
            pe.drain().then_inc(stage_closed, 1)
            pe.wait_ge(stage_closed, 4 * 2)
            pe_gates(pe)
            pe.drain().then_inc(stage_closed, 1)
            pe.wait_ge(stage_closed, 4 * 3)
            pe_core(pe)
            pe.drain().then_inc(stage_closed, 1)
            pe.wait_ge(stage_closed, 4 * 4)
            pe_gate_norm(pe)
            pe_add(pe, "gdn_out", lambda k: o_hi[k // 4][:, k % 4, :], lambda k: o_lo[k // 4][:, k % 4, :], VH)
            pe.drain().then_inc(stage_closed, 1)
            pe.wait_ge(stage_closed, 4 * 5)
            norm_f0["pe"](pe)
            ffns[0]["pe"](pe)
            pe.drain().then_inc(stage_closed, 1)
            pe.wait_ge(stage_closed, 4 * 6)
            ffns[0]["pe_down"](pe)
            pe.drain().then_inc(stage_closed, 1)
            pe.wait_ge(stage_closed, 4 * 7)
            compress(pe)
            pe.drain().then_inc(stage_closed, 1)
            pe.wait_ge(stage_closed, 4 * 8)
            norm_n["pe"](pe)
            project(pe)
            pe.drain().then_inc(stage_closed, 1)
            pe.wait_ge(stage_closed, 4 * 9)
            rows(pe)
            pe.drain().then_inc(stage_closed, 1)
            pe.wait_ge(stage_closed, 4 * 10)
            prompt(pe)
            pe.drain().then_inc(stage_closed, 1)
            pe.wait_ge(stage_closed, 4 * 11)
            prompt_turn(pe)
            pe.drain().then_inc(stage_closed, 1)
            pe.wait_ge(stage_closed, 4 * 12)
            sample(pe)
            pe.drain().then_inc(stage_closed, 1)
            pe.wait_ge(stage_closed, 4 * 13)
            project_out(pe)
            pe.drain().then_inc(stage_closed, 1)
            pe.wait_ge(stage_closed, 4 * 14)
            norm_f1["pe"](pe)
            ffns[1]["pe"](pe)
            pe.drain().then_inc(stage_closed, 1)
            pe.wait_ge(stage_closed, 4 * 15)
            ffns[1]["pe_down"](pe)
            pe.drain().then_inc(stage_closed, 1)
            pe.wait_ge(stage_closed, 4 * 16)
            norm_y["pe"](pe)
            pe.drain().then_inc(stage_closed, 1)
            pe.wait_ge(stage_closed, 4 * 17)
            fin["pe"](pe)

        @block.scalar
        def _(act):
            compress, project, rows, prompt, prompt_turn, sample, project_out = nsa["act"]
            copy_turned(act, "act")
            act.drain().then_inc(stage_closed, 1)
            act.wait_ge(stage_closed, 4 * 1)
            norm_g["act"](act)
            act_gdn_in(act)
            act.drain().then_inc(stage_closed, 1)
            act.wait_ge(stage_closed, 4 * 2)
            act_gates(act)
            act.drain().then_inc(stage_closed, 1)
            act.wait_ge(stage_closed, 4 * 3)
            act_core(act)
            act.drain().then_inc(stage_closed, 1)
            act.wait_ge(stage_closed, 4 * 4)
            act_gate_norm(act)
            act.drain().then_inc(stage_closed, 1)
            act.wait_ge(stage_closed, 4 * 5)
            norm_f0["act"](act)
            ffns[0]["act"](act)
            act.drain().then_inc(stage_closed, 1)
            act.wait_ge(stage_closed, 4 * 6)
            ffns[0]["act_down"](act)
            act.drain().then_inc(stage_closed, 1)
            act.wait_ge(stage_closed, 4 * 7)
            compress(act)
            act.drain().then_inc(stage_closed, 1)
            act.wait_ge(stage_closed, 4 * 8)
            norm_n["act"](act)
            project(act)
            act.drain().then_inc(stage_closed, 1)
            act.wait_ge(stage_closed, 4 * 9)
            rows(act)
            act.drain().then_inc(stage_closed, 1)
            act.wait_ge(stage_closed, 4 * 10)
            prompt(act)
            act.drain().then_inc(stage_closed, 1)
            act.wait_ge(stage_closed, 4 * 11)
            prompt_turn(act)
            act.drain().then_inc(stage_closed, 1)
            act.wait_ge(stage_closed, 4 * 12)
            sample(act)
            act.drain().then_inc(stage_closed, 1)
            act.wait_ge(stage_closed, 4 * 13)
            project_out(act)
            act.drain().then_inc(stage_closed, 1)
            act.wait_ge(stage_closed, 4 * 14)
            norm_f1["act"](act)
            ffns[1]["act"](act)
            act.drain().then_inc(stage_closed, 1)
            act.wait_ge(stage_closed, 4 * 15)
            ffns[1]["act_down"](act)
            act.drain().then_inc(stage_closed, 1)
            act.wait_ge(stage_closed, 4 * 16)
            norm_y["act"](act)
            act.drain().then_inc(stage_closed, 1)
            act.wait_ge(stage_closed, 4 * 17)
            fin["copy"](act, "act")

        @block.vector
        def _(dve):
            compress, rows, prompt, prompt_turn, sample, project_out = nsa["dve"]
            dve_prepare(dve)
            copy_turned(dve, "dve")
            dve.drain().then_inc(stage_closed, 1)
            dve.wait_ge(stage_closed, 4 * 1)
            norm_g["dve"](dve)
            dve_gdn_in(dve)
            dve.drain().then_inc(stage_closed, 1)
            dve.wait_ge(stage_closed, 4 * 2)
            dve_gates(dve)
            dve.drain().then_inc(stage_closed, 1)
            dve.wait_ge(stage_closed, 4 * 3)
            dve_core(dve)
            dve.drain().then_inc(stage_closed, 1)
            dve.wait_ge(stage_closed, 4 * 4)
            dve_gate_norm(dve)
            dve_add(dve, "gdn_out")
            dve.drain().then_inc(stage_closed, 1)
            dve.wait_ge(stage_closed, 4 * 5)
            norm_f0["dve"](dve)
            ffns[0]["dve"](dve)
            dve.drain().then_inc(stage_closed, 1)
            dve.wait_ge(stage_closed, 4 * 6)
            ffns[0]["dve_down"](dve)
            dve.drain().then_inc(stage_closed, 1)
            dve.wait_ge(stage_closed, 4 * 7)
            compress(dve)
            dve.drain().then_inc(stage_closed, 1)
            dve.wait_ge(stage_closed, 4 * 8)
            norm_n["dve"](dve)
            dve.drain().then_inc(stage_closed, 1)
            dve.wait_ge(stage_closed, 4 * 9)
            rows(dve)
            dve.drain().then_inc(stage_closed, 1)
            dve.wait_ge(stage_closed, 4 * 10)
            prompt(dve)
            dve.drain().then_inc(stage_closed, 1)
            dve.wait_ge(stage_closed, 4 * 11)
            prompt_turn(dve)
            dve.drain().then_inc(stage_closed, 1)
            dve.wait_ge(stage_closed, 4 * 12)
            sample(dve)
            dve.drain().then_inc(stage_closed, 1)
            dve.wait_ge(stage_closed, 4 * 13)
            project_out(dve)
            dve.drain().then_inc(stage_closed, 1)
            dve.wait_ge(stage_closed, 4 * 14)
            norm_f1["dve"](dve)
            ffns[1]["dve"](dve)
            dve.drain().then_inc(stage_closed, 1)
            dve.wait_ge(stage_closed, 4 * 15)
            ffns[1]["dve_down"](dve)
            dve.drain().then_inc(stage_closed, 1)
            dve.wait_ge(stage_closed, 4 * 16)
            norm_y["dve"](dve)
            dve.drain().then_inc(stage_closed, 1)
            dve.wait_ge(stage_closed, 4 * 17)
            fin["copy"](dve, "dve")

        @block.gpsimd
        def _(pool):
            compress, project, rows, sample, project_out = nsa["pool"]
            pool.drain().then_inc(stage_closed, 1)
            pool.wait_ge(stage_closed, 4 * 1)
            pool_gdn_in(pool)
            pool.drain().then_inc(stage_closed, 1)
            pool.wait_ge(stage_closed, 4 * 2)
            pool.drain().then_inc(stage_closed, 1)
            pool.wait_ge(stage_closed, 4 * 3)
            pool_core(pool)
            pool.drain().then_inc(stage_closed, 1)
            pool.wait_ge(stage_closed, 4 * 4)
            pool_gate_norm(pool)
            pool.drain().then_inc(stage_closed, 1)
            pool.wait_ge(stage_closed, 4 * 5)
            ffns[0]["pool"](pool)
            pool.drain().then_inc(stage_closed, 1)
            pool.wait_ge(stage_closed, 4 * 6)
            ffns[0]["pool_down"](pool)
            pool.drain().then_inc(stage_closed, 1)
            pool.wait_ge(stage_closed, 4 * 7)
            compress(pool)
            pool.drain().then_inc(stage_closed, 1)
            pool.wait_ge(stage_closed, 4 * 8)
            project(pool)
            pool.drain().then_inc(stage_closed, 1)
            pool.wait_ge(stage_closed, 4 * 9)
            rows(pool)
            pool.drain().then_inc(stage_closed, 1)
            pool.wait_ge(stage_closed, 4 * 10)
            pool.drain().then_inc(stage_closed, 1)
            pool.wait_ge(stage_closed, 4 * 11)
            pool.drain().then_inc(stage_closed, 1)
            pool.wait_ge(stage_closed, 4 * 12)
            sample(pool)
            pool.drain().then_inc(stage_closed, 1)
            pool.wait_ge(stage_closed, 4 * 13)
            project_out(pool)
            pool.drain().then_inc(stage_closed, 1)
            pool.wait_ge(stage_closed, 4 * 14)
            ffns[1]["pool"](pool)
            pool.drain().then_inc(stage_closed, 1)
            pool.wait_ge(stage_closed, 4 * 15)
            ffns[1]["pool_down"](pool)
            pool.drain().then_inc(stage_closed, 1)
            pool.wait_ge(stage_closed, 4 * 16)
            pool.drain().then_inc(stage_closed, 1)
            pool.wait_ge(stage_closed, 4 * 17)
            fin["pool"](pool)


_INS = ['x_prompt', 'x_sample', 'cache_nsa_kv', 'cache_nsa_win', 'state_gdn_s', 'state_gdn_conv', 'state_ffn_conv',
        'page_table', 'gdn_norm', 'gdn_w_in', 'gdn_conv_w', 'gdn_a_log', 'gdn_dt_bias', 'gdn_out_norm', 'gdn_w_out',
        'nsa_norm', 'nsa_w_in', 'nsa_cmp_pe', 'nsa_cmp_w1', 'nsa_cmp_w2', 'nsa_w_out',
        'ffn_norm', 'ffn_w_up', 'ffn_conv_w', 'ffn_w_down', 'final_norm']
_OUTS = [('y_prompt', (1, TP, D)), ('y_sample', (NB, TQ, D)),
         ('kv_rows_prompt', (1, 1, TP, 4, GROUPS, DH)), ('kv_rows_sample', (1, NB, TQ, 4, GROUPS, DH)),
         ('win_prompt', (1, 1, TP, 2, GROUPS, DH)), ('win_sample', (1, NB, WIN, 2, GROUPS, DH)),
         ('gdn_s_prompt', (1, 1, VH, DK, DK)), ('gdn_s_sample', (1, NB, VH, DK, DK)),
         ('gdn_conv_prompt', (1, 1, GP, CONV_CH)), ('gdn_conv_sample', (1, NB, GP, CONV_CH)),
         ('ffn_conv_prompt', (2, 1, FP, FF)), ('ffn_conv_sample', (2, NB, FP, FF))]


def kernel(**inputs):
    import numpy as _np
    import concourse.bacc as _bacc
    from concourse import mybir as _mybir
    from concourse.bass_utils import run_bass_kernel_spmd as _run

    nc = _bacc.Bacc("TRN2", target_bir_lowering=False, num_devices=1)
    tables, where, base_cols = constants()
    arrays, args = {"tables_dram": tables}, {}
    args["tables"] = nc.dram_tensor("tables_dram", tables.shape, _mybir.dt.float32, kind="ExternalInput").ap()
    for name in _INS:
        a = _np.ascontiguousarray(inputs[name])
        arrays[f"in_{name}_dram"] = a
        args[name] = nc.dram_tensor(f"in_{name}_dram", a.shape, _mybir.dt.from_np(a.dtype), kind="ExternalInput").ap()
    outs = {name: nc.dram_tensor(f"out_{name}_dram", shape, _mybir.dt.float32, kind="ExternalOutput").ap()
            for name, shape in _OUTS}
    build(nc, args, outs, where, base_cols)
    r = _run(nc, [arrays], core_ids=[0])
    return tuple(r.results[0][f"out_{name}_dram"] for name, _ in _OUTS)
```
